# Optimizing a Trainium2 kernel written in Bass

```python
import math
import jax, jax.numpy as jnp
from jax import lax
import numpy as np

D_MODEL = 1024
BATCH = 1
SEQ = 512
DEPTH = 1
DEC_BATCH = 1
DEC_SEQ = 256
PAST_LEN = 128

N_META = 16
HEAD_DIM = 64
N_HEADS = 8
N_KV = 2
GROUP = N_HEADS // N_KV
ATTN_WIDTH = N_HEADS * HEAD_DIM
KV_WIDTH = N_KV * HEAD_DIM
WINDOW = 128
BLOCK = 128
ROPE_THETA = 10000.0
HY_WIDTH = D_MODEL // 2
HY_ORDER = 2
HY_PROJ = (HY_ORDER + 1) * HY_WIDTH
SHORT_CONV = 3
FILT_EMB = 33
FILT_BANDS = (FILT_EMB - 1) // 2
FILT_HIDDEN = 64
FILT_OUT = 2 * HY_ORDER * HY_WIDTH
DECAY_TARGET = 1e-2
FAST_DECAY_PCT = 0.3
SLOW_DECAY_PCT = 1.5
N_EXPERTS = 16
CAPACITY_FACTOR = 2
D_EXPERT = 2048
EPS = 1e-6
IN_COLS = ATTN_WIDTH + 2 * KV_WIDTH + HY_PROJ + 2 * D_MODEL
SPLITS = [ATTN_WIDTH, ATTN_WIDTH + KV_WIDTH, ATTN_WIDTH + 2 * KV_WIDTH,
          ATTN_WIDTH + 2 * KV_WIDTH + HY_PROJ, ATTN_WIDTH + 2 * KV_WIDTH + HY_PROJ + D_MODEL]

kernel_name = 'hybrid_swa_hyena_ec_moe_encoder'

F32 = jnp.float32

def _rmsnorm(x, g):
    x32 = x.astype(F32)
    y = x32 * lax.rsqrt(jnp.mean(x32 * x32, axis=-1, keepdims=True) + EPS) * g.astype(F32)
    return y.astype(x.dtype)

def _rope(x):
    L = x.shape[1]
    half = HEAD_DIM // 2
    inv = 1.0 / (ROPE_THETA ** (jnp.arange(half, dtype=F32) / half))
    ang = jnp.arange(L, dtype=F32)[:, None] * inv[None]
    cos = jnp.cos(ang)[None, :, None, :]
    sin = jnp.sin(ang)[None, :, None, :]
    x1 = x[..., :half].astype(F32)
    x2 = x[..., half:].astype(F32)
    return jnp.concatenate([x1 * cos - x2 * sin, x2 * cos + x1 * sin], -1).astype(x.dtype)

def _window_attention(q, k, v, sink):
    B, L = q.shape[:2]
    Lp = -(-L // BLOCK) * BLOCK
    nb = Lp // BLOCK
    q = jnp.pad(q, ((0, 0), (0, Lp - L), (0, 0), (0, 0)))
    kvpad = ((0, 0), (BLOCK, Lp - L + BLOCK), (0, 0), (0, 0))
    kp = jnp.pad(k, kvpad).reshape(B, nb + 2, BLOCK, N_KV, HEAD_DIM)
    vp = jnp.pad(v, kvpad).reshape(B, nb + 2, BLOCK, N_KV, HEAD_DIM)
    kb = jnp.concatenate([kp[:, :-2], kp[:, 1:-1], kp[:, 2:]], axis=2)
    vb = jnp.concatenate([vp[:, :-2], vp[:, 1:-1], vp[:, 2:]], axis=2)
    qb = q.reshape(B, nb, BLOCK, N_KV, GROUP, HEAD_DIM)
    s = jnp.einsum('bnqkgd,bnckd->bnkgqc', qb, kb, preferred_element_type=F32) * (HEAD_DIM ** -0.5)
    qpos = jnp.arange(nb)[:, None] * BLOCK + jnp.arange(BLOCK)[None]
    kpos = (jnp.arange(nb)[:, None] - 1) * BLOCK + jnp.arange(3 * BLOCK)[None]
    rel = kpos[:, None, :] - qpos[:, :, None]
    mask = (jnp.abs(rel) <= WINDOW) & (kpos[:, None, :] >= 0) & (kpos[:, None, :] < L)
    s = jnp.where(mask[None, :, None, None], s, -jnp.inf)
    sk = sink.astype(F32).reshape(N_KV, GROUP)[None, None, :, :, None, None]
    m = jnp.maximum(jnp.max(s, axis=-1, keepdims=True), sk)
    p = jnp.exp(s - m)
    denom = jnp.sum(p, axis=-1, keepdims=True) + jnp.exp(sk - m)
    o = jnp.einsum('bnkgqc,bnckd->bnqkgd', (p / denom).astype(v.dtype), vb)
    return o.reshape(B, Lp, ATTN_WIDTH)[:, :L]

def _hyena_filter_spectra(L, w1, b1, w2, b2, w3, b3, freq, wout):
    n = jnp.arange(L, dtype=F32)
    t = n / max(L - 1, 1)
    f = jnp.linspace(1e-4, FILT_BANDS - 1, FILT_BANDS, dtype=F32)
    ang = (2.0 * math.pi / L) * n[:, None] * f[None]
    z = jnp.concatenate([t[:, None], jnp.cos(ang), -jnp.sin(ang)], axis=-1)
    fr = freq.astype(F32)
    a = jnp.sin(fr * (z @ w1.astype(F32) + b1.astype(F32)))
    a = jnp.sin(fr * (a @ w2.astype(F32) + b2.astype(F32)))
    a = jnp.sin(fr * (a @ w3.astype(F32) + b3.astype(F32)))
    h = (a @ wout.astype(F32)).reshape(L, 2, HY_ORDER, HY_WIDTH)
    max_decay = math.log(DECAY_TARGET) / FAST_DECAY_PCT
    min_decay = math.log(DECAY_TARGET) / SLOW_DECAY_PCT
    deltas = jnp.abs(jnp.linspace(min_decay, max_decay, HY_WIDTH, dtype=F32))
    h = h * jnp.exp(-t[:, None] * deltas[None])[:, None, None, :]
    hf, hb = h[:, 0], h[:, 1]
    circ = jnp.concatenate([hf[:1] + hb[:1], hf[1:], jnp.zeros_like(hf[:1]), hb[:0:-1]], axis=0)
    return jnp.fft.rfft(circ, axis=0)

def _long_conv(z, kf):
    L = z.shape[1]
    zf = jnp.fft.rfft(z, n=2 * L, axis=1)
    return jnp.fft.irfft(zf * kf[None], n=2 * L, axis=1)[:, :L]

def _hyena(u, conv_w, conv_b, kf, skip):
    up = jnp.pad(u, ((0, 0), (1, 1), (0, 0)))
    uc = conv_w[0] * up[:, :-2] + conv_w[1] * up[:, 1:-1] + conv_w[2] * up[:, 2:] + conv_b
    v, x1, x2 = jnp.split(uc, HY_ORDER + 1, axis=-1)
    z = v.astype(F32)
    sk = skip.astype(F32)
    for o, gate in enumerate((x1, x2)):
        z = gate.astype(F32) * (_long_conv(z, kf[:, o]) + sk[o] * z)
    return z.astype(u.dtype)

def _expert_choice(hn, w_router, w_gate, w_up, w_down):
    B, L, D = hn.shape
    t = hn.reshape(B * L, D)
    n = B * L
    cap = max(1, (CAPACITY_FACTOR * n) // N_EXPERTS)
    aff = jax.nn.softmax(jnp.matmul(t, w_router, preferred_element_type=F32), axis=-1)
    g, idx = lax.top_k(aff.T, cap)
    xe = t[idx]
    hid = jax.nn.silu(jnp.einsum('ecd,edf->ecf', xe, w_gate)) * jnp.einsum('ecd,edf->ecf', xe, w_up)
    ye = jnp.einsum('ecf,efd->ecd', hid, w_down) * g[..., None].astype(t.dtype)
    out = jnp.zeros_like(t).at[idx.reshape(-1)].add(ye.reshape(-1, D))
    return out.reshape(B, L, D)

def _encode(x, meta_tokens, norm_mix_g, w_in, attn_sink, hy_conv_w, hy_conv_b,
            hy_filt_w1, hy_filt_b1, hy_filt_w2, hy_filt_b2, hy_filt_w3, hy_filt_b3,
            hy_filt_freq, hy_filt_wout, hy_skip, w_attn_up, w_hyena_up, w_out,
            norm_ffn_g, w_router, w_exp_gate, w_exp_up, w_exp_down, norm_final_g):
    B = x.shape[0]
    meta = jnp.broadcast_to(meta_tokens.astype(x.dtype)[None], (B, N_META, D_MODEL))
    h = jnp.concatenate([meta, x], axis=1)
    L = h.shape[1]
    for i in range(DEPTH):
        n = _rmsnorm(h, norm_mix_g[i])
        proj = n @ w_in[i]
        q, k, v, hy, g_a, g_h = jnp.split(proj, SPLITS, axis=-1)
        q = _rope(q.reshape(B, L, N_HEADS, HEAD_DIM))
        k = _rope(k.reshape(B, L, N_KV, HEAD_DIM))
        v = v.reshape(B, L, N_KV, HEAD_DIM)
        a_out = _window_attention(q, k, v, attn_sink[i])
        kf = _hyena_filter_spectra(L, hy_filt_w1[i], hy_filt_b1[i], hy_filt_w2[i], hy_filt_b2[i],
                                   hy_filt_w3[i], hy_filt_b3[i], hy_filt_freq[i], hy_filt_wout[i])
        h_out = _hyena(hy, hy_conv_w[i], hy_conv_b[i], kf, hy_skip[i])
        merged = jax.nn.sigmoid(g_a) * (a_out @ w_attn_up[i]) + jax.nn.sigmoid(g_h) * (h_out @ w_hyena_up[i])
        h = h + merged @ w_out[i]
        h = h + _expert_choice(_rmsnorm(h, norm_ffn_g[i]), w_router[i], w_exp_gate[i], w_exp_up[i], w_exp_down[i])
    return _rmsnorm(h, norm_final_g)[:, N_META:]

def setup_inputs(seed: int = 0) -> dict:
    key = jax.random.key(seed)
    ks = jax.random.split(key, 32)
    nrm = lambda k, shape, scale: jax.random.normal(k, shape, F32) * scale
    return {
        'x_prompt': nrm(ks[0], (BATCH, SEQ, D_MODEL), 1.0),
        'x_sample': nrm(ks[1], (DEC_BATCH, DEC_SEQ, D_MODEL), 1.0),
        'meta_tokens': nrm(ks[2], (N_META, D_MODEL), 1.0),
        'norm_mix_g': 1.0 + nrm(ks[3], (DEPTH, D_MODEL), 0.01),
        'w_in': nrm(ks[4], (DEPTH, D_MODEL, IN_COLS), D_MODEL ** -0.5),
        'attn_sink': nrm(ks[5], (DEPTH, N_HEADS), 0.5),
        'hy_conv_w': nrm(ks[6], (DEPTH, SHORT_CONV, HY_PROJ), SHORT_CONV ** -0.5),
        'hy_conv_b': nrm(ks[7], (DEPTH, HY_PROJ), 0.01),
        'hy_filt_w1': nrm(ks[8], (DEPTH, FILT_EMB, FILT_HIDDEN), FILT_EMB ** -0.5),
        'hy_filt_b1': nrm(ks[9], (DEPTH, FILT_HIDDEN), 0.1),
        'hy_filt_w2': nrm(ks[10], (DEPTH, FILT_HIDDEN, FILT_HIDDEN), FILT_HIDDEN ** -0.5),
        'hy_filt_b2': nrm(ks[11], (DEPTH, FILT_HIDDEN), 0.1),
        'hy_filt_w3': nrm(ks[12], (DEPTH, FILT_HIDDEN, FILT_HIDDEN), FILT_HIDDEN ** -0.5),
        'hy_filt_b3': nrm(ks[13], (DEPTH, FILT_HIDDEN), 0.1),
        'hy_filt_freq': 1.0 + nrm(ks[14], (DEPTH, FILT_HIDDEN), 0.01),
        'hy_filt_wout': nrm(ks[15], (DEPTH, FILT_HIDDEN, FILT_OUT), 0.05 * FILT_HIDDEN ** -0.5),
        'hy_skip': nrm(ks[16], (DEPTH, HY_ORDER, HY_WIDTH), 0.5),
        'w_attn_up': nrm(ks[17], (DEPTH, ATTN_WIDTH, D_MODEL), ATTN_WIDTH ** -0.5),
        'w_hyena_up': nrm(ks[18], (DEPTH, HY_WIDTH, D_MODEL), HY_WIDTH ** -0.5),
        'w_out': nrm(ks[19], (DEPTH, D_MODEL, D_MODEL), D_MODEL ** -0.5),
        'norm_ffn_g': 1.0 + nrm(ks[20], (DEPTH, D_MODEL), 0.01),
        'w_router': nrm(ks[21], (DEPTH, D_MODEL, N_EXPERTS), D_MODEL ** -0.5),
        'w_exp_gate': nrm(ks[22], (DEPTH, N_EXPERTS, D_MODEL, D_EXPERT), D_MODEL ** -0.5),
        'w_exp_up': nrm(ks[23], (DEPTH, N_EXPERTS, D_MODEL, D_EXPERT), D_MODEL ** -0.5),
        'w_exp_down': nrm(ks[24], (DEPTH, N_EXPERTS, D_EXPERT, D_MODEL), D_EXPERT ** -0.5),
        'norm_final_g': 1.0 + nrm(ks[25], (D_MODEL,), 0.01),
    }

def reference(x_prompt, x_sample, meta_tokens, norm_mix_g, w_in, attn_sink, hy_conv_w, hy_conv_b,
              hy_filt_w1, hy_filt_b1, hy_filt_w2, hy_filt_b2, hy_filt_w3, hy_filt_b3,
              hy_filt_freq, hy_filt_wout, hy_skip, w_attn_up, w_hyena_up, w_out,
              norm_ffn_g, w_router, w_exp_gate, w_exp_up, w_exp_down, norm_final_g):
    y_prompt = _encode(x_prompt, meta_tokens, norm_mix_g, w_in, attn_sink, hy_conv_w, hy_conv_b,
                       hy_filt_w1, hy_filt_b1, hy_filt_w2, hy_filt_b2, hy_filt_w3, hy_filt_b3,
                       hy_filt_freq, hy_filt_wout, hy_skip, w_attn_up, w_hyena_up, w_out,
                       norm_ffn_g, w_router, w_exp_gate, w_exp_up, w_exp_down, norm_final_g)
    y_sample = _encode(x_sample, meta_tokens, norm_mix_g, w_in, attn_sink, hy_conv_w, hy_conv_b,
                       hy_filt_w1, hy_filt_b1, hy_filt_w2, hy_filt_b2, hy_filt_w3, hy_filt_b3,
                       hy_filt_freq, hy_filt_wout, hy_skip, w_attn_up, w_hyena_up, w_out,
                       norm_ffn_g, w_router, w_exp_gate, w_exp_up, w_exp_down, norm_final_g)
    return (y_prompt, y_sample)


_drawn_inputs = setup_inputs


def setup_inputs(seed=0):
    import zlib

    import numpy as np

    out = dict(_drawn_inputs(seed))
    spreads = {}
    factors = {'norm_mix_g': 8.0,
     'attn_sink': 8.0,
     'hy_conv_b': 20.868,
     'hy_filt_b1': 3.447,
     'hy_filt_b2': 3.434,
     'hy_filt_b3': 3.164,
     'hy_filt_freq': 8.0,
     'norm_ffn_g': 44.536,
     'norm_final_g': 31.498}
    for name, (base, spread) in spreads.items():
        noise = np.random.default_rng([zlib.crc32(name.encode()), seed]).standard_normal(out[name].shape)
        drawn = base * np.exp(spread * noise) if base else spread * noise
        out[name] = __import__('jax').numpy.asarray(drawn.astype(out[name].dtype))
    for name, factor in factors.items():
        out[name] = (out[name] * factor).astype(out[name].dtype)
    return out
```

```python
import math
from contextlib import ExitStack

import numpy as np

import concourse.bass as bass
from concourse import mybir

F32 = mybir.dt.float32
F32R = mybir.dt.float32r
U32 = mybir.dt.uint32
ALU = mybir.AluOpType
ACT = mybir.ActivationFunctionType
AX = mybir.AxisListType

P = 128
BANK = 512

D = 1024
KT = D // P
N_META = 16
SEQS = (512, 256)
LENS = tuple(s + N_META for s in SEQS)
STARTS = (0, LENS[0])
T = sum(LENS)
HALF = T // 2
TOK_TILES = [(t, min(P, T - t)) for t in range(0, T, P)]

HEAD_DIM = 64
N_HEADS = 8
N_KV = 2
GROUP = N_HEADS // N_KV
ATTN = N_HEADS * HEAD_DIM
KVW = N_KV * HEAD_DIM
WINDOW = 128
HYW = D // 2
CT = HYW // P
HY_TILES = 3 * CT
C_K, C_V = ATTN, ATTN + KVW
C_HY = ATTN + 2 * KVW
C_GATE = C_HY + 3 * HYW
WCH = 256

FILT_EMB, FILT_BANDS, FILT_HIDDEN = 33, 16, 64
E = 16
FE = 2048
CAPS = tuple(2 * n // E for n in LENS)
SLOTS = sum(CAPS)
EPS = 1e-6

BLOCKS = []
for _s, _n in zip(STARTS, LENS):
    for _q in range(0, _n, P):
        _k0, _k1 = max(0, _q - P), min(_n, _q + 2 * P)
        BLOCKS.append((_s + _q, min(P, _n - _q), _s + _k0, _k1 - _k0, _k0 - (_q - P)))
VBLOCK0 = {s + q: i for i, (s, q) in enumerate((s, q) for s, n in zip(STARTS, LENS) for q in range(0, n, P))}

GROUPS = (3, 2)
FG = (178, 138)
W = tuple(2 * g * f for g, f in zip(GROUPS, FG))
NT = tuple(-(-n // P) for n in LENS)
NK = tuple(-(-w // P) for w in W)

TWO_PI = 2.0 * math.pi
MAGIC = 1.5 * 2.0 ** 23
NEG = -1e30


def dft_tables(s):
    n, g, f = LENS[s], GROUPS[s], FG[s]
    size = 2 * n
    k = np.arange(g * f)
    live = (k <= n).astype(np.float64)
    phase = 2 * np.pi * ((np.arange(n)[:, None] * k[None]) % size) / size
    cos, sin = np.cos(phase) * live, np.sin(phase) * live
    ahead = np.stack([cos.reshape(n, g, f), sin.reshape(n, g, f)], 2).reshape(n, 2 * g * f)
    weight = np.where((k == 0) | (k == n), 1.0, 2.0) / size
    back = np.stack([(cos * weight).reshape(n, g, f), (sin * weight).reshape(n, g, f)], 2)
    return ahead.astype(np.float32), np.ascontiguousarray(back.reshape(n, 2 * g * f).T).astype(np.float32)


def halves12(x):
    def top(v):
        u = v.view(np.uint32).astype(np.uint64)
        return (((u + 0x7FF + ((u >> 12) & 1)) >> 12) << 12).astype(np.uint32).view(np.float32)
    hi = top(x)
    return np.stack([hi, top(x - hi)])


def shape_tables():
    c = {}
    pos = np.concatenate([np.arange(n, dtype=np.float32) for n in LENS])
    half = HEAD_DIM // 2
    inv = (np.float32(1.0) / (np.float32(10000.0) ** (np.arange(half, dtype=np.float32) / np.float32(half)))).astype(np.float32)
    ang = (pos[None, :] * inv[:, None]).astype(np.float32)
    cos, sin = np.cos(ang), np.sin(ang)
    c["rope_cos"] = np.tile(cos, (4, 1)).astype(np.float32)
    c["rope_sin"] = np.concatenate([-sin, sin, -sin, sin]).astype(np.float32)
    rel = np.arange(3 * P)[None, :] - P - np.arange(P)[:, None]
    c["band"] = np.where(np.abs(rel) <= WINDOW, 0.0, NEG).astype(np.float32)
    c["ident"] = np.eye(P, dtype=np.float32)
    feats = []
    for s, n in enumerate(LENS):
        k = np.arange(n, dtype=np.float32)
        t = (k / np.float32(max(n - 1, 1))).astype(np.float32)
        step = (np.arange(FILT_BANDS, dtype=np.float32) / np.float32(FILT_BANDS - 1)).astype(np.float32)
        f = (np.float32(1e-4) * (np.float32(1) - step) + np.float32(FILT_BANDS - 1) * step).astype(np.float32)
        f[-1] = FILT_BANDS - 1
        ang = ((np.float32(2.0 * math.pi / n) * k)[:, None] * f[None]).astype(np.float32)
        feats.append(np.concatenate([t[:, None], np.cos(ang), -np.sin(ang)], -1).astype(np.float32).T)
        lo, hi = math.log(1e-2) / 1.5, math.log(1e-2) / 0.3
        step = (np.arange(HYW, dtype=np.float32) / np.float32(HYW - 1)).astype(np.float32)
        dl = np.abs((np.float32(lo) * (np.float32(1) - step) + np.float32(hi) * step).astype(np.float32))
        dl[-1] = abs(np.float32(hi))
        c[f"decay{s}"] = np.exp((-t[:, None] * dl[None]).astype(np.float32)).astype(np.float32)
        ahead, back = dft_tables(s)
        c[f"ahead{s}"] = halves12(ahead)
        c[f"back{s}"] = halves12(back)
    c["filt_z"] = np.ascontiguousarray(np.concatenate(feats, 1))
    return c


class Map:

    def __init__(self, nc):
        self.nc, self.at, self.n = nc, -(-nc.sbuf_base // 64) * 64, 0

    def __call__(self, name, shape, dt=F32):
        self.n += 1
        size = 4
        for x in shape[1:]:
            size *= x
        t = self.nc.alloc_sbuf_tensor_at(f"{name}_{self.n}", list(shape), dt, offset=self.at)
        self.at += -(-size // 64) * 64
        return t


class Ctx:
    pass


class Semaphores:

    def __init__(self, nc):
        self.nc, self.held = nc, []

    def __call__(self, names):
        new = [self.nc.alloc_semaphore(n) for n in names.split()]
        self.held += new
        return new

    def end_stage(self):
        self.nc.clear_and_free_semaphores(self.held)
        self.nc.all_engine_barrier()
        self.held = []


def linked(eng, sem):
    n = [0]

    def link(ins):
        n[0] += 1
        ins.then_inc(sem, 1)
        eng.wait_ge(sem, n[0])
    return link


def three_passes(nc, out, whi, wlo, xhi, xlo, first, last):
    nc.tensor.matmul(out, whi, xhi, start=first, stop=False)
    nc.tensor.matmul(out, whi, xlo, start=False, stop=False)
    return nc.tensor.matmul(out, wlo, xhi, start=False, stop=last)


def token_pieces(t0, n, x_prompt, x_sample, meta):
    out = []
    for s, x in enumerate((x_prompt, x_sample)):
        for a, b, src, off in ((STARTS[s], STARTS[s] + N_META, meta, STARTS[s]),
                               (STARTS[s] + N_META, STARTS[s] + LENS[s], x, STARTS[s] + N_META)):
            lo, hi = max(a, t0), min(b, t0 + n)
            if lo < hi:
                out.append((lo - t0, src[lo - off:hi - off, :]))
    return out


def stage_project(g):
    nc, io, S = g.nc, g.io, g.sem
    top = g.sb.at
    sb = g.sb
    nhi = sb("normed_hi", [P, KT, T], F32R)
    nlo = sb("normed_lo", [P, KT, T], F32R)
    gain = sb("mix_gain", [P, D])
    h = [sb("tokens", [P, D]) for _ in range(2)]
    n = [sb("normed", [P, D]) for _ in range(2)]
    ss = sb("square_sums", [P, 2 * len(TOK_TILES)])
    junk = sb("squares", [P, D])
    raw = [sb("w_raw", [P, KT, WCH]) for _ in range(3)]
    whi = [sb("w_hi", [P, KT, WCH], F32R) for _ in range(2)]
    wlo = [sb("w_lo", [P, KT, WCH], F32R) for _ in range(2)]
    rows = sb("conv_rows", [3 * HY_TILES + HY_TILES + 2 * CT, P])
    upad = [sb("u_padded", [P, T + 3]) for _ in range(2)]
    uc = [sb("u_conv", [P, T + 1]) for _ in range(2)]
    part = sb("conv_part", [P, T + 1])
    cosT = sb("rope_cos", [P, 2, HALF])
    sinT = sb("rope_sin", [P, 2, HALF])
    qr = [sb("q_plain", [P, 2, HALF]) for _ in range(2)]
    qs = [sb("q_swapped", [P, 2, HALF]) for _ in range(2)]
    sg = [sb("gate_sig", [P, 2, HALF]) for _ in range(2)]
    ident, qk, v, taps = g.ident, g.qk, g.v, g.taps
    tp = [g.ps[0], g.ps[1], g.ps[2], g.ps[3]]
    acc = [(g.ps[4], g.ps[5]), (g.ps[6], g.ps[7])]

    (tok_in, const_in, rows_in, w_in0, w_in1, w_in2, squared, meaned, rooted, normed, n_turned, hi_out, lo_out,
     w_hi, w_lo, prod, evac, conv_in, conv_out, uc_store0, uc_store1, sig_out, sig_store0, sig_store1, rope_in, rope_cos_done,
     rope_sin_done, roped, v_own, pads, taps_turned, taps_out, rope_tab) = S(
        "tok_in const_in rows_in w_in0 w_in1 w_in2 squared meaned rooted normed n_turned hi_out lo_out "
        "w_hi w_lo prod evac conv_in conv_out uc_store0 uc_store1 sig_out sig_store0 sig_store1 rope_in rope_cos_done "
        "rope_sin_done roped v_own pads taps_turned taps_out rope_tab")
    w_in = [w_in0, w_in1, w_in2]
    uc_store, sig_store = [uc_store0, uc_store1], [sig_store0, sig_store1]
    ntok = len(TOK_TILES)
    w = io["w_in"][0].rearrange("(t p) c -> p t c", p=P)
    chunks = [("hy", i) for i in range(6)] + [("q", 0), ("q", 1), ("kv", 0)] + [("gate", i) for i in range(8)]
    tiles = [(c, kind, i, sub) for c, (kind, i) in enumerate(chunks) for sub in range(2)]
    tok_sems = []
    tok_in2 = S("tok_in_odd")[0]
    tok_ins = [tok_in, tok_in2]
    pieces = [token_pieces(t0, m, io["x_prompt"][0], io["x_sample"][0], io["meta_tokens"]) for t0, m in TOK_TILES]
    tok_total = [[0, 0]]
    for i, ps_ in enumerate(pieces):
        now = list(tok_total[-1])
        now[i % 2] += 16 * len(ps_)
        tok_total.append(now)

    with nc.Block() as block:
        @block.sync
        def _(sp):
            def load_tokens(i):
                if i >= 2:
                    sp.wait_ge(normed, i - 1)
                for r0, src in pieces[i]:
                    sp.dma_start(h[i % 2][r0:r0 + src.shape[0], :], src).then_inc(tok_ins[i % 2], 16)

            def load_w(c):
                kind, i = chunks[c]
                dst = raw[c % 3]
                if c >= 3:
                    sp.wait_ge(w_hi, c - 2)
                    sp.wait_ge(w_lo, c - 2)
                if kind == "q":
                    for j in range(2):
                        for kv in range(2):
                            col = (2 * i + j + kv * GROUP) * HEAD_DIM
                            at = j * P + kv * HEAD_DIM
                            sp.dma_start(dst[:, :, at:at + HEAD_DIM], w[:, :, col:col + HEAD_DIM]).then_inc(w_in[c % 3], 16)
                    return
                col = {"hy": C_HY, "kv": C_K, "gate": C_GATE}[kind] + i * WCH
                for j in range(4):
                    sp.dma_start(dst[:, 2 * j:2 * j + 2, :], w[:, 2 * j:2 * j + 2, col:col + WCH]).then_inc(w_in[c % 3], 16)

            load_tokens(0)
            sp.dma_start(gain[:, :], io["norm_mix_g"][0].partition_broadcast(P)).then_inc(const_in, 16)
            sp.dma_start(ident[:, :], io["ident"]).then_inc(const_in, 16)
            load_tokens(1)
            load_w(0)
            r = io["hy_conv_w"][0].rearrange("k (m p) -> (k m) p", p=P)
            sp.dma_start(rows[0:36, :], r).then_inc(rows_in, 16)
            sp.dma_start(rows[36:48, :], io["hy_conv_b"][0].rearrange("(m p) -> m p", p=P)).then_inc(rows_in, 16)
            sp.dma_start(rows[48:56, :], io["hy_skip"][0].rearrange("o (m p) -> (o m) p", p=P)).then_inc(rows_in, 16)
            load_w(1)
            for i in range(2, ntok):
                load_tokens(i)
            load_w(2)
            sp.dma_start(cosT[:, :, :], io["rope_cos"].rearrange("p (a c) -> p a c", a=2)).then_inc(rope_tab, 16)
            sp.dma_start(sinT[:, :, :], io["rope_sin"].rearrange("p (a c) -> p a c", a=2)).then_inc(rope_tab, 16)
            hy = gt = 0
            for c, kind, i, sub in tiles:
                if sub == 0 and c + 3 < len(chunks):
                    load_w(c + 3)
                if kind == "hy":
                    sp.wait_ge(conv_out, 3 * (hy + 1))
                    sp.dma_start(g.hyS[hy * P:(hy + 1) * P, :], uc[hy % 2][:, :]).then_inc(uc_store[hy % 2], 16)
                    hy += 1
                if kind == "gate":
                    sp.wait_ge(sig_out, gt + 1)
                    sp.dma_start(g.sigS[gt * P:(gt + 1) * P, :].rearrange("p (a c) -> p a c", a=2), sg[gt % 2][:, :, :])\
                      .then_inc(sig_store[gt % 2], 16)
                    gt += 1
            for k in range(2):
                sp.wait_ge(uc_store[k], 16 * (HY_TILES // 2))
                sp.wait_ge(sig_store[k], 16 * 8)

        def turn_out(act, i):
            t0, m = TOK_TILES[i]
            for b in range(2):
                act.wait_ge(n_turned, 2 * i + b + 1)
                act.activation(nhi[:, 4 * b:4 * b + 4, t0:t0 + m],
                               tp[(2 * i + b) % 4][:, :].rearrange("p (a c) -> p a c", a=4)[:, :, 0:m], ACT.Copy)\
                   .then_inc(hi_out, 1)

        @block.scalar
        def _(act):
            def take_hi(c):
                act.wait_ge(w_in[c % 3], 64 * (c // 3 + 1))
                if c >= 2:
                    act.wait_ge(prod, 2 * (c - 1))
                act.activation(whi[c % 2][:, :, :], raw[c % 3][:, :, :], ACT.Copy).then_inc(w_hi, 1)

            for k in range(2):
                act.wait_ge(pads, 2)
            for i, (t0, m) in enumerate(TOK_TILES):
                act.wait_ge(tok_ins[i % 2], tok_total[i + 1][i % 2])
                act.activation(junk[0:m, :], h[i % 2][0:m, :], ACT.Square, accum_out=ss[0:m, i:i + 1]).then_inc(squared, 1)
                act.wait_ge(meaned, i + 1)
                act.activation(ss[0:m, ntok + i:ntok + i + 1], ss[0:m, i:i + 1], ACT.Sqrt).then_inc(rooted, 1)
                if i == 1:
                    take_hi(0)
                if i == 3:
                    take_hi(1)
                if i >= 1:
                    turn_out(act, i - 1)
            turn_out(act, ntok - 1)
            hy = gt = rp = 0
            for a, (c, kind, i, sub) in enumerate(tiles):
                if sub == 0 and c + 1 < len(chunks) and c >= 1:
                    take_hi(c + 1)
                act.wait_ge(prod, a + 1)
                b0, b1 = acc[a % 2]
                if kind == "hy":
                    if hy >= 2:
                        act.wait_ge(conv_out, 3 * (hy - 1))
                    u = upad[hy % 2]
                    act.activation(u[:, 1:1 + HALF], b0[:, 0:HALF], ACT.Copy)
                    act.activation(u[:, 1 + HALF:1 + LENS[0]], b1[:, 0:LENS[0] - HALF], ACT.Copy)
                    act.activation(u[:, 2 + LENS[0]:2 + T], b1[:, LENS[0] - HALF:HALF], ACT.Copy).then_inc(evac, 1)
                    hy += 1
                elif kind == "gate":
                    if gt >= 2:
                        act.wait_ge(sig_store[gt % 2], 16 * (gt // 2))
                    act.activation(sg[gt % 2][:, 0, :], b0[:, 0:HALF], ACT.Sigmoid)
                    act.activation(sg[gt % 2][:, 1, :], b1[:, 0:HALF], ACT.Sigmoid).then_inc(sig_out, 1)
                    gt += 1
                elif kind == "kv" and sub == 1:
                    for k, b in enumerate((b0, b1)):
                        for j in range(4):
                            m = VB[4 * k + j][1]
                            last = act.activation(v[0:m, 4 * k + j, :], b[0:m, j * P:(j + 1) * P], ACT.Copy)
                    last.then_inc(evac, 1)
                else:
                    if rp >= 2:
                        act.wait_ge(roped, rp - 1)
                    for k, b in enumerate((b0, b1)):
                        act.activation(qr[rp % 2][:, k, :], b[:, 0:HALF], ACT.Copy)
                        for x in range(4):
                            last = act.activation(qs[rp % 2][32 * x:32 * x + 32, k, :],
                                                  b[32 * (x ^ 1):32 * (x ^ 1) + 32, 0:HALF], ACT.Copy)
                    last.then_inc(evac, 1)
                    rp += 1

        @block.vector
        def _(dve):
            link = linked(dve, v_own)
            for k in range(2):
                nc.vector.memset(upad[k][:, :], 0.0).then_inc(pads, 1)
            dve.wait_ge(const_in, 32)

            def take_lo(i):
                t0, m = TOK_TILES[i]
                for b in range(2):
                    dve.wait_ge(hi_out, 2 * i + b + 1)
                    nc.vector.tensor_tensor(nlo[:, 4 * b:4 * b + 4, t0:t0 + m],
                                            tp[(2 * i + b) % 4][:, :].rearrange("p (a c) -> p a c", a=4)[:, :, 0:m],
                                            nhi[:, 4 * b:4 * b + 4, t0:t0 + m].bitcast(F32), ALU.subtract).then_inc(lo_out, 1)

            for i, (t0, m) in enumerate(TOK_TILES):
                dve.wait_ge(squared, i + 1)
                nc.vector.tensor_scalar(ss[0:m, i:i + 1], ss[0:m, i:i + 1], 1.0 / D, EPS, ALU.mult, ALU.add).then_inc(meaned, 1)
                dve.wait_ge(rooted, i + 1)
                link(nc.vector.reciprocal(ss[0:m, i:i + 1], ss[0:m, ntok + i:ntok + i + 1]))
                if i >= 2:
                    dve.wait_ge(n_turned, 2 * (i - 1))
                nc.vector.scalar_tensor_tensor(n[i % 2][0:m, :], h[i % 2][0:m, :], ss[0:m, i:i + 1], gain[0:m, :],
                                               ALU.mult, ALU.mult).then_inc(normed, 1)
                if i >= 1:
                    take_lo(i - 1)
            take_lo(ntok - 1)
            dve.wait_ge(taps_turned, 1)
            nc.vector.tensor_copy(taps[:, :], tp[2 * ntok % 4][:, 0:taps.shape[1]]).then_inc(taps_out, 1)
            dve.wait_ge(taps_out, 1)
            dve.wait_ge(rope_tab, 32)
            hy = rp = 0
            for a, (c, kind, i, sub) in enumerate(tiles):
                if kind == "hy":
                    dve.wait_ge(evac, hy + 1)
                    u, o, m = upad[hy % 2], uc[hy % 2], hy
                    tap = [taps[:, k * HY_TILES + m:k * HY_TILES + m + 1] for k in range(4)]
                    if hy >= 2:
                        dve.wait_ge(uc_store[hy % 2], 16 * (hy // 2))
                    nc.vector.tensor_scalar(o[:, :], u[:, 0:T + 1], tap[0], tap[3], ALU.mult, ALU.add).then_inc(conv_out, 1)
                    dve.wait_ge(conv_out, 3 * hy + 1)
                    nc.vector.scalar_tensor_tensor(part[:, :], u[:, 1:T + 2], tap[1], o[:, :], ALU.mult, ALU.add).then_inc(conv_out, 1)
                    dve.wait_ge(conv_out, 3 * hy + 2)
                    nc.vector.scalar_tensor_tensor(o[:, :], u[:, 2:T + 3], tap[2], part[:, :], ALU.mult, ALU.add).then_inc(conv_out, 1)
                    hy += 1
                elif kind == "q" or (kind == "kv" and sub == 0):
                    dve.wait_ge(evac, HY_TILES + rp + 1)
                    link(nc.vector.tensor_tensor(qr[rp % 2][:, :, :], qr[rp % 2][:, :, :], cosT[:, :, :], ALU.mult))
                    dve.wait_ge(rope_sin_done, rp + 1)
                    nc.vector.tensor_tensor(qk[:, rp, :].rearrange("p (a c) -> p a c", a=2), qr[rp % 2][:, :, :],
                                            qs[rp % 2][:, :, :], ALU.add).then_inc(roped, 1)
                    rp += 1

        @block.gpsimd
        def _(pool):
            rp = 0
            done = 0

            def lo(c):
                pool.wait_ge(w_hi, c + 1)
                nc.gpsimd.tensor_tensor(wlo[c % 2][:, :, :], raw[c % 3][:, :, :], whi[c % 2][:, :, :].bitcast(F32),
                                        ALU.subtract).then_inc(w_lo, 1)
            lo(0)
            lo(1)
            pool.wait_ge(rope_tab, 32)
            for a, (c, kind, i, sub) in enumerate(tiles):
                if sub == 0 and 1 <= c and c + 1 < len(chunks):
                    lo(c + 1)
                if kind == "q" or (kind == "kv" and sub == 0):
                    pool.wait_ge(evac, HY_TILES + rp + 1)
                    nc.gpsimd.tensor_tensor(qs[rp % 2][:, :, :], qs[rp % 2][:, :, :], sinT[:, :, :], ALU.mult)\
                      .then_inc(rope_sin_done, 1)
                    rp += 1

        @block.tensor
        def _(pe):
            pe.wait_ge(const_in, 32)
            for i, (t0, m) in enumerate(TOK_TILES):
                pe.wait_ge(normed, i + 1)
                for b in range(2):
                    u = 2 * i + b
                    if u >= 4:
                        pe.wait_ge(lo_out, u - 3)
                    for k in range(4):
                        kt = 4 * b + k
                        last = nc.tensor.transpose(tp[u % 4][:, k * P:k * P + m], n[i % 2][0:m, kt * P:(kt + 1) * P],
                                                   ident[0:m, 0:m])
                    last.then_inc(n_turned, 1)
            pe.wait_ge(rows_in, 48)
            pe.wait_ge(lo_out, 2 * ntok - 3)
            nc.tensor.transpose(tp[2 * ntok % 4][:, 0:rows.shape[0]], rows[:, :], ident[0:rows.shape[0], 0:rows.shape[0]])\
              .then_inc(taps_turned, 1)
            pe.wait_ge(lo_out, 2 * ntok)
            ev = sg_n = 0
            freed = []
            for a, (c, kind, i, sub) in enumerate(tiles):
                if kind == "gate":
                    sg_n += 1
                    freed.append((sig_out, sg_n))
                else:
                    ev += 1
                    freed.append((evac, ev))
            for a, (c, kind, i, sub) in enumerate(tiles):
                if sub == 0:
                    pe.wait_ge(w_hi, c + 1)
                    pe.wait_ge(w_lo, c + 1)
                if a >= 2:
                    pe.wait_ge(*freed[a - 2])
                hi, lo_ = whi[c % 2], wlo[c % 2]
                if kind == "kv" and sub == 1:
                    for j, (t0, m) in enumerate(VB):
                        for kt in range(KT):
                            last = three_passes(nc, acc[a % 2][j // 4][0:m, (j % 4) * P:(j % 4 + 1) * P],
                                                nhi[:, kt, t0:t0 + m], nlo[:, kt, t0:t0 + m],
                                                hi[:, kt, P:2 * P], lo_[:, kt, P:2 * P], kt == 0, kt == KT - 1)
                else:
                    for k in range(2):
                        for kt in range(KT):
                            last = three_passes(nc, acc[a % 2][k][:, 0:HALF],
                                                hi[:, kt, sub * P:(sub + 1) * P], lo_[:, kt, sub * P:(sub + 1) * P],
                                                nhi[:, kt, k * HALF:(k + 1) * HALF], nlo[:, kt, k * HALF:(k + 1) * HALF],
                                                kt == 0, kt == KT - 1)
                last.then_inc(prod, 1)
    g.sb.at = top


VB = [(s + q, min(P, n - q)) for s, n in zip(STARTS, LENS) for q in range(0, n, P)]


def stage_filter_mlp(g):
    nc, io, S = g.nc, g.io, g.sem
    top = g.sb.at
    sb = g.sb
    H = FILT_HIDDEN
    z = sb("filt_z", [FILT_EMB, T])
    w1 = sb("filt_w1", [FILT_EMB, H])
    w2 = sb("filt_w2", [H, H])
    w3 = sb("filt_w3", [H, H])
    col = sb("filt_cols", [H, 4])
    x = sb("filt_x", [H, T])
    k = sb("filt_k", [H, T])
    y = sb("filt_y", [H, T])
    a = sb("filt_a", [H, T])
    ins, mm, own, sined = S("filt_in filt_mm filt_own filt_sine")
    c1 = float(np.float32(6.28125))
    c2 = float(np.float32(np.float64(TWO_PI - c1).astype(np.float32).view(np.uint32).__and__(0xFFFFF000).view(np.float32)))
    c3 = float(np.float32(TWO_PI - c1 - c2))
    pi = float(np.nextafter(np.float32(math.pi), np.float32(0)))
    with nc.Block() as block:
        @block.sync
        def _(sp):
            sp.dma_start(z[:, :], io["filt_z"]).then_inc(ins, 16)
            for t, name in ((w1, "w1"), (w2, "w2"), (w3, "w3")):
                sp.dma_start(t[:, :], io[f"hy_filt_{name}"][0]).then_inc(ins, 16)
            for j, name in enumerate(("b1", "b2", "b3", "freq")):
                sp.dma_start(col[:, j:j + 1], io[f"hy_filt_{name}"][0].rearrange("(p a) -> p a", a=1)).then_inc(ins, 16)
            sp.wait_ge(ins, 128)

        @block.tensor
        def _(pe):
            pe.wait_ge(ins, 128)
            for layer, (w, src) in enumerate(((w1, z), (w2, a), (w3, a))):
                if layer:
                    pe.wait_ge(sined, layer)
                for b in range(2):
                    last = nc.tensor.matmul(g.ps[b][0:H, 0:HALF], w[:, :], src[:, b * HALF:(b + 1) * HALF], start=True, stop=True)
                last.then_inc(mm, 1)

        @block.vector
        def _(dve):
            dve.wait_ge(ins, 128)
            link = linked(dve, own)
            for layer in range(3):
                dve.wait_ge(mm, layer + 1)
                for b in range(2):
                    link(nc.vector.tensor_scalar(x[:, b * HALF:(b + 1) * HALF], g.ps[b][0:H, 0:HALF], col[:, layer:layer + 1],
                                                 col[:, 3:4], ALU.add, ALU.mult))
                link(nc.vector.tensor_scalar(k[:, :], x[:, :], 1.0 / TWO_PI, MAGIC, ALU.mult, ALU.add))
                link(nc.vector.tensor_scalar(k[:, :], k[:, :], MAGIC, None, ALU.subtract))
                link(nc.vector.scalar_tensor_tensor(y[:, :], k[:, :], -c1, x[:, :], ALU.mult, ALU.add))
                link(nc.vector.scalar_tensor_tensor(x[:, :], k[:, :], -c2, y[:, :], ALU.mult, ALU.add))
                link(nc.vector.scalar_tensor_tensor(y[:, :], k[:, :], -c3, x[:, :], ALU.mult, ALU.add))
                link(nc.vector.tensor_scalar(x[:, :], y[:, :], pi, -pi, ALU.min, ALU.max))

        @block.scalar
        def _(act):
            for layer in range(3):
                act.wait_ge(own, 8 * (layer + 1))
                dst = a if layer < 2 else g.feat
                act.activation(dst[:, :], x[:, :], ACT.Sin).then_inc(sined, 1)
            act.wait_ge(sined, 3)
    g.sb.at = top


def stage_attend(g):
    nc, io, S = g.nc, g.io, g.sem
    top = g.sb.at
    sb = g.sb
    band = sb("band", [P, 3 * P])
    sinks = sb("sinks", [P, N_HEADS])
    s = [sb("scores", [P, N_HEADS, 3 * P]) for _ in range(2)]
    small = [sb("softmax_cols", [P, 6, N_HEADS]) for _ in range(2)]
    pt = [sb("probs_turned", [P, GROUP, P]) for _ in range(4)]
    o = [sb("attn_out", [P, GROUP, P]) for _ in range(2)]
    qk, v, ident = g.qk, g.v, g.ident
    cin, scored, masked, prep, exped, normed, turned, copied, pv, o_out, store0, store1, own = S(
        "at_in at_scored at_masked at_prep at_exped at_normed at_turned at_copied at_pv at_out at_store0 at_store1 at_own")
    store = [store0, store1]
    sc = [g.ps[0], g.ps[1]]
    tr = [g.ps[2], g.ps[3], g.ps[6], g.ps[7]]
    ob = [g.ps[4], g.ps[5]]
    HEADS = [(j, kv) for j in range(GROUP) for kv in range(N_KV)]
    nb = len(BLOCKS)

    def key_tiles(b):
        _, _, k0, nk, _ = BLOCKS[b]
        return [(c, min(P, nk - c)) for c in range(0, nk, P)]

    turns = [(b, kv, ci) for b in range(nb) for kv in range(N_KV) for ci in range(len(key_tiles(b)))]
    before = {}
    for n_, (b, kv, ci) in enumerate(turns):
        before[(b, kv, ci)] = n_

    with nc.Block() as block:
        @block.sync
        def _(sp):
            sp.dma_start(band[:, :], io["band"]).then_inc(cin, 16)
            sp.dma_start(sinks[:, :], io["attn_sink"][0].partition_broadcast(P)).then_inc(cin, 16)
            for b, (q0, lq, k0, nk, m0) in enumerate(BLOCKS):
                sp.wait_ge(o_out, b + 1)
                sp.dma_start(g.upS[0:ATTN, :].rearrange("(j p) t -> p j t", p=P)[:, :, q0:q0 + lq],
                             o[b % 2][:, :, 0:lq]).then_inc(store[b % 2], 16)
            sp.wait_ge(store[0], 16 * ((nb + 1) // 2))
            sp.wait_ge(store[1], 16 * (nb // 2))

        @block.tensor
        def _(pe):
            def scores(b):
                q0, lq, k0, nk, m0 = BLOCKS[b]
                for i, (j, kv) in enumerate(HEADS):
                    u = b * N_HEADS + i
                    if u >= 2:
                        pe.wait_ge(masked, u - 1)
                    r = slice(kv * HEAD_DIM, (kv + 1) * HEAD_DIM)
                    nc.tensor.matmul(sc[kv][0:lq, 0:nk], qk[r, j, q0:q0 + lq], qk[r, GROUP, k0:k0 + nk],
                                     start=True, stop=True).then_inc(scored, 1)

            def weigh(b):
                q0, lq, k0, nk, m0 = BLOCKS[b]
                pe.wait_ge(normed, b + 1)
                cts = key_tiles(b)
                for kv in range(N_KV):
                    for ci, (c, m) in enumerate(cts):
                        u = before[(b, kv, ci)]
                        if u >= 4:
                            pe.wait_ge(copied, u - 3)
                        for j in range(GROUP):
                            last = nc.tensor.transpose(tr[u % 4][0:m, j * P:j * P + lq],
                                                       s[b % 2][0:lq, kv * GROUP + j, c:c + m], ident[0:lq, 0:lq])
                        last.then_inc(turned, 1)
                    if kv == 0 and b >= 2:
                        pe.wait_ge(o_out, b - 1)
                    for ci, (c, m) in enumerate(cts):
                        u = before[(b, kv, ci)]
                        pe.wait_ge(copied, u + 1)
                        last = nc.tensor.matmul(ob[b % 2][kv * HEAD_DIM:(kv + 1) * HEAD_DIM, :]
                                                .rearrange("p (j q) -> p j q", j=GROUP)[:, :, 0:lq],
                                                v[0:m, VBI[k0 + c], kv * HEAD_DIM:(kv + 1) * HEAD_DIM],
                                                pt[u % 4][0:m, :, 0:lq], start=(ci == 0), stop=(ci == len(cts) - 1))
                last.then_inc(pv, 1)

            scores(0)
            for b in range(nb):
                if b + 1 < nb:
                    scores(b + 1)
                weigh(b)

        @block.vector
        def _(dve):
            dve.wait_ge(cin, 32)
            link = linked(dve, own)

            def mask(b):
                q0, lq, k0, nk, m0 = BLOCKS[b]
                if b >= 2:
                    dve.wait_ge(pv, b - 1)
                for i, (j, kv) in enumerate(HEADS):
                    dve.wait_ge(scored, b * N_HEADS + i + 1)
                    hd = kv * GROUP + j
                    nc.vector.tensor_tensor_reduce(s[b % 2][0:lq, hd, 0:nk], sc[kv][0:lq, 0:nk], band[0:lq, m0:m0 + nk],
                                                   1.0, NEG, ALU.add, ALU.max, small[b % 2][0:lq, 0, hd:hd + 1]).then_inc(masked, 1)
                dve.wait_ge(masked, N_HEADS * (b + 1))
                k = small[b % 2]
                link(nc.vector.scalar_tensor_tensor(k[0:lq, 1, :], k[0:lq, 0, :], HEAD_DIM ** -0.5, sinks[0:lq, :], ALU.mult, ALU.max))
                link(nc.vector.tensor_scalar(k[0:lq, 2, :], k[0:lq, 1, :], -1.0, None, ALU.mult))
                nc.vector.tensor_tensor(k[0:lq, 3, :], sinks[0:lq, :], k[0:lq, 1, :], ALU.subtract).then_inc(prep, 1)

            def norm(b):
                q0, lq, k0, nk, m0 = BLOCKS[b]
                k = small[b % 2]
                dve.wait_ge(exped, b + 1)
                link(nc.vector.tensor_tensor(k[0:lq, 1, :], k[0:lq, 4, :], k[0:lq, 3, :], ALU.add))
                link(nc.vector.reciprocal(k[0:lq, 5, :], k[0:lq, 1, :]))
                for hd in range(N_HEADS):
                    last = nc.vector.tensor_scalar(s[b % 2][0:lq, hd, 0:nk], s[b % 2][0:lq, hd, 0:nk], k[0:lq, 5, hd:hd + 1],
                                                   None, ALU.mult)
                last.then_inc(normed, 1)

            def out(b):
                lq = BLOCKS[b][1]
                dve.wait_ge(pv, b + 1)
                if b >= 2:
                    dve.wait_ge(store[b % 2], 16 * (b // 2))
                nc.vector.tensor_copy(o[b % 2][:, :, 0:lq], ob[b % 2][:, :].rearrange("p (j q) -> p j q", j=GROUP)[:, :, 0:lq])\
                  .then_inc(o_out, 1)

            mask(0)
            for b in range(nb):
                norm(b)
                if b + 1 < nb:
                    mask(b + 1)
                out(b)

        @block.scalar
        def _(act):
            for b, (q0, lq, k0, nk, m0) in enumerate(BLOCKS):
                act.wait_ge(prep, b + 1)
                k = small[b % 2]
                for hd in range(N_HEADS):
                    act.activation(s[b % 2][0:lq, hd, 0:nk], s[b % 2][0:lq, hd, 0:nk], ACT.Exp, bias=k[0:lq, 2, hd:hd + 1],
                                   scale=HEAD_DIM ** -0.5, accum_out=k[0:lq, 4, hd:hd + 1])
                act.activation(k[0:lq, 3, :], k[0:lq, 3, :], ACT.Exp).then_inc(exped, 1)
                for kv in range(N_KV):
                    for ci, (c, m) in enumerate(key_tiles(b)):
                        u = before[(b, kv, ci)]
                        act.wait_ge(turned, u + 1)
                        act.activation(pt[u % 4][0:m, :, 0:lq], tr[u % 4][0:m, :].rearrange("p (j q) -> p j q", j=GROUP)[:, :, 0:lq],
                                       ACT.Copy).then_inc(copied, 1)
    g.sb.at = top


VBI = {t0: i for i, (t0, _) in enumerate(VB)}


def hyena_steps():
    units = [(s, j) for s in (1, 0) for j in range(CT)]
    n = len(units)
    steps = [("hgen", 0), ("kf", 0, 0), ("kf", 0, 1), ("hgen", 1), ("zt", 0, 0)]
    for u in range(n):
        steps.append(("fwd", u, 0))
        if u + 1 < n:
            steps.append(("kf", u + 1, 0))
        steps += [("yt", u, 0), ("inv", u, 0)]
        if u + 1 < n:
            steps.append(("kf", u + 1, 1))
        steps += [("zt", u, 1), ("fwd", u, 1)]
        if u + 2 < n:
            steps.append(("hgen", u + 2))
        if u + 1 < n:
            steps.append(("zt", u + 1, 0))
        steps += [("yt", u, 1), ("inv", u, 1)]
    return units, steps


def stage_hyena(g):
    nc, io, S = g.nc, g.io, g.sem
    top = g.sb.at
    sb = g.sb
    ahead = [[sb(f"ahead{s}_{x}", [P, NT[s], W[s]], F32R) for x in ("hi", "lo")] for s in range(2)]
    back = [[sb(f"back{s}_{x}", [P, NK[s], LENS[s]], F32R) for x in ("hi", "lo")] for s in range(2)]
    decay = [sb("decay", [P, NT[0], P]) for _ in range(2)]
    wout = [sb("filt_wout", [FILT_HIDDEN, 4, P]) for _ in range(2)]
    taps = [sb("filter_taps", [P, 4, P]) for _ in range(2)]
    pair = [sb("taps_sum_diff", [P, 2, 2, P]) for _ in range(2)]
    hs = [sb(f"taps_{x}", [P, NT[0], 2, 2, P], F32R) for x in ("hi", "lo")]
    kf = [sb("spectrum", [P, 2, W[0]]) for _ in range(2)]
    src = [sb("v_x1_x2", [P, 3, LENS[0]]) for _ in range(2)]
    z = [sb("z", [P, LENS[0]]) for _ in range(2)]
    zt = [sb(f"z_turned_{x}", [P, NT[0], P], F32R) for x in ("hi", "lo")]
    prodA = [sb("zk_real", [P, 2, FG[0]]) for _ in range(2)]
    prodB = [sb("zk_imag", [P, 2, FG[0]]) for _ in range(2)]
    y = sb("y_spectrum", [P, W[0]])
    yt = [sb(f"y_turned_{x}", [P, NK[0], P], F32R) for x in ("hi", "lo")]
    ident = g.ident
    (cd, hg, h_decayed, h_sum, h_hi, h_lo, kmm, k_out, v_in0, v_in1, dec_in0, dec_in1, ztm, zt_hi, zt_lo, fmm, f_mul, y_out,
     ytm, yt_hi, yt_lo, imm_, gated, st0, st1, done_fwd, done_inv) = S(
        "hy_const0 hy_taps_mm hy_decayed hy_sum_diff hy_taps_hi hy_taps_lo hy_spec_mm hy_spec_out hy_v_in0 hy_v_in1 hy_dec_in0 "
        "hy_dec_in1 hy_zt_mm hy_zt_hi hy_zt_lo hy_fwd_mm hy_fwd_mul hy_y_out hy_yt_mm hy_yt_hi hy_yt_lo hy_inv_mm hy_gated "
        "hy_store0 hy_store1 hy_fwd_done hy_inv_done")
    cb, ca0, cb0 = S("hy_const_back1 hy_const_ahead0 hy_const_back0")
    const_a = [ca0, cd]
    const_b = [cb0, cb]
    v_in, dec_in, store = [v_in0, v_in1], [dec_in0, dec_in1], [st0, st1]
    units, steps = hyena_steps()
    hb, kb, tb, ib = [g.ps[0], g.ps[1]], [g.ps[2], g.ps[3]], [g.ps[4], g.ps[5]], [g.ps[6], g.ps[7]]
    pos, nh, nk, nt_, nf, nyt, nkf, nzt = {}, 0, 0, 0, 0, 0, 0, 0
    for st in steps:
        s = units[st[1]][0]
        pos[st] = dict(h=nh, k=nk, t=nt_, f=nf, yt=nyt, kf=nkf, zt=nzt)
        if st[0] == "hgen":
            nh += NT[s]
        elif st[0] == "kf":
            nk += GROUPS[s]
            nkf += GROUPS[s]
        elif st[0] == "fwd":
            nk += GROUPS[s]
            nf += GROUPS[s]
        elif st[0] == "zt":
            nt_ += -(-NT[s] // 4)
            nzt += -(-NT[s] // 4)
        elif st[0] == "yt":
            nt_ += -(-NK[s] // 4)
            nyt += -(-NK[s] // 4)
    kuse, tuse = [], []
    for st in steps:
        s = units[st[1]][0]
        if st[0] in ("kf", "fwd"):
            for q in range(GROUPS[s]):
                kuse.append((k_out, 1 + sum(1 for a, _ in kuse if a is k_out)) if st[0] == "kf"
                            else (f_mul, 1 + sum(1 for a, _ in kuse if a is f_mul)))
        if st[0] in ("zt", "yt"):
            for q in range(-(-(NT if st[0] == "zt" else NK)[s] // 4)):
                sm = zt_lo if st[0] == "zt" else yt_lo
                tuse.append((sm, 1 + sum(1 for a, _ in tuse if a is sm)))

    def tsize(s, t):
        return min(P, LENS[s] - t * P)

    def ksize(s, k):
        return min(P, W[s] - k * P)

    def order(st):
        return sum(1 for x in steps[:steps.index(st)] if x[0] == st[0])

    with nc.Block() as block:
        @block.gpsimd
        def _(pool):
            for s in (1, 0):
                for tab, dst, sem, full, rows in ((f"ahead{s}", ahead[s], const_a[s], NT[s] - 1, LENS[s]),
                                                  (f"back{s}", back[s], const_b[s], NK[s] - 1, W[s])):
                    for x in range(2):
                        if tab[0] == "a":
                            nc.gpsimd.dma_start(dst[x][:, 0:full, :], io[tab][x, 0:full * P, :].rearrange("(t p) w -> p t w", p=P)).then_inc(sem, 16)
                        else:
                            nc.gpsimd.dma_start(dst[x][:, 0:full, :], io[tab][x, 0:full * P, :].rearrange("(t p) w -> p t w", p=P)).then_inc(sem, 16)
                        nc.gpsimd.dma_start(dst[x][0:rows - full * P, full, :], io[tab][x, full * P:rows, :]).then_inc(sem, 16)
            for st in steps:
                s, j = units[st[1]]
                if st[0] == "hgen":
                    for t in range(NT[s]):
                        u, m = pos[st]["h"] + t, tsize(s, t)
                        pool.wait_ge(h_decayed, u + 1)
                        if u >= 2:
                            pool.wait_ge(h_lo, u - 1)
                        pool_a = taps[u % 2]
                        nc.gpsimd.tensor_tensor(pair[u % 2][0:m, 0, :, :], pool_a[0:m, 0:2, :], pool_a[0:m, 2:4, :], ALU.add)
                        nc.gpsimd.tensor_tensor(pair[u % 2][0:m, 1, :, :], pool_a[0:m, 0:2, :], pool_a[0:m, 2:4, :], ALU.subtract)\
                          .then_inc(h_sum, 1)
                elif st[0] == "fwd":
                    f = FG[s]
                    for q in range(GROUPS[s]):
                        u = pos[st]["f"] + q
                        pool.wait_ge(f_mul, u + 1)
                        if q == 0:
                            k = order(st)
                            if k:
                                pool.wait_ge(ytm, sum(-(-NK[units[x[1]][0]] // 4) for x in steps if x[0] == "yt" and order(x) < k))
                        A, B = prodA[u % 2], prodB[u % 2]
                        yy = y[:, 2 * f * q:2 * f * (q + 1)].rearrange("p (c f) -> p c f", c=2)
                        nc.gpsimd.tensor_tensor(yy[:, 0, :], A[:, 0, 0:f], B[:, 1, 0:f], ALU.subtract)
                        nc.gpsimd.tensor_tensor(yy[:, 1, :], B[:, 0, 0:f], A[:, 1, 0:f], ALU.add).then_inc(y_out, 1)

        @block.sync
        def _(sp):
            def unit_in(u):
                s, j = units[u]
                n = LENS[s]
                full = NT[s] - 1
                if u >= 2:
                    sp.wait_ge(hg, pos[("hgen", u - 2)]["h"] + NT[units[u - 2][0]])
                    sp.wait_ge(h_decayed, pos[("hgen", u - 2)]["h"] + NT[units[u - 2][0]])
                sp.dma_start(wout[u % 2][:, :, :], io["hy_filt_wout"][0].rearrange("k (q c) -> k q c", q=4)[:, :, j * P:(j + 1) * P])\
                  .then_inc(dec_in[u % 2], 16)
                sp.dma_start(decay[u % 2][:, 0:full, :], io[f"decay{s}"][0:full * P, j * P:(j + 1) * P].rearrange("(t p) c -> p t c", p=P))\
                  .then_inc(dec_in[u % 2], 16)
                sp.dma_start(decay[u % 2][0:n - full * P, full, :], io[f"decay{s}"][full * P:n, j * P:(j + 1) * P]).then_inc(dec_in[u % 2], 16)

            def gates_in(u):
                s, j = units[u]
                n = LENS[s]
                if u >= 2:
                    sp.wait_ge(gated, 2 * (u - 1))
                at = (0, LENS[0] + 1)[s]
                sp.dma_start(src[u % 2][:, :, 0:n], g.hyS.rearrange("(q j p) t -> j p q t", q=3, p=P)[j, :, :, at:at + n]).then_inc(v_in[u % 2], 16)

            unit_in(0)
            unit_in(1)
            gates_in(0)
            for u, (s, j) in enumerate(units):
                if u + 1 < len(units):
                    gates_in(u + 1)
                if u + 2 < len(units):
                    unit_in(u + 2)
                sp.wait_ge(gated, 2 * u + 2)
                sp.dma_start(g.upS[ATTN + j * P:ATTN + (j + 1) * P, STARTS[s]:STARTS[s] + LENS[s]], z[1][:, 0:LENS[s]] if u % 2 == 0 else g.zx[:, 0:LENS[s]])\
                  .then_inc(store[u % 2], 16)
            sp.wait_ge(store[0], 16 * CT)
            sp.wait_ge(store[1], 16 * CT)

        @block.tensor
        def _(pe):
            for st in steps:
                s, j = units[st[1]]
                p_ = pos[st]
                n, f = LENS[s], FG[s]
                if st[0] == "hgen":
                    pe.wait_ge(dec_in[st[1] % 2], 48 * (st[1] // 2 + 1))
                    for t in range(NT[s]):
                        u = p_["h"] + t
                        if u >= 2:
                            pe.wait_ge(h_decayed, u - 1)
                        t0 = STARTS[s] + t * P
                        nc.tensor.matmul(hb[u % 2][0:tsize(s, t), :], g.feat[:, t0:t0 + tsize(s, t)],
                                         wout[st[1] % 2][:, :, :].rearrange("k q c -> k (q c)"), start=True, stop=True).then_inc(hg, 1)
                elif st[0] == "kf":
                    o = st[2]
                    pe.wait_ge(h_lo, pos[("hgen", st[1])]["h"] + NT[s])
                    pe.wait_ge(const_a[s], 64)
                    for q in range(GROUPS[s]):
                        u = p_["k"] + q
                        if u >= 2:
                            pe.wait_ge(*kuse[u - 2])
                        for c in range(2):
                            for t in range(NT[s]):
                                m = tsize(s, t)
                                at = (2 * q + c) * f
                                last = three_passes(nc, kb[u % 2][:, c * f:(c + 1) * f], hs[0][0:m, t, c, o, :], hs[1][0:m, t, c, o, :],
                                                    ahead[s][0][0:m, t, at:at + f], ahead[s][1][0:m, t, at:at + f], t == 0, t == NT[s] - 1)
                        last.then_inc(kmm, 1)
                elif st[0] == "zt":
                    o = st[2]
                    if o == 0:
                        pe.wait_ge(v_in[st[1] % 2], 16 * (st[1] // 2 + 1))
                        zz = src[st[1] % 2][:, 0, :]
                    else:
                        pe.wait_ge(gated, 2 * st[1] + 1)
                        zz = z[0]
                    for b in range(-(-NT[s] // 4)):
                        u = p_["t"] + b
                        if u >= 2:
                            pe.wait_ge(*tuse[u - 2])
                        for t in range(4 * b, min(4 * b + 4, NT[s])):
                            m = tsize(s, t)
                            last = nc.tensor.transpose(tb[u % 2][0:m, (t % 4) * P:(t % 4 + 1) * P], zz[:, t * P:t * P + m], ident[:, :])
                        last.then_inc(ztm, 1)
                elif st[0] == "fwd":
                    pe.wait_ge(zt_lo, pos[("zt", st[1], st[2])]["zt"] + -(-NT[s] // 4))
                    for q in range(GROUPS[s]):
                        u = p_["k"] + q
                        if u >= 2:
                            pe.wait_ge(*kuse[u - 2])
                        for t in range(NT[s]):
                            m = tsize(s, t)
                            at = 2 * q * f
                            last = three_passes(nc, kb[u % 2][:, 0:2 * f], zt[0][0:m, t, :], zt[1][0:m, t, :],
                                                ahead[s][0][0:m, t, at:at + 2 * f], ahead[s][1][0:m, t, at:at + 2 * f], t == 0, t == NT[s] - 1)
                        last.then_inc(fmm, 1)
                elif st[0] == "yt":
                    pe.wait_ge(y_out, pos[("fwd", st[1], st[2])]["f"] + GROUPS[s])
                    for b in range(-(-NK[s] // 4)):
                        u = p_["t"] + b
                        if u >= 2:
                            pe.wait_ge(*tuse[u - 2])
                        for k in range(4 * b, min(4 * b + 4, NK[s])):
                            m = ksize(s, k)
                            last = nc.tensor.transpose(tb[u % 2][0:m, (k % 4) * P:(k % 4 + 1) * P], y[:, k * P:k * P + m], ident[:, :])
                        last.then_inc(ytm, 1)
                else:
                    pe.wait_ge(const_b[s], 64)
                    pe.wait_ge(yt_lo, pos[("yt", st[1], st[2])]["yt"] + -(-NK[s] // 4))
                    k_inv = order(st)
                    if k_inv:
                        pe.wait_ge(gated, k_inv)
                    cuts = [(0, 264), (264, 264)] if s == 0 else [(0, 272)]
                    for b, (c0, cn) in enumerate(cuts):
                        for k in range(NK[s]):
                            m = ksize(s, k)
                            last = three_passes(nc, ib[b][:, 0:cn], yt[0][0:m, k, :], yt[1][0:m, k, :],
                                                back[s][0][0:m, k, c0:c0 + cn], back[s][1][0:m, k, c0:c0 + cn], k == 0, k == NK[s] - 1)
                    last.then_inc(imm_, 1)

        def split_turns(eng, st, count, base_sem, base, dst, mine, size):
            s = units[st[1]][0]
            for b in range(-(-count // 4)):
                u = pos[st]["t"] + b
                eng.wait_ge(base_sem, base + b + 1)
                tiles = list(range(4 * b, min(4 * b + 4, count)))
                full = [t for t in tiles if size(s, t) == P]
                parts = ([(full[0], len(full), P)] if full else []) + [(t, 1, size(s, t)) for t in tiles if size(s, t) < P]
                for i, (t, k, m) in enumerate(parts):
                    bank = tb[u % 2][0:m, :].rearrange("p (k c) -> p k c", k=4)[:, t % 4:t % 4 + k, :]
                    yield b, i == len(parts) - 1, bank, [d[0:m, t:t + k, :] for d in dst]

        @block.scalar
        def _(act):
            for st in steps:
                s, j = units[st[1]]
                f = FG[s]
                if st[0] == "hgen":
                    for t in range(NT[s]):
                        u, m = pos[st]["h"] + t, tsize(s, t)
                        act.wait_ge(h_sum, u + 1)
                        if t == 0 and order(st):
                            act.wait_ge(kmm, pos[("kf", st[1] - 1, 1)]["kf"] + GROUPS[units[st[1] - 1][0]])
                        act.activation(hs[0][0:m, t, :, :, :], pair[u % 2][0:m, :, :, :], ACT.Copy).then_inc(h_hi, 1)
                elif st[0] == "kf":
                    o = st[2]
                    if o == 0 and st[1] >= 2:
                        act.wait_ge(f_mul, pos[("fwd", st[1] - 2, 1)]["f"] + GROUPS[units[st[1] - 2][0]])
                    for q in range(GROUPS[s]):
                        u = pos[st]["k"] + q
                        act.wait_ge(kmm, pos[st]["kf"] + q + 1)
                        dst = kf[st[1] % 2][:, o, 2 * q * f:2 * (q + 1) * f]
                        skip = g.taps[:, 4 * HY_TILES + o * CT + j:4 * HY_TILES + o * CT + j + 1]
                        act.activation(dst[:, 0:f], kb[u % 2][:, 0:f], ACT.Identity, bias=skip)
                        act.activation(dst[:, f:2 * f], kb[u % 2][:, f:2 * f], ACT.Copy).then_inc(k_out, 1)
                elif st[0] == "zt":
                    k = order(st)
                    if k:
                        act.wait_ge(fmm, sum(GROUPS[units[x[1]][0]] for x in steps if x[0] == "fwd" and order(x) < k))
                    for b, last, bank, (hi, lo) in split_turns(act, st, NT[s], ztm, pos[st]["zt"], zt, zt_hi, tsize):
                        ins = act.activation(hi, bank, ACT.Copy)
                        if last:
                            ins.then_inc(zt_hi, 1)
                elif st[0] == "yt":
                    k = order(st)
                    if k:
                        act.wait_ge(imm_, k)
                    for b, last, bank, (hi, lo) in split_turns(act, st, NK[s], ytm, pos[st]["yt"], yt, yt_hi, ksize):
                        ins = act.activation(hi, bank, ACT.Copy)
                        if last:
                            ins.then_inc(yt_hi, 1)

        @block.vector
        def _(dve):
            for st in steps:
                s, j = units[st[1]]
                n, f = LENS[s], FG[s]
                if st[0] == "hgen":
                    def lower(t):
                        u, m = pos[st]["h"] + t, tsize(s, t)
                        dve.wait_ge(h_hi, u + 1)
                        nc.vector.tensor_tensor(hs[1][0:m, t, :, :, :], pair[u % 2][0:m, :, :, :], hs[0][0:m, t, :, :, :].bitcast(F32),
                                                ALU.subtract).then_inc(h_lo, 1)
                    dve.wait_ge(dec_in[st[1] % 2], 48 * (st[1] // 2 + 1))
                    for t in range(NT[s]):
                        u, m = pos[st]["h"] + t, tsize(s, t)
                        dve.wait_ge(hg, u + 1)
                        if u >= 2:
                            dve.wait_ge(h_sum, u - 1)
                        nc.vector.tensor_tensor(taps[u % 2][0:m, :, :], hb[u % 2][0:m, :].rearrange("p (q c) -> p q c", q=4),
                                                decay[st[1] % 2][0:m, t, :].unsqueeze(1).broadcast_to([m, 4, P]), ALU.mult).then_inc(h_decayed, 1)
                        if t:
                            lower(t - 1)
                    lower(NT[s] - 1)
                elif st[0] == "zt":
                    for b, last, bank, (hi, lo) in split_turns(dve, st, NT[s], zt_hi, pos[st]["zt"], zt, zt_lo, tsize):
                        ins = nc.vector.tensor_tensor(lo, bank, hi.bitcast(F32), ALU.subtract)
                        if last:
                            ins.then_inc(zt_lo, 1)
                elif st[0] == "yt":
                    for b, last, bank, (hi, lo) in split_turns(dve, st, NK[s], yt_hi, pos[st]["yt"], yt, yt_lo, ksize):
                        ins = nc.vector.tensor_tensor(lo, bank, hi.bitcast(F32), ALU.subtract)
                        if last:
                            ins.then_inc(yt_lo, 1)
                elif st[0] == "fwd":
                    o = st[2]
                    dve.wait_ge(k_out, pos[("kf", st[1], o)]["kf"] + GROUPS[s])
                    for q in range(GROUPS[s]):
                        u, b = pos[st]["f"] + q, pos[st]["k"] + q
                        dve.wait_ge(fmm, u + 1)
                        if u >= 2:
                            dve.wait_ge(y_out, u - 1)
                        zf = kb[b % 2][:, 0:2 * f].rearrange("p (c f) -> p c f", c=2)
                        spec = kf[st[1] % 2][:, o, :]
                        for c, dst in enumerate((prodA[u % 2], prodB[u % 2])):
                            at = (2 * q + c) * f
                            last = nc.vector.tensor_tensor(dst[:, :, 0:f], zf, spec[:, at:at + f].unsqueeze(1).broadcast_to([P, 2, f]), ALU.mult)
                        last.then_inc(f_mul, 1)
                elif st[0] == "inv":
                    o, u = st[2], st[1]
                    dve.wait_ge(imm_, order(st) + 1)
                    if o == 0:
                        dst = z[0]
                    else:
                        dst = z[1] if u % 2 == 0 else g.zx
                        if u >= 2:
                            dve.wait_ge(store[u % 2], 16 * (u // 2))
                    cuts = [(0, 264), (264, 264)] if s == 0 else [(0, 272)]
                    if o == 0:
                        dve.wait_ge(v_in[u % 2], 16 * (u // 2 + 1))
                    for b, (c0, cn) in enumerate(cuts):
                        last = nc.vector.tensor_tensor(dst[:, c0:c0 + cn], ib[b][:, 0:cn], src[u % 2][:, 1 + o, c0:c0 + cn], ALU.mult)
                    last.then_inc(gated, 1)
    g.sb.at = top


def stage_merge(g):
    nc, io, S = g.nc, g.io, g.sem
    sb = g.sb
    mhi, mlo = g.mhi, g.mlo
    top = sb.at
    up = sb("up_in", [P, KT, T])
    uhi = sb("up_in_hi", [P, KT, T], F32R)
    ulo = sb("up_in_lo", [P, KT, T], F32R)
    raw = [sb("wu_raw", [P, KT, WCH]) for _ in range(2)]
    whi = [sb("wu_hi", [P, KT, WCH], F32R) for _ in range(1)]
    wlo = [sb("wu_lo", [P, KT, WCH], F32R) for _ in range(1)]
    sig = [sb("sig_pair", [P, 2, T]) for _ in range(2)]
    ga = [sb("gated_pair", [P, 2, HALF]) for _ in range(1)]
    mm_ = sb("merged", [P, HALF])
    (up_in, u_hi, u_lo, w0, w1, wh, wl, sg0, sg1, prod, gd, summed, m_hi, m_lo) = S(
        "mg_up_in mg_u_hi mg_u_lo mg_w0 mg_w1 mg_wh mg_wl mg_sg0 mg_sg1 mg_prod mg_gated mg_sum mg_m_hi mg_m_lo")
    wsem, sgs = [w0, w1], [sg0, sg1]
    NCH = D // WCH
    banks = [(g.ps[0], g.ps[1]), (g.ps[2], g.ps[3]), (g.ps[4], g.ps[5]), (g.ps[6], g.ps[7])]
    with nc.Block() as block:
        @block.sync
        def _(sp):
            def load(c):
                if c >= 2:
                    sp.wait_ge(wl, c - 1)
                w = raw[c % 2]
                for kv in range(N_KV):
                    sp.dma_start(w[kv * HEAD_DIM:(kv + 1) * HEAD_DIM, 0:GROUP, :],
                                 io["w_attn_up"][0].rearrange("(v j d) n -> v d j n", v=N_KV, d=HEAD_DIM)[kv, :, :, c * WCH:(c + 1) * WCH])\
                      .then_inc(wsem[c % 2], 16)
                sp.dma_start(w[:, GROUP:KT, :], io["w_hyena_up"][0].rearrange("(j p) n -> p j n", p=P)[:, :, c * WCH:(c + 1) * WCH])\
                  .then_inc(wsem[c % 2], 16)

            def load_sig(m):
                if m >= 2:
                    sp.wait_ge(gd, 2 * (m - 1))
                sp.dma_start(sig[m % 2][:, :, :], g.sigS.rearrange("(q m p) t -> m p q t", q=2, p=P)[m]).then_inc(sgs[m % 2], 16)
            for k in range(KT):
                sp.dma_start(up[:, k, :], g.upS[k * P:(k + 1) * P, :]).then_inc(up_in, 16)
            load(0)
            load(1)
            load_sig(0)
            load_sig(1)
            for m in range(2, KT):
                load_sig(m)
                if m % 2 == 0 and m // 2 + 1 < NCH:
                    load(m // 2 + 1)

        @block.scalar
        def _(act):
            act.wait_ge(up_in, 16 * KT)
            for k in range(KT):
                act.activation(uhi[:, k, :], up[:, k, :], ACT.Copy).then_inc(u_hi, 1)
            for m in range(KT):
                c = m // 2
                if m % 2 == 0:
                    act.wait_ge(wsem[c % 2], 48 * (c // 2 + 1))
                    if c:
                        act.wait_ge(prod, 4 * c)
                    act.activation(whi[0][:, :, :], raw[c % 2][:, :, :], ACT.Copy).then_inc(wh, 1)
                for h in range(2):
                    act.wait_ge(summed, 2 * m + h + 1)
                    act.activation(mhi[:, m, h * HALF:(h + 1) * HALF], mm_[:, :], ACT.Copy).then_inc(m_hi, 1)

        @block.vector
        def _(dve):
            for k in range(KT):
                dve.wait_ge(u_hi, k + 1)
                nc.vector.tensor_tensor(ulo[:, k, :], up[:, k, :], uhi[:, k, :].bitcast(F32), ALU.subtract).then_inc(u_lo, 1)
            for m in range(KT):
                dve.wait_ge(sgs[m % 2], 16 * (m // 2 + 1))
                for h in range(2):
                    u = 2 * m + h
                    dve.wait_ge(prod, u + 1)
                    if u:
                        dve.wait_ge(summed, u)
                    for q in range(2):
                        last = nc.vector.tensor_tensor(ga[0][:, q, :], banks[u % 4][q][:, 0:HALF], sig[m % 2][:, q, h * HALF:(h + 1) * HALF],
                                                       ALU.mult)
                    last.then_inc(gd, 1)
                    dve.wait_ge(gd, u + 1)
                    if u:
                        dve.wait_ge(m_lo, u)
                    nc.vector.tensor_tensor(mm_[:, :], ga[0][:, 0, :], ga[0][:, 1, :], ALU.add).then_inc(summed, 1)
                    dve.wait_ge(m_hi, u + 1)
                    nc.vector.tensor_tensor(mlo[:, m, h * HALF:(h + 1) * HALF], mm_[:, :], mhi[:, m, h * HALF:(h + 1) * HALF].bitcast(F32),
                                            ALU.subtract).then_inc(m_lo, 1)

        @block.gpsimd
        def _(pool):
            for c in range(NCH):
                pool.wait_ge(wh, c + 1)
                nc.gpsimd.tensor_tensor(wlo[0][:, :, :], raw[c % 2][:, :, :], whi[0][:, :, :].bitcast(F32), ALU.subtract).then_inc(wl, 1)

        @block.tensor
        def _(pe):
            pe.wait_ge(u_lo, KT)
            for m in range(KT):
                if m % 2 == 0:
                    pe.wait_ge(wh, m // 2 + 1)
                    pe.wait_ge(wl, m // 2 + 1)
                for h in range(2):
                    u = 2 * m + h
                    if u >= 4:
                        pe.wait_ge(gd, u - 3)
                    for q in range(2):
                        for k in range(4):
                            kt = 4 * q + k
                            c0 = (m % 2) * P
                            last = three_passes(nc, banks[u % 4][q][:, 0:HALF], whi[0][:, kt, c0:c0 + P], wlo[0][:, kt, c0:c0 + P],
                                                uhi[:, kt, h * HALF:(h + 1) * HALF], ulo[:, kt, h * HALF:(h + 1) * HALF], k == 0, k == 3)
                    last.then_inc(prod, 1)
    sb.at = top


def stage_route(g):
    nc, io, S = g.nc, g.io, g.sem
    sb = g.sb
    mhi, mlo, ident = g.mhi, g.mlo, g.ident
    top = sb.at
    NTOK = len(TOK_TILES)
    raw = sb("wo_raw", [P, KT, D])
    whi = sb("wo_hi", [P, KT, D], F32R)
    wlo = sb("wo_lo", [P, KT, D], F32R)
    h = [sb("residual_in", [P, D]) for _ in range(2)]
    hn = [sb("ffn_normed", [P, D]) for _ in range(2)]
    gain = sb("ffn_gain", [P, D])
    hT = sb("ffn_turned", [P, KT, P])
    wr = sb("w_router", [P, KT, E])
    ss = sb("square_sums", [P, 2 * NTOK])
    lg = sb("logits", [P, NTOK, E])
    red = sb("softmax_cols", [P, 2, NTOK])
    af = [[sb(f"affinity{s}_{x}", [E, LENS[s]]) for x in range(2)] for s in range(2)]
    rounds = [-(-c // 8) for c in CAPS]
    val = [sb(f"top_values{s}", [E, 8 * rounds[s]]) for s in range(2)]
    ix = [sb(f"top_index{s}", [E, 8 * rounds[s]], U32) for s in range(2)]
    both = sb("slots_by_expert", [E, 2, SLOTS])
    (w_in, w_hi, w_lo, hin0, hin1, cin, prod, h2d, sq, mean, root, hnd, st0, st1, trn, t_act, t_dve, lmm, lgd, exd, afd,
     aft, own, bd, btd, hT_used, hst0, hst1) = S(
        "rt_w_in rt_w_hi rt_w_lo rt_hin0 rt_hin1 rt_cin rt_prod rt_h2 rt_sq rt_mean rt_root rt_hn rt_st0 rt_st1 rt_trn "
        "rt_t_act rt_t_dve rt_lmm rt_lg rt_exp rt_aff rt_afft rt_own rt_both rt_both_turned rt_ht_used rt_hst0 rt_hst1")
    hin, st, hst = [hin0, hin1], [st0, st1], [hst0, hst1]
    pieces = [token_pieces(t0, m, io["x_prompt"][0], io["x_sample"][0], io["meta_tokens"]) for t0, m in TOK_TILES]
    total = [[0, 0]]
    for i, ps_ in enumerate(pieces):
        now = list(total[-1])
        now[i % 2] += 16 * len(ps_)
        total.append(now)
    acc = [(g.ps[0], g.ps[1]), (g.ps[2], g.ps[3])]
    w_sems = S(" ".join(f"rt_w{k}" for k in range(KT)))

    with nc.Block() as block:
        @block.sync
        def _(sp):
            def load(i):
                if i >= 2:
                    sp.wait_ge(hnd, i - 1)
                    sp.wait_ge(hst[i % 2], 16 * (i // 2))
                for r0, src in pieces[i]:
                    sp.dma_start(h[i % 2][r0:r0 + src.shape[0], :], src).then_inc(hin[i % 2], 16)
            for k in range(KT):
                sp.dma_start(raw[:, k, :], io["w_out"][0, k * P:(k + 1) * P, :]).then_inc(w_sems[k], 16)
            load(0)
            load(1)
            sp.dma_start(gain[:, :], io["norm_ffn_g"][0].partition_broadcast(P)).then_inc(cin, 16)
            sp.dma_start(wr[:, :, :], io["w_router"][0].rearrange("(t p) e -> p t e", p=P)).then_inc(cin, 16)
            for i, (t0, m) in enumerate(TOK_TILES):
                sp.wait_ge(h2d, i + 1)
                sp.dma_start(g.accS[t0:t0 + m, :], h[i % 2][0:m, :]).then_inc(hst[i % 2], 16)
                sp.wait_ge(hnd, i + 1)
                sp.dma_start(g.hnS[t0:t0 + m, :], hn[i % 2][0:m, :]).then_inc(st[i % 2], 16)
                if i + 2 < NTOK:
                    load(i + 2)
            for k in range(2):
                sp.wait_ge(st[k], 16 * ((NTOK + 1 - k) // 2))
                sp.wait_ge(hst[k], 16 * ((NTOK + 1 - k) // 2))

        @block.tensor
        def _(pe):
            def product(i):
                t0, m = TOK_TILES[i]
                if i >= 2:
                    pe.wait_ge(h2d, i - 1)
                for b in range(2):
                    for k in range(KT):
                        if i == 0 and b == 0:
                            pe.wait_ge(w_hi, k + 1)
                            pe.wait_ge(w_lo, k + 1)
                        last = three_passes(nc, acc[i % 2][b][0:m, :], mhi[:, k, t0:t0 + m], mlo[:, k, t0:t0 + m],
                                            whi[:, k, b * BANK:(b + 1) * BANK], wlo[:, k, b * BANK:(b + 1) * BANK], k == 0, k == KT - 1)
                last.then_inc(prod, 1)

            def turn(i):
                t0, m = TOK_TILES[i]
                pe.wait_ge(hnd, i + 1)
                if i:
                    pe.wait_ge(t_act, i)
                    pe.wait_ge(t_dve, i)
                for k in range(KT):
                    last = nc.tensor.transpose(g.ps[4 + k // 4][:, (k % 4) * P:(k % 4) * P + m], hn[i % 2][0:m, k * P:(k + 1) * P],
                                               ident[0:m, 0:m])
                last.then_inc(trn, 1)

            def logits(i):
                t0, m = TOK_TILES[i]
                pe.wait_ge(t_act, i + 1)
                pe.wait_ge(t_dve, i + 1)
                if i:
                    pe.wait_ge(lgd, i)
                for k in range(KT):
                    last = nc.tensor.matmul(g.ps[6][0:m, 0:E], hT[:, k, 0:m], wr[:, k, :], start=(k == 0), stop=(k == KT - 1))
                last.then_inc(lmm, 1)

            pe.wait_ge(cin, 32)
            product(0)
            for i in range(1, NTOK):
                product(i)
                turn(i - 1)
                logits(i - 1)
            turn(NTOK - 1)
            logits(NTOK - 1)
            pe.wait_ge(afd, 1)
            pe.wait_ge(lgd, NTOK)
            for i, (t0, m) in enumerate(TOK_TILES):
                last = nc.tensor.transpose(g.ps[7 - i // 4][0:E, (i % 4) * P:(i % 4) * P + m], lg[0:m, i, :], ident[0:m, 0:m])
            last.then_inc(aft, 1)
            pe.wait_ge(bd, 4)
            for q in range(2):
                last = nc.tensor.transpose(g.ps[4][0:SLOTS, q * P:q * P + E], both[:, q, :], ident[0:E, 0:E])
            last.then_inc(btd, 1)

        @block.gpsimd
        def _(pool):
            for k in range(KT):
                pool.wait_ge(w_hi, k + 1)
                nc.gpsimd.tensor_tensor(wlo[:, k, :], raw[:, k, :], whi[:, k, :].bitcast(F32), ALU.subtract).then_inc(w_lo, 1)

        @block.scalar
        def _(act):
            for k in range(KT):
                act.wait_ge(w_sems[k], 16)
                act.activation(whi[:, k, :], raw[:, k, :], ACT.Copy).then_inc(w_hi, 1)
            for i, (t0, m) in enumerate(TOK_TILES):
                act.wait_ge(h2d, i + 1)
                if i >= 2:
                    act.wait_ge(trn, i - 1)
                    act.wait_ge(st[i % 2], 16 * (i // 2))
                act.activation(hn[i % 2][0:m, :], h[i % 2][0:m, :], ACT.Square, accum_out=ss[0:m, i:i + 1]).then_inc(sq, 1)
                act.wait_ge(mean, i + 1)
                act.activation(ss[0:m, NTOK + i:NTOK + i + 1], ss[0:m, i:i + 1], ACT.Sqrt).then_inc(root, 1)
                act.wait_ge(trn, i + 1)
                if i:
                    act.wait_ge(lmm, i)
                act.activation(hT[:, 0:4, 0:m], g.ps[4][:, :].rearrange("p (k t) -> p k t", k=4)[:, :, 0:m], ACT.Copy).then_inc(t_act, 1)
            act.wait_ge(own, NTOK + 3)
            act.activation(lg[:, :, :], lg[:, :, :], ACT.Exp).then_inc(exd, 1)

        @block.vector
        def _(dve):
            link = linked(dve, own)
            link(nc.vector.memset(lg[:, :, :], 0.0))
            dve.wait_ge(cin, 32)
            for i, (t0, m) in enumerate(TOK_TILES):
                dve.wait_ge(hin[i % 2], total[i + 1][i % 2])
                dve.wait_ge(prod, i + 1)
                for b in range(2):
                    last = nc.vector.tensor_tensor(h[i % 2][0:m, b * BANK:(b + 1) * BANK], acc[i % 2][b][0:m, :],
                                                   h[i % 2][0:m, b * BANK:(b + 1) * BANK], ALU.add)
                last.then_inc(h2d, 1)
                dve.wait_ge(sq, i + 1)
                nc.vector.tensor_scalar(ss[0:m, i:i + 1], ss[0:m, i:i + 1], 1.0 / D, EPS, ALU.mult, ALU.add).then_inc(mean, 1)
                dve.wait_ge(root, i + 1)
                link(nc.vector.reciprocal(ss[0:m, i:i + 1], ss[0:m, NTOK + i:NTOK + i + 1]))
                nc.vector.scalar_tensor_tensor(hn[i % 2][0:m, :], h[i % 2][0:m, :], ss[0:m, i:i + 1], gain[0:m, :],
                                               ALU.mult, ALU.mult).then_inc(hnd, 1)
                dve.wait_ge(trn, i + 1)
                if i:
                    dve.wait_ge(lmm, i)
                nc.vector.tensor_copy(hT[:, 4:8, 0:m], g.ps[5][:, :].rearrange("p (k t) -> p k t", k=4)[:, :, 0:m]).then_inc(t_dve, 1)
                dve.wait_ge(lmm, i + 1)
                nc.vector.tensor_copy(lg[0:m, i, :], g.ps[6][0:m, 0:E]).then_inc(lgd, 1)
            dve.wait_ge(lgd, NTOK)
            link(nc.vector.tensor_reduce(red[:, 0, :], lg[:, :, :], AX.X, ALU.max))
            link(nc.vector.tensor_tensor(lg[:, :, :], lg[:, :, :], red[:, 0, :].unsqueeze(2).broadcast_to([P, NTOK, E]), ALU.subtract))
            dve.wait_ge(exd, 1)
            link(nc.vector.tensor_reduce(red[:, 0, :], lg[:, :, :], AX.X, ALU.add))
            link(nc.vector.reciprocal(red[:, 1, :], red[:, 0, :]))
            nc.vector.tensor_tensor(lg[:, :, :], lg[:, :, :], red[:, 1, :].unsqueeze(2).broadcast_to([P, NTOK, E]), ALU.mult).then_inc(afd, 1)
            dve.wait_ge(aft, 1)
            link(nc.vector.tensor_copy(af[0][0][:, 0:BANK], g.ps[7][0:E, :]))
            link(nc.vector.tensor_copy(af[0][0][:, BANK:LENS[0]], g.ps[6][0:E, 0:LENS[0] - BANK]))
            link(nc.vector.tensor_copy(af[1][0][:, :], g.ps[6][0:E, LENS[0] - BANK:T - BANK]))
            for s in range(2):
                for r in range(rounds[s]):
                    a, b = af[s][r % 2], af[s][(r + 1) % 2]
                    c = slice(8 * r, 8 * r + 8)
                    link(nc.vector.max(val[s][:, c], a[:, :]))
                    link(nc.vector.max_index(ix[s][:, c], val[s][:, c], a[:, :]))
                    if r + 1 < rounds[s]:
                        link(nc.vector.match_replace(b[:, :], val[s][:, c], a[:, :], -1.0))
            c0 = CAPS[0]
            nc.vector.tensor_copy(both[:, 0, 0:c0], val[0][:, 0:c0]).then_inc(bd, 1)
            nc.vector.tensor_copy(both[:, 0, c0:SLOTS], val[1][:, 0:CAPS[1]]).then_inc(bd, 1)
            nc.vector.tensor_copy(both[:, 1, 0:c0], ix[0][:, 0:c0]).then_inc(bd, 1)
            nc.vector.tensor_scalar(both[:, 1, c0:SLOTS], ix[1][:, 0:CAPS[1]], float(STARTS[1]), None, ALU.add).then_inc(bd, 1)
            dve.wait_ge(btd, 1)
            link(nc.vector.tensor_copy(g.gate_w[0:SLOTS, :], g.ps[4][0:SLOTS, 0:E]))
            link(nc.vector.tensor_copy(g.slot_tok[0:SLOTS, 0:E], g.ps[4][0:SLOTS, P:P + E]))
            link(nc.vector.tensor_copy(g.slot_tok[0:SLOTS, E:E + 1], g.ps[4][0:SLOTS, P:P + 1]))
    sb.at = top


CHUNKS = 12
RING = 6
FCH = FE // 4
FT = FCH // P


def stage_experts(g):
    nc, io, S = g.nc, g.io, g.sem
    sb = g.sb
    ident = g.ident
    top = sb.at
    ring = [sb(f"w_ring{k}", [P, 4096]) for k in range(RING)]
    xe = sb("gathered", [P, D])
    xT = sb("gathered_turned", [P, KT, SLOTS])
    sig = [sb("gate_sigmoid", [P, FT * SLOTS]) for _ in range(2)]
    act_ = [sb("gate_silu", [P, FT * SLOTS]) for _ in range(2)]
    hid = sb("hidden", [P, 4 * FT, SLOTS])
    ye = sb("expert_out", [P, D])
    nxt = sb("slots_next", [P, 1], U32)
    cur = sb("slots_now", [P, 1], U32)
    gcur = sb("gate_now", [P, 1])
    credit = sb("start_credits", [P, 4])
    ld = S(" ".join(f"ex_ld{k}" for k in range(RING)))
    (nxt_set, cur_set, gath, turned, xt_a, xt_d, gmm, umm, sg_done, silu_done, hid_done, ymm, y_done, scat) = S(
        "ex_next ex_cur ex_gathered ex_turned ex_xt_act ex_xt_dve ex_gate_mm ex_up_mm ex_sig ex_silu ex_hid ex_down_mm "
        "ex_y_done ex_scattered")
    gb, ub, yb = [g.ps[0], g.ps[1]], [g.ps[2], g.ps[3]], [g.ps[6], g.ps[7]]
    wg = io["w_exp_gate"][0].rearrange("e (t p) f -> e p t f", p=P)
    wu = io["w_exp_up"][0].rearrange("e (t p) f -> e p t f", p=P)
    wd = io["w_exp_down"][0].rearrange("e (c t p) d -> e c p t d", c=4, p=P)

    with nc.Block() as block:
        @block.sync
        def _(sp):
            def load(e, k):
                dst = ring[k % RING]
                if k < 8:
                    src = (wg, wu)[k % 2][e, :, :, (k // 2) * FCH:(k // 2 + 1) * FCH]
                    sp.dma_start(dst[:, :].rearrange("p (t f) -> p t f", t=KT), src).then_inc(ld[k % RING], 16)
                else:
                    sp.dma_start(dst[:, :].rearrange("p (t d) -> p t d", t=4), wd[e, k - 8]).then_inc(ld[k % RING], 16)

            def used(e, k):
                if k < 8:
                    sp.wait_ge((gmm, umm)[k % 2], 4 * e + k // 2 + 1)
                else:
                    sp.wait_ge(ymm, 4 * e + k - 8 + 1)

            def second_half(e):
                for k in range(RING, CHUNKS):
                    used(e, k - RING)
                    load(e, k)
            for k in range(RING):
                load(0, k)
            for e in range(E - 1):
                second_half(e)
                for k in range(RING):
                    used(e, k + RING)
                    load(e + 1, k)
            second_half(E - 1)

        @block.gpsimd
        def _(pool):
            def gather():
                pool.indirect_dma_start(xe[0:SLOTS, :], None, g.hnS[:, :], bass.IndirectOffsetOnAxis(ap=nxt[0:SLOTS, 0:1], axis=0))\
                    .then_inc(gath, 16)
            pool.wait_ge(nxt_set, 1)
            gather()
            for e in range(E):
                pool.wait_ge(nxt_set, e + 2)
                pool.wait_ge(turned, e + 1)
                gather()
                pool.wait_ge(cur_set, e + 1)
                pool.wait_ge(y_done, e + 2)
                pool.indirect_dma_start(g.accS[:, :], bass.IndirectOffsetOnAxis(ap=cur[0:SLOTS, 0:1], axis=0), ye[0:SLOTS, :], None,
                                        compute_op=ALU.add).then_inc(scat, 16)
                pool.wait_ge(scat, 16 * e + 16)
            pool.wait_ge(gath, 16 * (E + 1))

        @block.tensor
        def _(pe):
            def turn():
                for k in range(KT):
                    last = nc.tensor.transpose(g.ps[4 + k // 4][:, (k % 4) * P:(k % 4) * P + SLOTS], xe[0:SLOTS, k * P:(k + 1) * P],
                                               ident[0:SLOTS, 0:SLOTS])
                last.then_inc(turned, 1)
            pe.wait_ge(gath, 16)
            turn()
            with pe.Fori(0, E) as e:
                pe.wait_ge(xt_a, e + 1)
                pe.wait_ge(xt_d, e + 1)
                for c in range(4):
                    pe.wait_ge(hid_done, 4 * e + c + 1)
                    for q, (bank, sem) in enumerate(((gb[c % 2], gmm), (ub[c % 2], umm))):
                        k = 2 * c + q
                        pe.wait_ge(ld[k % RING], 32 * e + 16 * (k // RING + 1))
                        w = ring[k % RING][:, :].rearrange("p (t f) -> p t f", t=KT)
                        for f in range(FT):
                            for t in range(KT):
                                last = nc.tensor.matmul(bank[:, f * SLOTS:(f + 1) * SLOTS], w[:, t, f * P:(f + 1) * P], xT[:, t, :],
                                                        start=(t == 0), stop=(t == KT - 1))
                        last.then_inc(sem, 1)
                pe.wait_ge(gath, 16 * e + 32)
                turn()
                pe.wait_ge(y_done, e + 1)
                for c in range(4):
                    k = 8 + c
                    pe.wait_ge(ld[k % RING], 32 * e + 32)
                    pe.wait_ge(hid_done, 4 * e + c + 3)
                    w = ring[k % RING][:, :].rearrange("p (t d) -> p t d", t=4)
                    for t in range(4):
                        for b in range(2):
                            last = nc.tensor.matmul(yb[b][0:SLOTS, :], hid[:, 4 * c + t, :], w[:, t, b * BANK:(b + 1) * BANK],
                                                    start=(c == 0 and t == 0), stop=(c == 3 and t == 3))
                    last.then_inc(ymm, 1)

        @block.scalar
        def _(act):
            def turn_out():
                act.activation(xT[:, 0:4, :], g.ps[4][:, :].rearrange("p (k s) -> p k s", k=4)[:, :, 0:SLOTS], ACT.Copy).then_inc(xt_a, 1)
            act.wait_ge(turned, 1)
            turn_out()
            with act.Fori(0, E) as e:
                for c in range(4):
                    act.wait_ge(gmm, 4 * e + c + 1)
                    act.wait_ge(silu_done, 4 * e + c + 1)
                    act.activation(sig[c % 2][:, :], gb[c % 2][:, 0:FT * SLOTS], ACT.Sigmoid).then_inc(sg_done, 1)
                act.wait_ge(turned, e + 2)
                turn_out()

        @block.vector
        def _(dve):
            def turn_out():
                nc.vector.tensor_copy(xT[:, 4:8, :], g.ps[5][:, :].rearrange("p (k s) -> p k s", k=4)[:, :, 0:SLOTS]).then_inc(xt_d, 1)
            nc.vector.tensor_copy(nxt[0:SLOTS, :], g.slot_tok[0:SLOTS, 0:1]).then_inc(nxt_set, 1)
            nc.vector.memset(credit[0:1, 0:1], 0.0).then_inc(hid_done, 2)
            nc.vector.memset(credit[0:1, 1:2], 0.0).then_inc(silu_done, 2)
            nc.vector.memset(credit[0:1, 2:3], 0.0).then_inc(y_done, 1)
            dve.wait_ge(turned, 1)
            turn_out()
            with dve.Fori(0, E) as e:
                dve.wait_ge(gath, 16 * e + 16)
                nc.vector.tensor_copy(nxt[0:SLOTS, :], g.slot_tok[0:SLOTS, bass.ds(e + 1, 1)]).then_inc(nxt_set, 1)
                for c in range(4):
                    dve.wait_ge(sg_done, 4 * e + c + 1)
                    nc.vector.tensor_tensor(act_[c % 2][:, :], gb[c % 2][:, 0:FT * SLOTS], sig[c % 2][:, :], ALU.mult).then_inc(silu_done, 1)
                    dve.wait_ge(silu_done, 4 * e + c + 3)
                    dve.wait_ge(umm, 4 * e + c + 1)
                    nc.vector.tensor_tensor(hid[:, 4 * c:4 * c + 4, :].rearrange("p a s -> p (a s)"), ub[c % 2][:, 0:FT * SLOTS],
                                            act_[c % 2][:, :], ALU.mult).then_inc(hid_done, 1)
                dve.wait_ge(turned, e + 2)
                turn_out()
                dve.wait_ge(gath, 16 * e + 32)
                nc.vector.tensor_copy(gcur[0:SLOTS, :], g.gate_w[0:SLOTS, bass.ds(e, 1)])
                nc.vector.tensor_copy(cur[0:SLOTS, :], g.slot_tok[0:SLOTS, bass.ds(e, 1)]).then_inc(cur_set, 1)
                dve.wait_ge(ymm, 4 * e + 4)
                dve.wait_ge(cur_set, e + 1)
                for b in range(2):
                    last = nc.vector.tensor_scalar(ye[0:SLOTS, b * BANK:(b + 1) * BANK], yb[b][0:SLOTS, :], gcur[0:SLOTS, :], None, ALU.mult)
                last.then_inc(y_done, 1)
    sb.at = top


def stage_finish(g):
    nc, io, S = g.nc, g.io, g.sem
    sb = g.sb
    top = sb.at
    NTOK = len(TOK_TILES)
    h = [sb("h_final", [P, D]) for _ in range(NTOK)]
    o = [sb("out_rows", [P, D]) for _ in range(NTOK)]
    gain = sb("final_gain", [P, D])
    ss = sb("square_sums", [P, 2 * NTOK])
    (cin, sq, mean, root, outd, outs, own) = S("fi_cin fi_sq fi_mean fi_root fi_out fi_stored fi_own")
    hin = S(" ".join(f"fi_in{k}" for k in range(NTOK)))
    with nc.Block() as block:
        @block.sync
        def _(sp):
            for i, (t0, m) in enumerate(TOK_TILES):
                sp.dma_start(h[i][0:m, :], g.accS[t0:t0 + m, :]).then_inc(hin[i], 16)
                if i == 0:
                    sp.dma_start(gain[:, :], io["norm_final_g"].partition_broadcast(P)).then_inc(cin, 16)
            n = 0
            for i, (t0, m) in enumerate(TOK_TILES):
                sp.wait_ge(outd, i + 1)
                for s, y in enumerate(g.out):
                    lo, hi = max(t0, STARTS[s] + N_META), min(t0 + m, STARTS[s] + LENS[s])
                    if lo < hi:
                        off = STARTS[s] + N_META
                        sp.dma_start(y[0, lo - off:hi - off, :], o[i][lo - t0:hi - t0, :]).then_inc(outs, 16)
                        n += 16
            sp.wait_ge(outs, n)

        @block.scalar
        def _(act):
            for i, (t0, m) in enumerate(TOK_TILES):
                act.wait_ge(hin[i], 16)
                act.activation(o[i][0:m, :], h[i][0:m, :], ACT.Square, accum_out=ss[0:m, i:i + 1]).then_inc(sq, 1)
                act.wait_ge(mean, i + 1)
                act.activation(ss[0:m, NTOK + i:NTOK + i + 1], ss[0:m, i:i + 1], ACT.Sqrt).then_inc(root, 1)

        @block.vector
        def _(dve):
            link = linked(dve, own)
            dve.wait_ge(cin, 16)
            for i, (t0, m) in enumerate(TOK_TILES):
                dve.wait_ge(sq, i + 1)
                nc.vector.tensor_scalar(ss[0:m, i:i + 1], ss[0:m, i:i + 1], 1.0 / D, EPS, ALU.mult, ALU.add).then_inc(mean, 1)
                dve.wait_ge(root, i + 1)
                link(nc.vector.reciprocal(ss[0:m, i:i + 1], ss[0:m, NTOK + i:NTOK + i + 1]))
                nc.vector.scalar_tensor_tensor(o[i][0:m, :], h[i][0:m, :], ss[0:m, i:i + 1], gain[0:m, :], ALU.mult, ALU.mult).then_inc(outd, 1)
    sb.at = top


def encode_layer(nc, io, out, debug=None):
    with ExitStack() as ctx:
        g = Ctx()
        g.nc, g.io, g.out = nc, io, out
        g.sem = Semaphores(nc)
        sb = g.sb = Map(nc)
        g.ps = [ctx.enter_context(nc.psum_tensor(f"bank{k}", [P, BANK], F32)) for k in range(8)]

        def scratch(name, shape):
            if debug is not None and name in debug:
                return debug[name]
            return nc.dram_tensor(name, shape, F32, kind="Internal").ap()
        g.hyS = scratch("hy_conv_rows", (3 * HYW, T + 1))
        g.sigS = scratch("gate_rows", (2 * D, T))
        g.upS = scratch("mixer_rows", (D, T))
        g.accS = scratch("residual_rows", (T, D))
        g.hnS = scratch("ffn_rows", (T, D))
        g.ident = sb("ident", [P, P])
        g.taps = sb("conv_taps", [P, 4 * HY_TILES + 2 * CT])
        g.gate_w = sb("slot_gates", [P, E])
        g.slot_tok = sb("slot_tokens", [P, E + 1], U32)
        top = sb.at
        g.feat = sb("filter_features", [FILT_HIDDEN, T])
        g.qk = sb("q_k_rotated", [P, GROUP + 1, T])
        g.v = sb("values", [P, len(VB), P])
        stage_project(g)
        g.sem.end_stage()
        stage_filter_mlp(g)
        g.sem.end_stage()
        stage_attend(g)
        g.sem.end_stage()
        sb.at = top
        sb.at = top + T * 4
        g.zx = sb("z_second", [P, LENS[0]])
        stage_hyena(g)
        g.sem.end_stage()
        sb.at = top
        g.mhi = sb("merged_hi", [P, KT, T], F32R)
        g.mlo = sb("merged_lo", [P, KT, T], F32R)
        stage_merge(g)
        g.sem.end_stage()
        stage_route(g)
        g.sem.end_stage()
        sb.at = top
        stage_experts(g)
        g.sem.end_stage()
        stage_finish(g)
        g.sem.end_stage()


_INS = ["x_prompt", "x_sample", "meta_tokens", "norm_mix_g", "w_in", "attn_sink", "hy_conv_w", "hy_conv_b",
        "hy_filt_w1", "hy_filt_b1", "hy_filt_w2", "hy_filt_b2", "hy_filt_w3", "hy_filt_b3", "hy_filt_freq",
        "hy_filt_wout", "hy_skip", "w_attn_up", "w_hyena_up", "w_out", "norm_ffn_g", "w_router", "w_exp_gate",
        "w_exp_up", "w_exp_down", "norm_final_g"]
_OUTS = [(1, SEQS[0], D), (1, SEQS[1], D)]


def kernel(**inputs):
    import concourse.bacc as _bacc
    from concourse.bass_utils import run_bass_kernel_spmd as _run

    nc = _bacc.Bacc("TRN2", target_bir_lowering=False, num_devices=1)
    arrays = {f"in_{name}": np.ascontiguousarray(inputs[name]) for name in _INS}
    arrays.update({f"in_{name}": a for name, a in shape_tables().items()})
    io = {name[3:]: nc.dram_tensor(name, a.shape, mybir.dt.from_np(a.dtype), kind="ExternalInput").ap()
          for name, a in arrays.items()}
    out = [nc.dram_tensor(f"out_{i}", shape, F32, kind="ExternalOutput").ap() for i, shape in enumerate(_OUTS)]
    encode_layer(nc, io, out)
    r = _run(nc, [arrays], core_ids=[0])
    return tuple(r.results[0][f"out_{i}"] for i in range(len(_OUTS)))
```

```python
import math
from contextlib import ExitStack

import numpy as np

import concourse.bass as bass
from concourse import mybir

F32 = mybir.dt.float32
F32R = mybir.dt.float32r
U32 = mybir.dt.uint32
ALU = mybir.AluOpType
ACT = mybir.ActivationFunctionType
AX = mybir.AxisListType

P = 128
BANK = 512

D = 1024
KT = D // P
N_META = 16
SEQS = (512, 256)
LENS = tuple(s + N_META for s in SEQS)
STARTS = (0, LENS[0])
T = sum(LENS)
HALF = T // 2
TOK_TILES = [(t, min(P, T - t)) for t in range(0, T, P)]

HEAD_DIM = 64
N_HEADS = 8
N_KV = 2
GROUP = N_HEADS // N_KV
ATTN = N_HEADS * HEAD_DIM
KVW = N_KV * HEAD_DIM
WINDOW = 128
HYW = D // 2
CT = HYW // P
HY_TILES = 3 * CT
C_K, C_V = ATTN, ATTN + KVW
C_HY = ATTN + 2 * KVW
C_GATE = C_HY + 3 * HYW
WCH = 256

FILT_EMB, FILT_BANDS, FILT_HIDDEN = 33, 16, 64
E = 16
FE = 2048
CAPS = tuple(2 * n // E for n in LENS)
SLOTS = sum(CAPS)
EPS = 1e-6

BLOCKS = []
for _s, _n in zip(STARTS, LENS):
    for _q in range(0, _n, P):
        _k0, _k1 = max(0, _q - P), min(_n, _q + 2 * P)
        BLOCKS.append((_s + _q, min(P, _n - _q), _s + _k0, _k1 - _k0, _k0 - (_q - P)))
VBLOCK0 = {s + q: i for i, (s, q) in enumerate((s, q) for s, n in zip(STARTS, LENS) for q in range(0, n, P))}

GROUPS = (3, 2)
FG = (178, 138)
W = tuple(2 * g * f for g, f in zip(GROUPS, FG))
NT = tuple(-(-n // P) for n in LENS)
NK = tuple(-(-w // P) for w in W)

TWO_PI = 2.0 * math.pi
MAGIC = 1.5 * 2.0 ** 23
NEG = -1e30


def dft_tables(s):
    n, g, f = LENS[s], GROUPS[s], FG[s]
    size = 2 * n
    k = np.arange(g * f)
    live = (k <= n).astype(np.float64)
    phase = 2 * np.pi * ((np.arange(n)[:, None] * k[None]) % size) / size
    cos, sin = np.cos(phase) * live, np.sin(phase) * live
    ahead = np.stack([cos.reshape(n, g, f), sin.reshape(n, g, f)], 2).reshape(n, 2 * g * f)
    weight = np.where((k == 0) | (k == n), 1.0, 2.0) / size
    back = np.stack([(cos * weight).reshape(n, g, f), (sin * weight).reshape(n, g, f)], 2)
    return ahead.astype(np.float32), np.ascontiguousarray(back.reshape(n, 2 * g * f).T).astype(np.float32)


def halves12(x):
    def top(v):
        u = v.view(np.uint32).astype(np.uint64)
        return (((u + 0x7FF + ((u >> 12) & 1)) >> 12) << 12).astype(np.uint32).view(np.float32)
    hi = top(x)
    return np.stack([hi, top(x - hi)])


def shape_tables():
    c = {}
    pos = np.concatenate([np.arange(n, dtype=np.float32) for n in LENS])
    half = HEAD_DIM // 2
    inv = (np.float32(1.0) / (np.float32(10000.0) ** (np.arange(half, dtype=np.float32) / np.float32(half)))).astype(np.float32)
    ang = (pos[None, :] * inv[:, None]).astype(np.float32)
    cos, sin = np.cos(ang), np.sin(ang)
    c["rope_cos"] = np.tile(cos, (4, 1)).astype(np.float32)
    c["rope_sin"] = np.concatenate([-sin, sin, -sin, sin]).astype(np.float32)
    rel = np.arange(3 * P)[None, :] - P - np.arange(P)[:, None]
    c["band"] = np.where(np.abs(rel) <= WINDOW, 0.0, NEG).astype(np.float32)
    c["ident"] = np.eye(P, dtype=np.float32)
    feats = []
    for s, n in enumerate(LENS):
        k = np.arange(n, dtype=np.float32)
        t = (k / np.float32(max(n - 1, 1))).astype(np.float32)
        step = (np.arange(FILT_BANDS, dtype=np.float32) / np.float32(FILT_BANDS - 1)).astype(np.float32)
        f = (np.float32(1e-4) * (np.float32(1) - step) + np.float32(FILT_BANDS - 1) * step).astype(np.float32)
        f[-1] = FILT_BANDS - 1
        ang = ((np.float32(2.0 * math.pi / n) * k)[:, None] * f[None]).astype(np.float32)
        feats.append(np.concatenate([t[:, None], np.cos(ang), -np.sin(ang)], -1).astype(np.float32).T)
        lo, hi = math.log(1e-2) / 1.5, math.log(1e-2) / 0.3
        step = (np.arange(HYW, dtype=np.float32) / np.float32(HYW - 1)).astype(np.float32)
        dl = np.abs((np.float32(lo) * (np.float32(1) - step) + np.float32(hi) * step).astype(np.float32))
        dl[-1] = abs(np.float32(hi))
        c[f"decay{s}"] = np.exp((-t[:, None] * dl[None]).astype(np.float32)).astype(np.float32)
        ahead, back = dft_tables(s)
        c[f"ahead{s}"] = halves12(ahead)
        c[f"back{s}"] = halves12(back)
    c["filt_z"] = np.ascontiguousarray(np.concatenate(feats, 1))
    return c


class Map:

    def __init__(self, nc):
        self.nc, self.at, self.n = nc, -(-nc.sbuf_base // 64) * 64, 0

    def __call__(self, name, shape, dt=F32):
        self.n += 1
        size = 4
        for x in shape[1:]:
            size *= x
        t = self.nc.alloc_sbuf_tensor_at(f"{name}_{self.n}", list(shape), dt, offset=self.at)
        self.at += -(-size // 64) * 64
        return t


class Ctx:
    pass


class Semaphores:

    def __init__(self, nc):
        self.nc, self.held = nc, []

    def __call__(self, names):
        new = [self.nc.alloc_semaphore(n) for n in names.split()]
        self.held += new
        return new

    def end_stage(self):
        self.nc.clear_and_free_semaphores(self.held)
        self.nc.all_engine_barrier()
        self.held = []


def linked(eng, sem):
    n = [0]

    def link(ins):
        n[0] += 1
        ins.then_inc(sem, 1)
        eng.wait_ge(sem, n[0])
    return link


def three_passes(nc, out, whi, wlo, xhi, xlo, first, last):
    nc.tensor.matmul(out, whi, xhi, start=first, stop=False)
    nc.tensor.matmul(out, whi, xlo, start=False, stop=False)
    return nc.tensor.matmul(out, wlo, xhi, start=False, stop=last)


def token_pieces(t0, n, x_prompt, x_sample, meta):
    out = []
    for s, x in enumerate((x_prompt, x_sample)):
        for a, b, src, off in ((STARTS[s], STARTS[s] + N_META, meta, STARTS[s]),
                               (STARTS[s] + N_META, STARTS[s] + LENS[s], x, STARTS[s] + N_META)):
            lo, hi = max(a, t0), min(b, t0 + n)
            if lo < hi:
                out.append((lo - t0, src[lo - off:hi - off, :]))
    return out


def stage_project(g):
    nc, io, S = g.nc, g.io, g.sem
    top = g.sb.at
    sb = g.sb
    nhi = sb("normed_hi", [P, KT, T], F32R)
    nlo = sb("normed_lo", [P, KT, T], F32R)
    gain = sb("mix_gain", [P, D])
    h = [sb("tokens", [P, D]) for _ in range(2)]
    n = [sb("normed", [P, D]) for _ in range(2)]
    ss = sb("square_sums", [P, 2 * len(TOK_TILES)])
    junk = sb("squares", [P, D])
    raw = [sb("w_raw", [P, KT, WCH]) for _ in range(3)]
    whi = [sb("w_hi", [P, KT, WCH], F32R) for _ in range(2)]
    wlo = [sb("w_lo", [P, KT, WCH], F32R) for _ in range(2)]
    rows = sb("conv_rows", [3 * HY_TILES + HY_TILES + 2 * CT, P])
    upad = [sb("u_padded", [P, T + 3]) for _ in range(2)]
    uc = [sb("u_conv", [P, T + 1]) for _ in range(2)]
    part = sb("conv_part", [P, T + 1])
    cosT = sb("rope_cos", [P, 2, HALF])
    sinT = sb("rope_sin", [P, 2, HALF])
    qr = [sb("q_plain", [P, 2, HALF]) for _ in range(2)]
    qs = [sb("q_swapped", [P, 2, HALF]) for _ in range(2)]
    sg = [sb("gate_sig", [P, 2, HALF]) for _ in range(2)]
    ident, qk, v, taps = g.ident, g.qk, g.v, g.taps
    tp = [g.ps[0], g.ps[1], g.ps[2], g.ps[3]]
    acc = [(g.ps[4], g.ps[5]), (g.ps[6], g.ps[7])]

    (tok_in, const_in, rows_in, w_in0, w_in1, w_in2, squared, meaned, rooted, normed, n_turned, hi_out, lo_out,
     w_hi, w_lo, prod, evac, conv_in, conv_out, uc_store0, uc_store1, sig_out, sig_store0, sig_store1, rope_in, rope_cos_done,
     rope_sin_done, roped, v_own, pads, taps_turned, taps_out, rope_tab) = S(
        "tok_in const_in rows_in w_in0 w_in1 w_in2 squared meaned rooted normed n_turned hi_out lo_out "
        "w_hi w_lo prod evac conv_in conv_out uc_store0 uc_store1 sig_out sig_store0 sig_store1 rope_in rope_cos_done "
        "rope_sin_done roped v_own pads taps_turned taps_out rope_tab")
    w_in = [w_in0, w_in1, w_in2]
    uc_store, sig_store = [uc_store0, uc_store1], [sig_store0, sig_store1]
    ntok = len(TOK_TILES)
    w = io["w_in"][0].rearrange("(t p) c -> p t c", p=P)
    chunks = [("hy", i) for i in range(6)] + [("q", 0), ("q", 1), ("kv", 0)] + [("gate", i) for i in range(8)]
    tiles = [(c, kind, i, sub) for c, (kind, i) in enumerate(chunks) for sub in range(2)]
    tok_sems = []
    tok_in2 = S("tok_in_odd")[0]
    tok_ins = [tok_in, tok_in2]
    pieces = [token_pieces(t0, m, io["x_prompt"][0], io["x_sample"][0], io["meta_tokens"]) for t0, m in TOK_TILES]
    tok_total = [[0, 0]]
    for i, ps_ in enumerate(pieces):
        now = list(tok_total[-1])
        now[i % 2] += 16 * len(ps_)
        tok_total.append(now)

    with nc.Block() as block:
        @block.sync
        def _(sp):
            def load_tokens(i):
                if i >= 2:
                    sp.wait_ge(normed, i - 1)
                for r0, src in pieces[i]:
                    sp.dma_start(h[i % 2][r0:r0 + src.shape[0], :], src).then_inc(tok_ins[i % 2], 16)

            def load_w(c):
                kind, i = chunks[c]
                dst = raw[c % 3]
                if c >= 3:
                    sp.wait_ge(w_hi, c - 2)
                    sp.wait_ge(w_lo, c - 2)
                if kind == "q":
                    for j in range(2):
                        for kv in range(2):
                            col = (2 * i + j + kv * GROUP) * HEAD_DIM
                            at = j * P + kv * HEAD_DIM
                            sp.dma_start(dst[:, :, at:at + HEAD_DIM], w[:, :, col:col + HEAD_DIM]).then_inc(w_in[c % 3], 16)
                    return
                col = {"hy": C_HY, "kv": C_K, "gate": C_GATE}[kind] + i * WCH
                for j in range(4):
                    sp.dma_start(dst[:, 2 * j:2 * j + 2, :], w[:, 2 * j:2 * j + 2, col:col + WCH]).then_inc(w_in[c % 3], 16)

            load_tokens(0)
            sp.dma_start(gain[:, :], io["norm_mix_g"][0].partition_broadcast(P)).then_inc(const_in, 16)
            sp.dma_start(ident[:, :], io["ident"]).then_inc(const_in, 16)
            load_tokens(1)
            load_w(0)
            r = io["hy_conv_w"][0].rearrange("k (m p) -> (k m) p", p=P)
            sp.dma_start(rows[0:36, :], r).then_inc(rows_in, 16)
            sp.dma_start(rows[36:48, :], io["hy_conv_b"][0].rearrange("(m p) -> m p", p=P)).then_inc(rows_in, 16)
            sp.dma_start(rows[48:56, :], io["hy_skip"][0].rearrange("o (m p) -> (o m) p", p=P)).then_inc(rows_in, 16)
            load_w(1)
            for i in range(2, ntok):
                load_tokens(i)
            load_w(2)
            sp.dma_start(cosT[:, :, :], io["rope_cos"].rearrange("p (a c) -> p a c", a=2)).then_inc(rope_tab, 16)
            sp.dma_start(sinT[:, :, :], io["rope_sin"].rearrange("p (a c) -> p a c", a=2)).then_inc(rope_tab, 16)
            hy = gt = 0
            for c, kind, i, sub in tiles:
                if sub == 0 and c + 3 < len(chunks):
                    load_w(c + 3)
                if kind == "hy":
                    sp.wait_ge(conv_out, 3 * (hy + 1))
                    sp.dma_start(g.hyS[hy * P:(hy + 1) * P, :], uc[hy % 2][:, :]).then_inc(uc_store[hy % 2], 16)
                    hy += 1
                if kind == "gate":
                    sp.wait_ge(sig_out, gt + 1)
                    sp.dma_start(g.sigS[gt * P:(gt + 1) * P, :].rearrange("p (a c) -> p a c", a=2), sg[gt % 2][:, :, :])\
                      .then_inc(sig_store[gt % 2], 16)
                    gt += 1
            for k in range(2):
                sp.wait_ge(uc_store[k], 16 * (HY_TILES // 2))
                sp.wait_ge(sig_store[k], 16 * 8)

        def turn_out(act, i):
            t0, m = TOK_TILES[i]
            for b in range(2):
                act.wait_ge(n_turned, 2 * i + b + 1)
                act.activation(nhi[:, 4 * b:4 * b + 4, t0:t0 + m],
                               tp[(2 * i + b) % 4][:, :].rearrange("p (a c) -> p a c", a=4)[:, :, 0:m], ACT.Copy)\
                   .then_inc(hi_out, 1)

        @block.scalar
        def _(act):
            def take_hi(c):
                act.wait_ge(w_in[c % 3], 64 * (c // 3 + 1))
                if c >= 2:
                    act.wait_ge(prod, 2 * (c - 1))
                act.activation(whi[c % 2][:, :, :], raw[c % 3][:, :, :], ACT.Copy).then_inc(w_hi, 1)

            for k in range(2):
                act.wait_ge(pads, 2)
            for i, (t0, m) in enumerate(TOK_TILES):
                act.wait_ge(tok_ins[i % 2], tok_total[i + 1][i % 2])
                act.activation(junk[0:m, :], h[i % 2][0:m, :], ACT.Square, accum_out=ss[0:m, i:i + 1]).then_inc(squared, 1)
                act.wait_ge(meaned, i + 1)
                act.activation(ss[0:m, ntok + i:ntok + i + 1], ss[0:m, i:i + 1], ACT.Sqrt).then_inc(rooted, 1)
                if i == 1:
                    take_hi(0)
                if i == 3:
                    take_hi(1)
                if i >= 1:
                    turn_out(act, i - 1)
            turn_out(act, ntok - 1)
            hy = gt = rp = 0
            for a, (c, kind, i, sub) in enumerate(tiles):
                if sub == 0 and c + 1 < len(chunks) and c >= 1:
                    take_hi(c + 1)
                act.wait_ge(prod, a + 1)
                b0, b1 = acc[a % 2]
                if kind == "hy":
                    if hy >= 2:
                        act.wait_ge(conv_out, 3 * (hy - 1))
                    u = upad[hy % 2]
                    act.activation(u[:, 1:1 + HALF], b0[:, 0:HALF], ACT.Copy)
                    act.activation(u[:, 1 + HALF:1 + LENS[0]], b1[:, 0:LENS[0] - HALF], ACT.Copy)
                    act.activation(u[:, 2 + LENS[0]:2 + T], b1[:, LENS[0] - HALF:HALF], ACT.Copy).then_inc(evac, 1)
                    hy += 1
                elif kind == "gate":
                    if gt >= 2:
                        act.wait_ge(sig_store[gt % 2], 16 * (gt // 2))
                    act.activation(sg[gt % 2][:, 0, :], b0[:, 0:HALF], ACT.Sigmoid)
                    act.activation(sg[gt % 2][:, 1, :], b1[:, 0:HALF], ACT.Sigmoid).then_inc(sig_out, 1)
                    gt += 1
                elif kind == "kv" and sub == 1:
                    for k, b in enumerate((b0, b1)):
                        for j in range(4):
                            m = VB[4 * k + j][1]
                            last = act.activation(v[0:m, 4 * k + j, :], b[0:m, j * P:(j + 1) * P], ACT.Copy)
                    last.then_inc(evac, 1)
                else:
                    if rp >= 2:
                        act.wait_ge(roped, rp - 1)
                    for k, b in enumerate((b0, b1)):
                        act.activation(qr[rp % 2][:, k, :], b[:, 0:HALF], ACT.Copy)
                        for x in range(4):
                            last = act.activation(qs[rp % 2][32 * x:32 * x + 32, k, :],
                                                  b[32 * (x ^ 1):32 * (x ^ 1) + 32, 0:HALF], ACT.Copy)
                    last.then_inc(evac, 1)
                    rp += 1

        @block.vector
        def _(dve):
            link = linked(dve, v_own)
            for k in range(2):
                nc.vector.memset(upad[k][:, :], 0.0).then_inc(pads, 1)
            dve.wait_ge(const_in, 32)

            def take_lo(i):
                t0, m = TOK_TILES[i]
                for b in range(2):
                    dve.wait_ge(hi_out, 2 * i + b + 1)
                    nc.vector.tensor_tensor(nlo[:, 4 * b:4 * b + 4, t0:t0 + m],
                                            tp[(2 * i + b) % 4][:, :].rearrange("p (a c) -> p a c", a=4)[:, :, 0:m],
                                            nhi[:, 4 * b:4 * b + 4, t0:t0 + m].bitcast(F32), ALU.subtract).then_inc(lo_out, 1)

            for i, (t0, m) in enumerate(TOK_TILES):
                dve.wait_ge(squared, i + 1)
                nc.vector.tensor_scalar(ss[0:m, i:i + 1], ss[0:m, i:i + 1], 1.0 / D, EPS, ALU.mult, ALU.add).then_inc(meaned, 1)
                dve.wait_ge(rooted, i + 1)
                link(nc.vector.reciprocal(ss[0:m, i:i + 1], ss[0:m, ntok + i:ntok + i + 1]))
                if i >= 2:
                    dve.wait_ge(n_turned, 2 * (i - 1))
                nc.vector.scalar_tensor_tensor(n[i % 2][0:m, :], h[i % 2][0:m, :], ss[0:m, i:i + 1], gain[0:m, :],
                                               ALU.mult, ALU.mult).then_inc(normed, 1)
                if i >= 1:
                    take_lo(i - 1)
            take_lo(ntok - 1)
            dve.wait_ge(taps_turned, 1)
            nc.vector.tensor_copy(taps[:, :], tp[2 * ntok % 4][:, 0:taps.shape[1]]).then_inc(taps_out, 1)
            dve.wait_ge(taps_out, 1)
            dve.wait_ge(rope_tab, 32)
            hy = rp = 0
            for a, (c, kind, i, sub) in enumerate(tiles):
                if kind == "hy":
                    dve.wait_ge(evac, hy + 1)
                    u, o, m = upad[hy % 2], uc[hy % 2], hy
                    tap = [taps[:, k * HY_TILES + m:k * HY_TILES + m + 1] for k in range(4)]
                    if hy >= 2:
                        dve.wait_ge(uc_store[hy % 2], 16 * (hy // 2))
                    nc.vector.tensor_scalar(o[:, :], u[:, 0:T + 1], tap[0], tap[3], ALU.mult, ALU.add).then_inc(conv_out, 1)
                    dve.wait_ge(conv_out, 3 * hy + 1)
                    nc.vector.scalar_tensor_tensor(part[:, :], u[:, 1:T + 2], tap[1], o[:, :], ALU.mult, ALU.add).then_inc(conv_out, 1)
                    dve.wait_ge(conv_out, 3 * hy + 2)
                    nc.vector.scalar_tensor_tensor(o[:, :], u[:, 2:T + 3], tap[2], part[:, :], ALU.mult, ALU.add).then_inc(conv_out, 1)
                    hy += 1
                elif kind == "q" or (kind == "kv" and sub == 0):
                    dve.wait_ge(evac, HY_TILES + rp + 1)
                    link(nc.vector.tensor_tensor(qr[rp % 2][:, :, :], qr[rp % 2][:, :, :], cosT[:, :, :], ALU.mult))
                    dve.wait_ge(rope_sin_done, rp + 1)
                    nc.vector.tensor_tensor(qk[:, rp, :].rearrange("p (a c) -> p a c", a=2), qr[rp % 2][:, :, :],
                                            qs[rp % 2][:, :, :], ALU.add).then_inc(roped, 1)
                    rp += 1

        @block.gpsimd
        def _(pool):
            rp = 0
            done = 0

            def lo(c):
                pool.wait_ge(w_hi, c + 1)
                nc.gpsimd.tensor_tensor(wlo[c % 2][:, :, :], raw[c % 3][:, :, :], whi[c % 2][:, :, :].bitcast(F32),
                                        ALU.subtract).then_inc(w_lo, 1)
            lo(0)
            lo(1)
            pool.wait_ge(rope_tab, 32)
            for a, (c, kind, i, sub) in enumerate(tiles):
                if sub == 0 and 1 <= c and c + 1 < len(chunks):
                    lo(c + 1)
                if kind == "q" or (kind == "kv" and sub == 0):
                    pool.wait_ge(evac, HY_TILES + rp + 1)
                    nc.gpsimd.tensor_tensor(qs[rp % 2][:, :, :], qs[rp % 2][:, :, :], sinT[:, :, :], ALU.mult)\
                      .then_inc(rope_sin_done, 1)
                    rp += 1

        @block.tensor
        def _(pe):
            pe.wait_ge(const_in, 32)
            for i, (t0, m) in enumerate(TOK_TILES):
                pe.wait_ge(normed, i + 1)
                for b in range(2):
                    u = 2 * i + b
                    if u >= 4:
                        pe.wait_ge(lo_out, u - 3)
                    for k in range(4):
                        kt = 4 * b + k
                        last = nc.tensor.transpose(tp[u % 4][:, k * P:k * P + m], n[i % 2][0:m, kt * P:(kt + 1) * P],
                                                   ident[0:m, 0:m])
                    last.then_inc(n_turned, 1)
            pe.wait_ge(rows_in, 48)
            pe.wait_ge(lo_out, 2 * ntok - 3)
            nc.tensor.transpose(tp[2 * ntok % 4][:, 0:rows.shape[0]], rows[:, :], ident[0:rows.shape[0], 0:rows.shape[0]])\
              .then_inc(taps_turned, 1)
            pe.wait_ge(lo_out, 2 * ntok)
            ev = sg_n = 0
            freed = []
            for a, (c, kind, i, sub) in enumerate(tiles):
                if kind == "gate":
                    sg_n += 1
                    freed.append((sig_out, sg_n))
                else:
                    ev += 1
                    freed.append((evac, ev))
            for a, (c, kind, i, sub) in enumerate(tiles):
                if sub == 0:
                    pe.wait_ge(w_hi, c + 1)
                    pe.wait_ge(w_lo, c + 1)
                if a >= 2:
                    pe.wait_ge(*freed[a - 2])
                hi, lo_ = whi[c % 2], wlo[c % 2]
                if kind == "kv" and sub == 1:
                    for j, (t0, m) in enumerate(VB):
                        for kt in range(KT):
                            last = three_passes(nc, acc[a % 2][j // 4][0:m, (j % 4) * P:(j % 4 + 1) * P],
                                                nhi[:, kt, t0:t0 + m], nlo[:, kt, t0:t0 + m],
                                                hi[:, kt, P:2 * P], lo_[:, kt, P:2 * P], kt == 0, kt == KT - 1)
                else:
                    for k in range(2):
                        for kt in range(KT):
                            last = three_passes(nc, acc[a % 2][k][:, 0:HALF],
                                                hi[:, kt, sub * P:(sub + 1) * P], lo_[:, kt, sub * P:(sub + 1) * P],
                                                nhi[:, kt, k * HALF:(k + 1) * HALF], nlo[:, kt, k * HALF:(k + 1) * HALF],
                                                kt == 0, kt == KT - 1)
                last.then_inc(prod, 1)
    g.sb.at = top


VB = [(s + q, min(P, n - q)) for s, n in zip(STARTS, LENS) for q in range(0, n, P)]


def stage_filter_mlp(g):
    nc, io, S = g.nc, g.io, g.sem
    top = g.sb.at
    sb = g.sb
    H = FILT_HIDDEN
    z = sb("filt_z", [FILT_EMB, T])
    w1 = sb("filt_w1", [FILT_EMB, H])
    w2 = sb("filt_w2", [H, H])
    w3 = sb("filt_w3", [H, H])
    col = sb("filt_cols", [H, 4])
    x = sb("filt_x", [H, T])
    k = sb("filt_k", [H, T])
    y = sb("filt_y", [H, T])
    a = sb("filt_a", [H, T])
    ins, mm, own, sined = S("filt_in filt_mm filt_own filt_sine")
    c1 = float(np.float32(6.28125))
    c2 = float(np.float32(np.float64(TWO_PI - c1).astype(np.float32).view(np.uint32).__and__(0xFFFFF000).view(np.float32)))
    c3 = float(np.float32(TWO_PI - c1 - c2))
    pi = float(np.nextafter(np.float32(math.pi), np.float32(0)))
    with nc.Block() as block:
        @block.sync
        def _(sp):
            sp.dma_start(z[:, :], io["filt_z"]).then_inc(ins, 16)
            for t, name in ((w1, "w1"), (w2, "w2"), (w3, "w3")):
                sp.dma_start(t[:, :], io[f"hy_filt_{name}"][0]).then_inc(ins, 16)
            for j, name in enumerate(("b1", "b2", "b3", "freq")):
                sp.dma_start(col[:, j:j + 1], io[f"hy_filt_{name}"][0].rearrange("(p a) -> p a", a=1)).then_inc(ins, 16)
            sp.wait_ge(ins, 128)

        @block.tensor
        def _(pe):
            pe.wait_ge(ins, 128)
            for layer, (w, src) in enumerate(((w1, z), (w2, a), (w3, a))):
                if layer:
                    pe.wait_ge(sined, layer)
                for b in range(2):
                    last = nc.tensor.matmul(g.ps[b][0:H, 0:HALF], w[:, :], src[:, b * HALF:(b + 1) * HALF], start=True, stop=True)
                last.then_inc(mm, 1)

        @block.vector
        def _(dve):
            dve.wait_ge(ins, 128)
            link = linked(dve, own)
            for layer in range(3):
                dve.wait_ge(mm, layer + 1)
                for b in range(2):
                    link(nc.vector.tensor_scalar(x[:, b * HALF:(b + 1) * HALF], g.ps[b][0:H, 0:HALF], col[:, layer:layer + 1],
                                                 col[:, 3:4], ALU.add, ALU.mult))
                link(nc.vector.tensor_scalar(k[:, :], x[:, :], 1.0 / TWO_PI, MAGIC, ALU.mult, ALU.add))
                link(nc.vector.tensor_scalar(k[:, :], k[:, :], MAGIC, None, ALU.subtract))
                link(nc.vector.scalar_tensor_tensor(y[:, :], k[:, :], -c1, x[:, :], ALU.mult, ALU.add))
                link(nc.vector.scalar_tensor_tensor(x[:, :], k[:, :], -c2, y[:, :], ALU.mult, ALU.add))
                link(nc.vector.scalar_tensor_tensor(y[:, :], k[:, :], -c3, x[:, :], ALU.mult, ALU.add))
                link(nc.vector.tensor_scalar(x[:, :], y[:, :], pi, -pi, ALU.min, ALU.max))

        @block.scalar
        def _(act):
            for layer in range(3):
                act.wait_ge(own, 8 * (layer + 1))
                dst = a if layer < 2 else g.feat
                act.activation(dst[:, :], x[:, :], ACT.Sin).then_inc(sined, 1)
            act.wait_ge(sined, 3)
    g.sb.at = top


def stage_attend(g):
    nc, io, S = g.nc, g.io, g.sem
    top = g.sb.at
    sb = g.sb
    band = sb("band", [P, 3 * P])
    sinks = sb("sinks", [P, N_HEADS])
    s = [sb("scores", [P, N_HEADS, 3 * P]) for _ in range(2)]
    small = [sb("softmax_cols", [P, 6, N_HEADS]) for _ in range(2)]
    pt = [sb("probs_turned", [P, GROUP, P]) for _ in range(4)]
    o = [sb("attn_out", [P, GROUP, P]) for _ in range(2)]
    qk, v, ident = g.qk, g.v, g.ident
    cin, scored, masked, prep, exped, normed, turned, copied, pv, o_out, store0, store1, own = S(
        "at_in at_scored at_masked at_prep at_exped at_normed at_turned at_copied at_pv at_out at_store0 at_store1 at_own")
    store = [store0, store1]
    sc = [g.ps[0], g.ps[1]]
    tr = [g.ps[2], g.ps[3], g.ps[6], g.ps[7]]
    ob = [g.ps[4], g.ps[5]]
    HEADS = [(j, kv) for j in range(GROUP) for kv in range(N_KV)]
    nb = len(BLOCKS)

    def key_tiles(b):
        _, _, k0, nk, _ = BLOCKS[b]
        return [(c, min(P, nk - c)) for c in range(0, nk, P)]

    turns = [(b, kv, ci) for b in range(nb) for kv in range(N_KV) for ci in range(len(key_tiles(b)))]
    before = {}
    for n_, (b, kv, ci) in enumerate(turns):
        before[(b, kv, ci)] = n_

    with nc.Block() as block:
        @block.sync
        def _(sp):
            sp.dma_start(band[:, :], io["band"]).then_inc(cin, 16)
            sp.dma_start(sinks[:, :], io["attn_sink"][0].partition_broadcast(P)).then_inc(cin, 16)
            for b, (q0, lq, k0, nk, m0) in enumerate(BLOCKS):
                sp.wait_ge(o_out, b + 1)
                sp.dma_start(g.upS[0:ATTN, :].rearrange("(j p) t -> p j t", p=P)[:, :, q0:q0 + lq],
                             o[b % 2][:, :, 0:lq]).then_inc(store[b % 2], 16)
            sp.wait_ge(store[0], 16 * ((nb + 1) // 2))
            sp.wait_ge(store[1], 16 * (nb // 2))

        @block.tensor
        def _(pe):
            def scores(b):
                q0, lq, k0, nk, m0 = BLOCKS[b]
                for i, (j, kv) in enumerate(HEADS):
                    u = b * N_HEADS + i
                    if u >= 2:
                        pe.wait_ge(masked, u - 1)
                    r = slice(kv * HEAD_DIM, (kv + 1) * HEAD_DIM)
                    nc.tensor.matmul(sc[kv][0:lq, 0:nk], qk[r, j, q0:q0 + lq], qk[r, GROUP, k0:k0 + nk],
                                     start=True, stop=True).then_inc(scored, 1)

            def weigh(b):
                q0, lq, k0, nk, m0 = BLOCKS[b]
                pe.wait_ge(normed, b + 1)
                cts = key_tiles(b)
                for kv in range(N_KV):
                    for ci, (c, m) in enumerate(cts):
                        u = before[(b, kv, ci)]
                        if u >= 4:
                            pe.wait_ge(copied, u - 3)
                        for j in range(GROUP):
                            last = nc.tensor.transpose(tr[u % 4][0:m, j * P:j * P + lq],
                                                       s[b % 2][0:lq, kv * GROUP + j, c:c + m], ident[0:lq, 0:lq])
                        last.then_inc(turned, 1)
                    if kv == 0 and b >= 2:
                        pe.wait_ge(o_out, b - 1)
                    for ci, (c, m) in enumerate(cts):
                        u = before[(b, kv, ci)]
                        pe.wait_ge(copied, u + 1)
                        last = nc.tensor.matmul(ob[b % 2][kv * HEAD_DIM:(kv + 1) * HEAD_DIM, :]
                                                .rearrange("p (j q) -> p j q", j=GROUP)[:, :, 0:lq],
                                                v[0:m, VBI[k0 + c], kv * HEAD_DIM:(kv + 1) * HEAD_DIM],
                                                pt[u % 4][0:m, :, 0:lq], start=(ci == 0), stop=(ci == len(cts) - 1))
                last.then_inc(pv, 1)

            scores(0)
            for b in range(nb):
                if b + 1 < nb:
                    scores(b + 1)
                weigh(b)

        @block.vector
        def _(dve):
            dve.wait_ge(cin, 32)
            link = linked(dve, own)

            def mask(b):
                q0, lq, k0, nk, m0 = BLOCKS[b]
                if b >= 2:
                    dve.wait_ge(pv, b - 1)
                for i, (j, kv) in enumerate(HEADS):
                    dve.wait_ge(scored, b * N_HEADS + i + 1)
                    hd = kv * GROUP + j
                    nc.vector.tensor_tensor_reduce(s[b % 2][0:lq, hd, 0:nk], sc[kv][0:lq, 0:nk], band[0:lq, m0:m0 + nk],
                                                   1.0, NEG, ALU.add, ALU.max, small[b % 2][0:lq, 0, hd:hd + 1]).then_inc(masked, 1)
                dve.wait_ge(masked, N_HEADS * (b + 1))
                k = small[b % 2]
                link(nc.vector.scalar_tensor_tensor(k[0:lq, 1, :], k[0:lq, 0, :], HEAD_DIM ** -0.5, sinks[0:lq, :], ALU.mult, ALU.max))
                link(nc.vector.tensor_scalar(k[0:lq, 2, :], k[0:lq, 1, :], -1.0, None, ALU.mult))
                nc.vector.tensor_tensor(k[0:lq, 3, :], sinks[0:lq, :], k[0:lq, 1, :], ALU.subtract).then_inc(prep, 1)

            def norm(b):
                q0, lq, k0, nk, m0 = BLOCKS[b]
                k = small[b % 2]
                dve.wait_ge(exped, b + 1)
                link(nc.vector.tensor_tensor(k[0:lq, 1, :], k[0:lq, 4, :], k[0:lq, 3, :], ALU.add))
                link(nc.vector.reciprocal(k[0:lq, 5, :], k[0:lq, 1, :]))
                for hd in range(N_HEADS):
                    last = nc.vector.tensor_scalar(s[b % 2][0:lq, hd, 0:nk], s[b % 2][0:lq, hd, 0:nk], k[0:lq, 5, hd:hd + 1],
                                                   None, ALU.mult)
                last.then_inc(normed, 1)

            def out(b):
                lq = BLOCKS[b][1]
                dve.wait_ge(pv, b + 1)
                if b >= 2:
                    dve.wait_ge(store[b % 2], 16 * (b // 2))
                nc.vector.tensor_copy(o[b % 2][:, :, 0:lq], ob[b % 2][:, :].rearrange("p (j q) -> p j q", j=GROUP)[:, :, 0:lq])\
                  .then_inc(o_out, 1)

            mask(0)
            for b in range(nb):
                norm(b)
                if b + 1 < nb:
                    mask(b + 1)
                out(b)

        @block.scalar
        def _(act):
            for b, (q0, lq, k0, nk, m0) in enumerate(BLOCKS):
                act.wait_ge(prep, b + 1)
                k = small[b % 2]
                for hd in range(N_HEADS):
                    act.activation(s[b % 2][0:lq, hd, 0:nk], s[b % 2][0:lq, hd, 0:nk], ACT.Exp, bias=k[0:lq, 2, hd:hd + 1],
                                   scale=HEAD_DIM ** -0.5, accum_out=k[0:lq, 4, hd:hd + 1])
                act.activation(k[0:lq, 3, :], k[0:lq, 3, :], ACT.Exp).then_inc(exped, 1)
                for kv in range(N_KV):
                    for ci, (c, m) in enumerate(key_tiles(b)):
                        u = before[(b, kv, ci)]
                        act.wait_ge(turned, u + 1)
                        act.activation(pt[u % 4][0:m, :, 0:lq], tr[u % 4][0:m, :].rearrange("p (j q) -> p j q", j=GROUP)[:, :, 0:lq],
                                       ACT.Copy).then_inc(copied, 1)
    g.sb.at = top


VBI = {t0: i for i, (t0, _) in enumerate(VB)}


CUTS = (((0, 264), (264, 264)), ((0, 272),))
KF_FILLS = (((0, 0, 2), (1, 0, 2), (2, 2, 1)), ((0, 0, 2), (1, 0, 2)))


def hyena_steps():
    units = [(s, j) for s in (1, 0) for j in range(CT)]
    n = len(units)
    steps = [("hgen", 0), ("kf", 0, 0), ("kf", 0, 1), ("hgen", 1), ("zt", 0, 0)]
    for u in range(n):
        steps.append(("fwd", u, 0))
        if u + 1 < n:
            steps.append(("kf", u + 1, 0))
        steps += [("yt", u, 0), ("inv", u, 0), ("zt", u, 1)]
        if u + 1 < n:
            steps.append(("kf", u + 1, 1))
        steps.append(("fwd", u, 1))
        if u + 2 < n:
            steps.append(("hgen", u + 2))
        steps.append(("yt", u, 1))
        if u + 1 < n:
            steps.append(("zt", u + 1, 0))
        steps.append(("inv", u, 1))
    return units, steps


def stage_hyena(g):
    nc, io, S = g.nc, g.io, g.sem
    top = g.sb.at
    sb = g.sb
    ahead = [[sb(f"ahead{s}_{x}", [P, NT[s], W[s]], F32R) for x in ("hi", "lo")] for s in range(2)]
    back = [[sb(f"back{s}_{x}", [P, NK[s], LENS[s]], F32R) for x in ("hi", "lo")] for s in range(2)]
    decay = [sb("decay", [P, NT[0], P]) for _ in range(2)]
    wout = [sb("filt_wout", [FILT_HIDDEN, 4, P]) for _ in range(2)]
    taps = [sb("filter_taps", [P, 4, P]) for _ in range(2)]
    pair = [sb("taps_sum_diff", [P, 2, 2, P]) for _ in range(2)]
    hs = [sb(f"taps_{x}", [P, NT[0], 2, 2, P], F32R) for x in ("hi", "lo")]
    kf = [sb("spectrum", [P, 2, W[0]]) for _ in range(2)]
    src = [sb("v_x1_x2", [P, 3, LENS[0]]) for _ in range(2)]
    z = [sb("z", [P, LENS[0]]) for _ in range(2)]
    zt = [sb(f"z_turned_{x}", [P, NT[0], P], F32R) for x in ("hi", "lo")]
    prodA = [sb("zk_real", [P, 2, FG[0]]) for _ in range(2)]
    prodB = [sb("zk_imag", [P, 2, FG[0]]) for _ in range(2)]
    y = sb("y_spectrum", [P, W[0]])
    yt = [sb(f"y_turned_{x}", [P, NK[0], P], F32R) for x in ("hi", "lo")]
    ident = g.ident
    (cd, hg, h_decayed, h_sum, h_hi, h_lo, kmm, k_out, v_in0, v_in1, dec_in0, dec_in1, ztm, zt_hi, zt_lo, fmm, f_mul, y_out,
     ytm, yt_hi, yt_lo, imm_, gated, st0, st1, done_fwd, done_inv) = S(
        "hy_const0 hy_taps_mm hy_decayed hy_sum_diff hy_taps_hi hy_taps_lo hy_spec_mm hy_spec_out hy_v_in0 hy_v_in1 hy_dec_in0 "
        "hy_dec_in1 hy_zt_mm hy_zt_hi hy_zt_lo hy_fwd_mm hy_fwd_mul hy_y_out hy_yt_mm hy_yt_hi hy_yt_lo hy_inv_mm hy_gated "
        "hy_store0 hy_store1 hy_fwd_done hy_inv_done")
    cb, ca0, cb0 = S("hy_const_back1 hy_const_ahead0 hy_const_back0")
    const_a = [ca0, cd]
    const_b = [cb0, cb]
    v_in, dec_in, store = [v_in0, v_in1], [dec_in0, dec_in1], [st0, st1]
    units, steps = hyena_steps()
    hb, kb, tb, ib = [g.ps[0], g.ps[1]], [g.ps[2], g.ps[3]], [g.ps[4], g.ps[5]], [g.ps[6], g.ps[7]]
    pos, nh, nk, nt_, nf, nyt, nkf, nzt = {}, 0, 0, 0, 0, 0, 0, 0
    for st in steps:
        s = units[st[1]][0]
        pos[st] = dict(h=nh, k=nk, t=nt_, f=nf, yt=nyt, kf=nkf, zt=nzt)
        if st[0] == "hgen":
            nh += NT[s]
        elif st[0] == "kf":
            nk += len(KF_FILLS[s])
            nkf += len(KF_FILLS[s])
        elif st[0] == "fwd":
            nk += GROUPS[s]
            nf += GROUPS[s]
        elif st[0] == "zt":
            nt_ += -(-NT[s] // 4)
            nzt += -(-NT[s] // 4)
        elif st[0] == "yt":
            nt_ += -(-NK[s] // 4)
            nyt += -(-NK[s] // 4)
    kuse, tuse = [], []
    for st in steps:
        s = units[st[1]][0]
        if st[0] in ("kf", "fwd"):
            for q in range(len(KF_FILLS[s]) if st[0] == "kf" else GROUPS[s]):
                kuse.append((k_out, 1 + sum(1 for a, _ in kuse if a is k_out)) if st[0] == "kf"
                            else (f_mul, 1 + sum(1 for a, _ in kuse if a is f_mul)))
        if st[0] in ("zt", "yt"):
            for q in range(-(-(NT if st[0] == "zt" else NK)[s] // 4)):
                sm = zt_lo if st[0] == "zt" else yt_lo
                tuse.append((sm, 1 + sum(1 for a, _ in tuse if a is sm)))

    def tsize(s, t):
        return min(P, LENS[s] - t * P)

    def ksize(s, k):
        return min(P, W[s] - k * P)

    def cuts_before(st):
        return sum(len(CUTS[units[x[1]][0]]) for x in steps[:steps.index(st)] if x[0] == "inv")

    def order(st):
        return sum(1 for x in steps[:steps.index(st)] if x[0] == st[0])

    with nc.Block() as block:
        @block.gpsimd
        def _(pool):
            for s in (1, 0):
                if s == 0:
                    pool.wait_ge(hg, 1)
                for tab, dst, sem, full, rows in ((f"ahead{s}", ahead[s], const_a[s], NT[s] - 1, LENS[s]),
                                                  (f"back{s}", back[s], const_b[s], NK[s] - 1, W[s])):
                    for x in range(2):
                        if tab[0] == "a":
                            nc.gpsimd.dma_start(dst[x][:, 0:full, :], io[tab][x, 0:full * P, :].rearrange("(t p) w -> p t w", p=P)).then_inc(sem, 16)
                        else:
                            nc.gpsimd.dma_start(dst[x][:, 0:full, :], io[tab][x, 0:full * P, :].rearrange("(t p) w -> p t w", p=P)).then_inc(sem, 16)
                        nc.gpsimd.dma_start(dst[x][0:rows - full * P, full, :], io[tab][x, full * P:rows, :]).then_inc(sem, 16)
            for st in steps:
                s, j = units[st[1]]
                if st[0] == "hgen":
                    for t in range(NT[s]):
                        u, m = pos[st]["h"] + t, tsize(s, t)
                        pool.wait_ge(h_decayed, u + 1)
                        if u >= 2:
                            pool.wait_ge(h_lo, u - 1)
                        pool_a = taps[u % 2]
                        nc.gpsimd.tensor_tensor(pair[u % 2][0:m, 0, :, :], pool_a[0:m, 0:2, :], pool_a[0:m, 2:4, :], ALU.add)
                        nc.gpsimd.tensor_tensor(pair[u % 2][0:m, 1, :, :], pool_a[0:m, 0:2, :], pool_a[0:m, 2:4, :], ALU.subtract)\
                          .then_inc(h_sum, 1)
                elif st[0] == "fwd":
                    f = FG[s]
                    for q in range(GROUPS[s]):
                        u = pos[st]["f"] + q
                        pool.wait_ge(f_mul, u + 1)
                        if q == 0:
                            k = order(st)
                            if k:
                                pool.wait_ge(ytm, sum(-(-NK[units[x[1]][0]] // 4) for x in steps if x[0] == "yt" and order(x) < k))
                        A, B = prodA[u % 2], prodB[u % 2]
                        yy = y[:, 2 * f * q:2 * f * (q + 1)].rearrange("p (c f) -> p c f", c=2)
                        nc.gpsimd.tensor_tensor(yy[:, 0, :], A[:, 0, 0:f], B[:, 1, 0:f], ALU.subtract)
                        nc.gpsimd.tensor_tensor(yy[:, 1, :], B[:, 0, 0:f], A[:, 1, 0:f], ALU.add).then_inc(y_out, 1)

        @block.sync
        def _(sp):
            def unit_in(u):
                s, j = units[u]
                n = LENS[s]
                full = NT[s] - 1
                if u >= 2:
                    sp.wait_ge(hg, pos[("hgen", u - 2)]["h"] + NT[units[u - 2][0]])
                    sp.wait_ge(h_decayed, pos[("hgen", u - 2)]["h"] + NT[units[u - 2][0]])
                sp.dma_start(wout[u % 2][:, :, :], io["hy_filt_wout"][0].rearrange("k (q c) -> k q c", q=4)[:, :, j * P:(j + 1) * P])\
                  .then_inc(dec_in[u % 2], 16)
                sp.dma_start(decay[u % 2][:, 0:full, :], io[f"decay{s}"][0:full * P, j * P:(j + 1) * P].rearrange("(t p) c -> p t c", p=P))\
                  .then_inc(dec_in[u % 2], 16)
                sp.dma_start(decay[u % 2][0:n - full * P, full, :], io[f"decay{s}"][full * P:n, j * P:(j + 1) * P]).then_inc(dec_in[u % 2], 16)

            def gates_in(u):
                s, j = units[u]
                n = LENS[s]
                if u >= 2:
                    sp.wait_ge(gated, cuts_before(("inv", u - 2, 1)) + len(CUTS[units[u - 2][0]]))
                at = (0, LENS[0] + 1)[s]
                sp.dma_start(src[u % 2][:, :, 0:n], g.hyS.rearrange("(q j p) t -> j p q t", q=3, p=P)[j, :, :, at:at + n]).then_inc(v_in[u % 2], 16)

            unit_in(0)
            unit_in(1)
            gates_in(0)
            for u, (s, j) in enumerate(units):
                if u + 1 < len(units):
                    gates_in(u + 1)
                if u + 2 < len(units):
                    unit_in(u + 2)
                sp.wait_ge(gated, cuts_before(("inv", u, 1)) + len(CUTS[s]))
                sp.dma_start(g.upS[ATTN + j * P:ATTN + (j + 1) * P, STARTS[s]:STARTS[s] + LENS[s]], z[1][:, 0:LENS[s]] if u % 2 == 0 else g.zx[:, 0:LENS[s]])\
                  .then_inc(store[u % 2], 16)
            sp.wait_ge(store[0], 16 * CT)
            sp.wait_ge(store[1], 16 * CT)

        @block.tensor
        def _(pe):
            for st in steps:
                s, j = units[st[1]]
                p_ = pos[st]
                n, f = LENS[s], FG[s]
                if st[0] == "hgen":
                    pe.wait_ge(dec_in[st[1] % 2], 48 * (st[1] // 2 + 1))
                    for t in range(NT[s]):
                        u = p_["h"] + t
                        if u >= 2:
                            pe.wait_ge(h_decayed, u - 1)
                        t0 = STARTS[s] + t * P
                        nc.tensor.matmul(hb[u % 2][0:tsize(s, t), :], g.feat[:, t0:t0 + tsize(s, t)],
                                         wout[st[1] % 2][:, :, :].rearrange("k q c -> k (q c)"), start=True, stop=True).then_inc(hg, 1)
                elif st[0] == "kf":
                    o = st[2]
                    pe.wait_ge(h_lo, pos[("hgen", st[1])]["h"] + NT[s])
                    pe.wait_ge(const_a[s], 64)
                    for q, (part, g0, ng) in enumerate(KF_FILLS[s]):
                        u = p_["k"] + q
                        if u >= 2:
                            pe.wait_ge(*kuse[u - 2])
                        for c in ((0, 1) if part == 2 else (part,)):
                            at = c * f if part == 2 else 0
                            for t in range(NT[s]):
                                m = tsize(s, t)
                                tab = [ahead[s][x][0:m, t, :].rearrange("p (g c f) -> p g c f", c=2, f=f)[:, g0:g0 + ng, c, :] for x in range(2)]
                                last = three_passes(nc, kb[u % 2][:, at:at + ng * f], hs[0][0:m, t, c, o, :], hs[1][0:m, t, c, o, :],
                                                    tab[0], tab[1], t == 0, t == NT[s] - 1)
                        last.then_inc(kmm, 1)
                elif st[0] == "zt":
                    o = st[2]
                    if o == 0:
                        pe.wait_ge(v_in[st[1] % 2], 16 * (st[1] // 2 + 1))
                        zz = src[st[1] % 2][:, 0, :]
                    else:
                        zz = z[0]
                    for b in range(-(-NT[s] // 4)):
                        u = p_["t"] + b
                        if u >= 2:
                            pe.wait_ge(*tuse[u - 2])
                        for t in range(4 * b, min(4 * b + 4, NT[s])):
                            m = tsize(s, t)
                            if o == 1:
                                pe.wait_ge(gated, cuts_before(("inv", st[1], 0)) + sum(c0 < t * P + m for c0, cn in CUTS[s]))
                            last = nc.tensor.transpose(tb[u % 2][0:m, (t % 4) * P:(t % 4 + 1) * P], zz[:, t * P:t * P + m], ident[:, :])
                        last.then_inc(ztm, 1)
                elif st[0] == "fwd":
                    pe.wait_ge(zt_lo, pos[("zt", st[1], st[2])]["zt"] + -(-NT[s] // 4))
                    for q in range(GROUPS[s]):
                        u = p_["k"] + q
                        if u >= 2:
                            pe.wait_ge(*kuse[u - 2])
                        for t in range(NT[s]):
                            m = tsize(s, t)
                            at = 2 * q * f
                            last = three_passes(nc, kb[u % 2][:, 0:2 * f], zt[0][0:m, t, :], zt[1][0:m, t, :],
                                                ahead[s][0][0:m, t, at:at + 2 * f], ahead[s][1][0:m, t, at:at + 2 * f], t == 0, t == NT[s] - 1)
                        last.then_inc(fmm, 1)
                elif st[0] == "yt":
                    pe.wait_ge(y_out, pos[("fwd", st[1], st[2])]["f"] + GROUPS[s])
                    for b in range(-(-NK[s] // 4)):
                        u = p_["t"] + b
                        if u >= 2:
                            pe.wait_ge(*tuse[u - 2])
                        for k in range(4 * b, min(4 * b + 4, NK[s])):
                            m = ksize(s, k)
                            last = nc.tensor.transpose(tb[u % 2][0:m, (k % 4) * P:(k % 4 + 1) * P], y[:, k * P:k * P + m], ident[:, :])
                        last.then_inc(ytm, 1)
                else:
                    pe.wait_ge(const_b[s], 64)
                    if order(st):
                        pe.wait_ge(gated, cuts_before(st))
                    runs = [(b, range(0, 4)) for b in range(len(CUTS[s]))] + [(b, range(4, NK[s])) for b in range(len(CUTS[s]))]
                    for b, ks in runs:
                        c0, cn = CUTS[s][b]
                        for k in ks:
                            pe.wait_ge(yt_lo, pos[("yt", st[1], st[2])]["yt"] + k // 4 + 1)
                            m = ksize(s, k)
                            last = three_passes(nc, ib[b][:, 0:cn], yt[0][0:m, k, :], yt[1][0:m, k, :],
                                                back[s][0][0:m, k, c0:c0 + cn], back[s][1][0:m, k, c0:c0 + cn], k == 0, k == NK[s] - 1)
                        if ks[0]:
                            last.then_inc(imm_, 1)


        def split_turns(eng, st, count, base_sem, base, dst, mine, size):
            s = units[st[1]][0]
            for b in range(-(-count // 4)):
                u = pos[st]["t"] + b
                eng.wait_ge(base_sem, base + b + 1)
                tiles = list(range(4 * b, min(4 * b + 4, count)))
                full = [t for t in tiles if size(s, t) == P]
                parts = ([(full[0], len(full), P)] if full else []) + [(t, 1, size(s, t)) for t in tiles if size(s, t) < P]
                for i, (t, k, m) in enumerate(parts):
                    bank = tb[u % 2][0:m, :].rearrange("p (k c) -> p k c", k=4)[:, t % 4:t % 4 + k, :]
                    yield b, i == len(parts) - 1, bank, [d[0:m, t:t + k, :] for d in dst]

        @block.scalar
        def _(act):
            for st in steps:
                s, j = units[st[1]]
                f = FG[s]
                if st[0] == "hgen":
                    for t in range(NT[s]):
                        u, m = pos[st]["h"] + t, tsize(s, t)
                        act.wait_ge(h_sum, u + 1)
                        if t == 0 and order(st):
                            act.wait_ge(kmm, pos[("kf", st[1] - 1, 1)]["kf"] + len(KF_FILLS[units[st[1] - 1][0]]))
                        act.activation(hs[0][0:m, t, :, :, :], pair[u % 2][0:m, :, :, :], ACT.Copy).then_inc(h_hi, 1)
                elif st[0] == "kf":
                    o = st[2]
                    if o == 0 and st[1] >= 2:
                        act.wait_ge(f_mul, pos[("fwd", st[1] - 2, 1)]["f"] + GROUPS[units[st[1] - 2][0]])
                    skip = g.taps[:, 4 * HY_TILES + o * CT + j:4 * HY_TILES + o * CT + j + 1]
                    spec = kf[st[1] % 2][:, o, 0:W[s]].rearrange("p (g c f) -> p g c f", c=2, f=f)
                    for q, (part, g0, ng) in enumerate(KF_FILLS[s]):
                        u = pos[st]["k"] + q
                        act.wait_ge(kmm, pos[st]["kf"] + q + 1)
                        for c in ((0, 1) if part == 2 else (part,)):
                            at = c * f if part == 2 else 0
                            bank = kb[u % 2][:, at:at + ng * f].rearrange("p (g f) -> p g f", f=f)
                            if c == 0:
                                ins = act.activation(spec[:, g0:g0 + ng, c, :], bank, ACT.Identity, bias=skip)
                            else:
                                ins = act.activation(spec[:, g0:g0 + ng, c, :], bank, ACT.Copy)
                        ins.then_inc(k_out, 1)
                elif st[0] == "zt":
                    k = order(st)
                    if k:
                        act.wait_ge(fmm, sum(GROUPS[units[x[1]][0]] for x in steps if x[0] == "fwd" and order(x) < k))
                    for b, last, bank, (hi, lo) in split_turns(act, st, NT[s], ztm, pos[st]["zt"], zt, zt_hi, tsize):
                        ins = act.activation(hi, bank, ACT.Copy)
                        if last:
                            ins.then_inc(zt_hi, 1)
                elif st[0] == "yt":
                    k = order(st)
                    if k:
                        act.wait_ge(imm_, cuts_before(("inv",) + st[1:]))
                    for b, last, bank, (hi, lo) in split_turns(act, st, NK[s], ytm, pos[st]["yt"], yt, yt_hi, ksize):
                        ins = act.activation(hi, bank, ACT.Copy)
                        if last:
                            ins.then_inc(yt_hi, 1)

        @block.vector
        def _(dve):
            for st in steps:
                s, j = units[st[1]]
                n, f = LENS[s], FG[s]
                if st[0] == "hgen":
                    def lower(t):
                        u, m = pos[st]["h"] + t, tsize(s, t)
                        dve.wait_ge(h_hi, u + 1)
                        nc.vector.tensor_tensor(hs[1][0:m, t, :, :, :], pair[u % 2][0:m, :, :, :], hs[0][0:m, t, :, :, :].bitcast(F32),
                                                ALU.subtract).then_inc(h_lo, 1)
                    dve.wait_ge(dec_in[st[1] % 2], 48 * (st[1] // 2 + 1))
                    for t in range(NT[s]):
                        u, m = pos[st]["h"] + t, tsize(s, t)
                        dve.wait_ge(hg, u + 1)
                        if u >= 2:
                            dve.wait_ge(h_sum, u - 1)
                        nc.vector.tensor_tensor(taps[u % 2][0:m, :, :], hb[u % 2][0:m, :].rearrange("p (q c) -> p q c", q=4),
                                                decay[st[1] % 2][0:m, t, :].unsqueeze(1).broadcast_to([m, 4, P]), ALU.mult).then_inc(h_decayed, 1)
                        if t:
                            lower(t - 1)
                    lower(NT[s] - 1)
                elif st[0] == "zt":
                    for b, last, bank, (hi, lo) in split_turns(dve, st, NT[s], zt_hi, pos[st]["zt"], zt, zt_lo, tsize):
                        ins = nc.vector.tensor_tensor(lo, bank, hi.bitcast(F32), ALU.subtract)
                        if last:
                            ins.then_inc(zt_lo, 1)
                elif st[0] == "yt":
                    for b, last, bank, (hi, lo) in split_turns(dve, st, NK[s], yt_hi, pos[st]["yt"], yt, yt_lo, ksize):
                        ins = nc.vector.tensor_tensor(lo, bank, hi.bitcast(F32), ALU.subtract)
                        if last:
                            ins.then_inc(yt_lo, 1)
                elif st[0] == "fwd":
                    o = st[2]
                    dve.wait_ge(k_out, pos[("kf", st[1], o)]["kf"] + len(KF_FILLS[s]))
                    for q in range(GROUPS[s]):
                        u, b = pos[st]["f"] + q, pos[st]["k"] + q
                        dve.wait_ge(fmm, u + 1)
                        if u >= 2:
                            dve.wait_ge(y_out, u - 1)
                        zf = kb[b % 2][:, 0:2 * f].rearrange("p (c f) -> p c f", c=2)
                        spec = kf[st[1] % 2][:, o, :]
                        for c, dst in enumerate((prodA[u % 2], prodB[u % 2])):
                            at = (2 * q + c) * f
                            last = nc.vector.tensor_tensor(dst[:, :, 0:f], zf, spec[:, at:at + f].unsqueeze(1).broadcast_to([P, 2, f]), ALU.mult)
                        last.then_inc(f_mul, 1)
                elif st[0] == "inv":
                    o, u = st[2], st[1]
                    if o == 0:
                        dst = z[0]
                    else:
                        dst = z[1] if u % 2 == 0 else g.zx
                        if u >= 2:
                            dve.wait_ge(store[u % 2], 16 * (u // 2))
                    if o == 0:
                        dve.wait_ge(v_in[u % 2], 16 * (u // 2 + 1))
                    for b, (c0, cn) in enumerate(CUTS[s]):
                        dve.wait_ge(imm_, cuts_before(st) + b + 1)
                        nc.vector.tensor_tensor(dst[:, c0:c0 + cn], ib[b][:, 0:cn], src[u % 2][:, 1 + o, c0:c0 + cn], ALU.mult)\
                          .then_inc(gated, 1)
    g.sb.at = top


def stage_merge(g):
    nc, io, S = g.nc, g.io, g.sem
    sb = g.sb
    mhi, mlo = g.mhi, g.mlo
    top = sb.at
    up = sb("up_in", [P, KT, T])
    uhi = sb("up_in_hi", [P, KT, T], F32R)
    ulo = sb("up_in_lo", [P, KT, T], F32R)
    raw = [sb("wu_raw", [P, KT, WCH]) for _ in range(2)]
    whi = [sb("wu_hi", [P, KT, WCH], F32R) for _ in range(1)]
    wlo = [sb("wu_lo", [P, KT, WCH], F32R) for _ in range(1)]
    sig = [sb("sig_pair", [P, 2, T]) for _ in range(2)]
    ga = [sb("gated_pair", [P, 2, HALF]) for _ in range(1)]
    mm_ = sb("merged", [P, HALF])
    (up_in, u_hi, u_lo, w0, w1, wh, wl, sg0, sg1, prod, gd, summed, m_hi, m_lo) = S(
        "mg_up_in mg_u_hi mg_u_lo mg_w0 mg_w1 mg_wh mg_wl mg_sg0 mg_sg1 mg_prod mg_gated mg_sum mg_m_hi mg_m_lo")
    wsem, sgs = [w0, w1], [sg0, sg1]
    NCH = D // WCH
    banks = [(g.ps[0], g.ps[1]), (g.ps[2], g.ps[3]), (g.ps[4], g.ps[5]), (g.ps[6], g.ps[7])]
    with nc.Block() as block:
        @block.sync
        def _(sp):
            def load(c):
                if c >= 2:
                    sp.wait_ge(wl, c - 1)
                w = raw[c % 2]
                for kv in range(N_KV):
                    sp.dma_start(w[kv * HEAD_DIM:(kv + 1) * HEAD_DIM, 0:GROUP, :],
                                 io["w_attn_up"][0].rearrange("(v j d) n -> v d j n", v=N_KV, d=HEAD_DIM)[kv, :, :, c * WCH:(c + 1) * WCH])\
                      .then_inc(wsem[c % 2], 16)
                sp.dma_start(w[:, GROUP:KT, :], io["w_hyena_up"][0].rearrange("(j p) n -> p j n", p=P)[:, :, c * WCH:(c + 1) * WCH])\
                  .then_inc(wsem[c % 2], 16)

            def load_sig(m):
                if m >= 2:
                    sp.wait_ge(gd, 2 * (m - 1))
                sp.dma_start(sig[m % 2][:, :, :], g.sigS.rearrange("(q m p) t -> m p q t", q=2, p=P)[m]).then_inc(sgs[m % 2], 16)
            for k in range(KT):
                sp.dma_start(up[:, k, :], g.upS[k * P:(k + 1) * P, :]).then_inc(up_in, 16)
            load(0)
            load(1)
            load_sig(0)
            load_sig(1)
            for m in range(2, KT):
                load_sig(m)
                if m % 2 == 0 and m // 2 + 1 < NCH:
                    load(m // 2 + 1)

        @block.scalar
        def _(act):
            act.wait_ge(up_in, 16 * KT)
            for k in range(KT):
                act.activation(uhi[:, k, :], up[:, k, :], ACT.Copy).then_inc(u_hi, 1)
            for m in range(KT):
                c = m // 2
                if m % 2 == 0:
                    act.wait_ge(wsem[c % 2], 48 * (c // 2 + 1))
                    if c:
                        act.wait_ge(prod, 4 * c)
                    act.activation(whi[0][:, :, :], raw[c % 2][:, :, :], ACT.Copy).then_inc(wh, 1)
                for h in range(2):
                    act.wait_ge(summed, 2 * m + h + 1)
                    act.activation(mhi[:, m, h * HALF:(h + 1) * HALF], mm_[:, :], ACT.Copy).then_inc(m_hi, 1)

        @block.vector
        def _(dve):
            for k in range(KT):
                dve.wait_ge(u_hi, k + 1)
                nc.vector.tensor_tensor(ulo[:, k, :], up[:, k, :], uhi[:, k, :].bitcast(F32), ALU.subtract).then_inc(u_lo, 1)
            for m in range(KT):
                dve.wait_ge(sgs[m % 2], 16 * (m // 2 + 1))
                for h in range(2):
                    u = 2 * m + h
                    dve.wait_ge(prod, u + 1)
                    if u:
                        dve.wait_ge(summed, u)
                    for q in range(2):
                        last = nc.vector.tensor_tensor(ga[0][:, q, :], banks[u % 4][q][:, 0:HALF], sig[m % 2][:, q, h * HALF:(h + 1) * HALF],
                                                       ALU.mult)
                    last.then_inc(gd, 1)
                    dve.wait_ge(gd, u + 1)
                    if u:
                        dve.wait_ge(m_lo, u)
                    nc.vector.tensor_tensor(mm_[:, :], ga[0][:, 0, :], ga[0][:, 1, :], ALU.add).then_inc(summed, 1)
                    dve.wait_ge(m_hi, u + 1)
                    nc.vector.tensor_tensor(mlo[:, m, h * HALF:(h + 1) * HALF], mm_[:, :], mhi[:, m, h * HALF:(h + 1) * HALF].bitcast(F32),
                                            ALU.subtract).then_inc(m_lo, 1)

        @block.gpsimd
        def _(pool):
            for c in range(NCH):
                pool.wait_ge(wh, c + 1)
                nc.gpsimd.tensor_tensor(wlo[0][:, :, :], raw[c % 2][:, :, :], whi[0][:, :, :].bitcast(F32), ALU.subtract).then_inc(wl, 1)

        @block.tensor
        def _(pe):
            pe.wait_ge(u_lo, KT)
            for m in range(KT):
                if m % 2 == 0:
                    pe.wait_ge(wh, m // 2 + 1)
                    pe.wait_ge(wl, m // 2 + 1)
                for h in range(2):
                    u = 2 * m + h
                    if u >= 4:
                        pe.wait_ge(gd, u - 3)
                    for q in range(2):
                        for k in range(4):
                            kt = 4 * q + k
                            c0 = (m % 2) * P
                            last = three_passes(nc, banks[u % 4][q][:, 0:HALF], whi[0][:, kt, c0:c0 + P], wlo[0][:, kt, c0:c0 + P],
                                                uhi[:, kt, h * HALF:(h + 1) * HALF], ulo[:, kt, h * HALF:(h + 1) * HALF], k == 0, k == 3)
                    last.then_inc(prod, 1)
    sb.at = top


def stage_route(g):
    nc, io, S = g.nc, g.io, g.sem
    sb = g.sb
    mhi, mlo, ident = g.mhi, g.mlo, g.ident
    top = sb.at
    NTOK = len(TOK_TILES)
    raw = sb("wo_raw", [P, KT, D])
    whi = sb("wo_hi", [P, KT, D], F32R)
    wlo = sb("wo_lo", [P, KT, D], F32R)
    h = [sb("residual_in", [P, D]) for _ in range(2)]
    hn = [sb("ffn_normed", [P, D]) for _ in range(2)]
    gain = sb("ffn_gain", [P, D])
    hT = sb("ffn_turned", [P, KT, P])
    wr = sb("w_router", [P, KT, E])
    ss = sb("square_sums", [P, 2 * NTOK])
    lg = sb("logits", [P, NTOK, E])
    red = sb("softmax_cols", [P, 2, NTOK])
    af = [[sb(f"affinity{s}_{x}", [E, LENS[s]]) for x in range(2)] for s in range(2)]
    rounds = [-(-c // 8) for c in CAPS]
    val = [sb(f"top_values{s}", [E, 8 * rounds[s]]) for s in range(2)]
    ix = [sb(f"top_index{s}", [E, 8 * rounds[s]], U32) for s in range(2)]
    both = sb("slots_by_expert", [E, 2, SLOTS])
    (w_in, w_hi, w_lo, hin0, hin1, cin, prod, h2d, sq, mean, root, hnd, st0, st1, trn, t_act, t_dve, lmm, lgd, exd, afd,
     aft, own, bd, btd, hT_used, hst0, hst1) = S(
        "rt_w_in rt_w_hi rt_w_lo rt_hin0 rt_hin1 rt_cin rt_prod rt_h2 rt_sq rt_mean rt_root rt_hn rt_st0 rt_st1 rt_trn "
        "rt_t_act rt_t_dve rt_lmm rt_lg rt_exp rt_aff rt_afft rt_own rt_both rt_both_turned rt_ht_used rt_hst0 rt_hst1")
    hin, st, hst = [hin0, hin1], [st0, st1], [hst0, hst1]
    pieces = [token_pieces(t0, m, io["x_prompt"][0], io["x_sample"][0], io["meta_tokens"]) for t0, m in TOK_TILES]
    total = [[0, 0]]
    for i, ps_ in enumerate(pieces):
        now = list(total[-1])
        now[i % 2] += 16 * len(ps_)
        total.append(now)
    acc = [(g.ps[0], g.ps[1]), (g.ps[2], g.ps[3])]
    w_sems = S(" ".join(f"rt_w{k}" for k in range(KT)))

    with nc.Block() as block:
        @block.sync
        def _(sp):
            def load(i):
                if i >= 2:
                    sp.wait_ge(hnd, i - 1)
                    sp.wait_ge(hst[i % 2], 16 * (i // 2))
                for r0, src in pieces[i]:
                    sp.dma_start(h[i % 2][r0:r0 + src.shape[0], :], src).then_inc(hin[i % 2], 16)
            for k in range(KT):
                sp.dma_start(raw[:, k, :], io["w_out"][0, k * P:(k + 1) * P, :]).then_inc(w_sems[k], 16)
            load(0)
            load(1)
            sp.dma_start(gain[:, :], io["norm_ffn_g"][0].partition_broadcast(P)).then_inc(cin, 16)
            sp.dma_start(wr[:, :, :], io["w_router"][0].rearrange("(t p) e -> p t e", p=P)).then_inc(cin, 16)
            for i, (t0, m) in enumerate(TOK_TILES):
                sp.wait_ge(h2d, i + 1)
                sp.dma_start(g.accS[t0:t0 + m, :], h[i % 2][0:m, :]).then_inc(hst[i % 2], 16)
                sp.wait_ge(hnd, i + 1)
                sp.dma_start(g.hnS[t0:t0 + m, :], hn[i % 2][0:m, :]).then_inc(st[i % 2], 16)
                if i + 2 < NTOK:
                    load(i + 2)
            sp.wait_ge(prod, NTOK)
            for n in range(RING):
                load_chunk(sp, g, n)
            for k in range(2):
                sp.wait_ge(st[k], 16 * ((NTOK + 1 - k) // 2))
                sp.wait_ge(hst[k], 16 * ((NTOK + 1 - k) // 2))

        @block.tensor
        def _(pe):
            def product(i):
                t0, m = TOK_TILES[i]
                if i >= 2:
                    pe.wait_ge(h2d, i - 1)
                for b in range(2):
                    for k in range(KT):
                        if i == 0 and b == 0:
                            pe.wait_ge(w_hi, k + 1)
                            pe.wait_ge(w_lo, k + 1)
                        last = three_passes(nc, acc[i % 2][b][0:m, :], mhi[:, k, t0:t0 + m], mlo[:, k, t0:t0 + m],
                                            whi[:, k, b * BANK:(b + 1) * BANK], wlo[:, k, b * BANK:(b + 1) * BANK], k == 0, k == KT - 1)
                last.then_inc(prod, 1)

            def turn(i):
                t0, m = TOK_TILES[i]
                pe.wait_ge(hnd, i + 1)
                if i:
                    pe.wait_ge(t_act, i)
                    pe.wait_ge(t_dve, i)
                for k in range(KT):
                    last = nc.tensor.transpose(g.ps[4 + k // 4][:, (k % 4) * P:(k % 4) * P + m], hn[i % 2][0:m, k * P:(k + 1) * P],
                                               ident[0:m, 0:m])
                last.then_inc(trn, 1)

            def logits(i):
                t0, m = TOK_TILES[i]
                pe.wait_ge(t_act, i + 1)
                pe.wait_ge(t_dve, i + 1)
                if i:
                    pe.wait_ge(lgd, i)
                for k in range(KT):
                    last = nc.tensor.matmul(g.ps[6][0:m, 0:E], hT[:, k, 0:m], wr[:, k, :], start=(k == 0), stop=(k == KT - 1))
                last.then_inc(lmm, 1)

            pe.wait_ge(cin, 32)
            product(0)
            for i in range(1, NTOK):
                product(i)
                turn(i - 1)
                logits(i - 1)
            turn(NTOK - 1)
            logits(NTOK - 1)
            pe.wait_ge(afd, 1)
            pe.wait_ge(lgd, NTOK)
            for i, (t0, m) in enumerate(TOK_TILES):
                last = nc.tensor.transpose(g.ps[7 - i // 4][0:E, (i % 4) * P:(i % 4) * P + m], lg[0:m, i, :], ident[0:m, 0:m])
            last.then_inc(aft, 1)
            pe.wait_ge(bd, 4)
            for q in range(2):
                last = nc.tensor.transpose(g.ps[4][0:SLOTS, q * P:q * P + E], both[:, q, :], ident[0:E, 0:E])
            last.then_inc(btd, 1)

        @block.gpsimd
        def _(pool):
            for k in range(KT):
                pool.wait_ge(w_hi, k + 1)
                nc.gpsimd.tensor_tensor(wlo[:, k, :], raw[:, k, :], whi[:, k, :].bitcast(F32), ALU.subtract).then_inc(w_lo, 1)

        @block.scalar
        def _(act):
            for k in range(KT):
                act.wait_ge(w_sems[k], 16)
                act.activation(whi[:, k, :], raw[:, k, :], ACT.Copy).then_inc(w_hi, 1)
            for i, (t0, m) in enumerate(TOK_TILES):
                act.wait_ge(h2d, i + 1)
                if i >= 2:
                    act.wait_ge(trn, i - 1)
                    act.wait_ge(st[i % 2], 16 * (i // 2))
                act.activation(hn[i % 2][0:m, :], h[i % 2][0:m, :], ACT.Square, accum_out=ss[0:m, i:i + 1]).then_inc(sq, 1)
                act.wait_ge(mean, i + 1)
                act.activation(ss[0:m, NTOK + i:NTOK + i + 1], ss[0:m, i:i + 1], ACT.Sqrt).then_inc(root, 1)
                act.wait_ge(trn, i + 1)
                if i:
                    act.wait_ge(lmm, i)
                act.activation(hT[:, 0:4, 0:m], g.ps[4][:, :].rearrange("p (k t) -> p k t", k=4)[:, :, 0:m], ACT.Copy).then_inc(t_act, 1)
            act.wait_ge(own, NTOK + 3)
            act.activation(lg[:, :, :], lg[:, :, :], ACT.Exp).then_inc(exd, 1)

        @block.vector
        def _(dve):
            link = linked(dve, own)
            link(nc.vector.memset(lg[:, :, :], 0.0))
            dve.wait_ge(cin, 32)
            for i, (t0, m) in enumerate(TOK_TILES):
                dve.wait_ge(hin[i % 2], total[i + 1][i % 2])
                dve.wait_ge(prod, i + 1)
                for b in range(2):
                    last = nc.vector.tensor_tensor(h[i % 2][0:m, b * BANK:(b + 1) * BANK], acc[i % 2][b][0:m, :],
                                                   h[i % 2][0:m, b * BANK:(b + 1) * BANK], ALU.add)
                last.then_inc(h2d, 1)
                dve.wait_ge(sq, i + 1)
                nc.vector.tensor_scalar(ss[0:m, i:i + 1], ss[0:m, i:i + 1], 1.0 / D, EPS, ALU.mult, ALU.add).then_inc(mean, 1)
                dve.wait_ge(root, i + 1)
                link(nc.vector.reciprocal(ss[0:m, i:i + 1], ss[0:m, NTOK + i:NTOK + i + 1]))
                nc.vector.scalar_tensor_tensor(hn[i % 2][0:m, :], h[i % 2][0:m, :], ss[0:m, i:i + 1], gain[0:m, :],
                                               ALU.mult, ALU.mult).then_inc(hnd, 1)
                dve.wait_ge(trn, i + 1)
                if i:
                    dve.wait_ge(lmm, i)
                nc.vector.tensor_copy(hT[:, 4:8, 0:m], g.ps[5][:, :].rearrange("p (k t) -> p k t", k=4)[:, :, 0:m]).then_inc(t_dve, 1)
                dve.wait_ge(lmm, i + 1)
                nc.vector.tensor_copy(lg[0:m, i, :], g.ps[6][0:m, 0:E]).then_inc(lgd, 1)
            dve.wait_ge(lgd, NTOK)
            link(nc.vector.tensor_reduce(red[:, 0, :], lg[:, :, :], AX.X, ALU.max))
            link(nc.vector.tensor_tensor(lg[:, :, :], lg[:, :, :], red[:, 0, :].unsqueeze(2).broadcast_to([P, NTOK, E]), ALU.subtract))
            dve.wait_ge(exd, 1)
            link(nc.vector.tensor_reduce(red[:, 0, :], lg[:, :, :], AX.X, ALU.add))
            link(nc.vector.reciprocal(red[:, 1, :], red[:, 0, :]))
            nc.vector.tensor_tensor(lg[:, :, :], lg[:, :, :], red[:, 1, :].unsqueeze(2).broadcast_to([P, NTOK, E]), ALU.mult).then_inc(afd, 1)
            dve.wait_ge(aft, 1)
            link(nc.vector.tensor_copy(af[0][0][:, 0:BANK], g.ps[7][0:E, :]))
            link(nc.vector.tensor_copy(af[0][0][:, BANK:LENS[0]], g.ps[6][0:E, 0:LENS[0] - BANK]))
            link(nc.vector.tensor_copy(af[1][0][:, :], g.ps[6][0:E, LENS[0] - BANK:T - BANK]))
            for s in range(2):
                for r in range(rounds[s]):
                    a, b = af[s][r % 2], af[s][(r + 1) % 2]
                    c = slice(8 * r, 8 * r + 8)
                    link(nc.vector.max(val[s][:, c], a[:, :]))
                    link(nc.vector.max_index(ix[s][:, c], val[s][:, c], a[:, :]))
                    if r + 1 < rounds[s]:
                        link(nc.vector.match_replace(b[:, :], val[s][:, c], a[:, :], -1.0))
            c0 = CAPS[0]
            nc.vector.tensor_copy(both[:, 0, 0:c0], val[0][:, 0:c0]).then_inc(bd, 1)
            nc.vector.tensor_copy(both[:, 0, c0:SLOTS], val[1][:, 0:CAPS[1]]).then_inc(bd, 1)
            nc.vector.tensor_copy(both[:, 1, 0:c0], ix[0][:, 0:c0]).then_inc(bd, 1)
            nc.vector.tensor_scalar(both[:, 1, c0:SLOTS], ix[1][:, 0:CAPS[1]], float(STARTS[1]), None, ALU.add).then_inc(bd, 1)
            dve.wait_ge(btd, 1)
            link(nc.vector.tensor_copy(g.gate_w[0:SLOTS, :], g.ps[4][0:SLOTS, 0:E]))
            link(nc.vector.tensor_copy(g.slot_tok[0:SLOTS, 0:E], g.ps[4][0:SLOTS, P:P + E]))
            link(nc.vector.tensor_copy(g.slot_tok[0:SLOTS, E:E + 1], g.ps[4][0:SLOTS, P:P + 1]))
    sb.at = top


CHUNKS = 12
RING = 6
FCH = FE // 4
FT = FCH // P
HC = 2048


def expert_chunk(io, e, k):
    if k < 8:
        w = io[("w_exp_gate", "w_exp_up")[k % 2]][0].rearrange("e (t p) f -> e p t f", p=P)
        return w[e, :, :, (k // 2) * FCH:(k // 2 + 1) * FCH]
    return io["w_exp_down"][0].rearrange("e (c t p) d -> e c p t d", c=4, p=P)[e, k - 8]


def load_chunk(sp, g, n):
    e, k = divmod(n, CHUNKS)
    src = expert_chunk(g.io, e, k)
    sp.dma_start(g.ring[n % RING][:, :].rearrange("p (t f) -> p t f", t=src.shape[1]), src).then_inc(g.ring_in[n % RING], 16)


def stage_experts(g):
    nc, S = g.nc, g.sem
    sb = g.sb
    ident = g.ident
    top = sb.at
    sb.at = g.ring_end
    ring = g.ring
    whi = [sb("we_hi", [P, HC], F32R) for _ in range(4)]
    wlo = [sb("we_lo", [P, HC], F32R) for _ in range(4)]
    xe = sb("gathered", [P, D])
    xT = [sb(f"gathered_turned_{x}", [P, KT, SLOTS], F32R) for x in ("hi", "lo")]
    sig = sb("gate_sigmoid", [P, FCH])
    silu = sb("gate_silu", [P, FCH])
    hid = sb("hidden", [P, FCH])
    hT = [sb(f"hidden_turned_{x}", [P, 4 * FT, SLOTS], F32R) for x in ("hi", "lo")]
    ye = sb("expert_out", [P, D])
    nxt = sb("slots_next", [P, 1], U32)
    cur = sb("slots_now", [P, 1], U32)
    gcur = sb("gate_now", [P, 1])
    credit = sb("start_credits", [P, 4])
    (nxt_set, cur_set, gath, turned, t_hi, t_lo, used, w_hi, w_lo, sg_done, silu_done, hid_done, y_done, scat) = S(
        "ex_next ex_cur ex_gathered ex_turned ex_turned_hi ex_turned_lo ex_used ex_w_hi ex_w_lo ex_sig ex_silu ex_hid "
        "ex_y_done ex_scattered")
    gb, ub, tb, yb = [g.ps[0], g.ps[1]], [g.ps[2], g.ps[3]], [g.ps[4], g.ps[5]], [g.ps[6], g.ps[7]]
    TURNS = [(2, "h", 0), (4, "h", 1), (6, "h", 2), (7, "x", 0), (8, "h", 3), (9, "x", 1)]
    NTURN = len(TURNS)

    def turn_dst(kind, c, half):
        return (hT if kind == "h" else xT)[half][:, 4 * c:4 * c + 4, :]

    def turn_bank(n):
        return tb[n % 2][:, :].rearrange("p (k s) -> p k s", k=4)[:, :, 0:SLOTS]

    with nc.Block() as block:
        @block.sync
        def _(sp):
            for n in range(RING, E * CHUNKS):
                sp.wait_ge(w_lo, 2 * (n - RING + 1))
                load_chunk(sp, g, n)

        @block.gpsimd
        def _(pool):
            def gather():
                pool.indirect_dma_start(xe[0:SLOTS, :], None, g.hnS[:, :], bass.IndirectOffsetOnAxis(ap=nxt[0:SLOTS, 0:1], axis=0))\
                    .then_inc(gath, 16)
            pool.wait_ge(nxt_set, 1)
            gather()
            for e in range(E):
                pool.wait_ge(nxt_set, e + 2)
                pool.wait_ge(turned, NTURN * e + 2)
                gather()
                pool.wait_ge(cur_set, 2 * e + 2)
                pool.wait_ge(y_done, e + 2)
                pool.indirect_dma_start(g.accS[:, :], bass.IndirectOffsetOnAxis(ap=cur[0:SLOTS, 0:1], axis=0), ye[0:SLOTS, :], None,
                                        compute_op=ALU.add).then_inc(scat, 16)
                pool.wait_ge(scat, 16 * e + 16)
            pool.wait_ge(gath, 16 * (E + 1))

        @block.tensor
        def _(pe):
            def turn(kind, c, n):
                for k in range(4):
                    src = hid[0:SLOTS, k * P:(k + 1) * P] if kind == "h" else xe[0:SLOTS, (4 * c + k) * P:(4 * c + k + 1) * P]
                    last = nc.tensor.transpose(tb[n % 2][:, k * P:k * P + SLOTS], src, ident[0:SLOTS, 0:SLOTS])
                last.then_inc(turned, 1)

            def body(e):
                for k in range(CHUNKS):
                    if k == 0:
                        pe.wait_ge(t_lo, NTURN * e + 4)
                    if k < 8 and k % 2 == 0:
                        pe.wait_ge(hid_done, 4 * e + k // 2 + 1)
                    if k == 8:
                        pe.wait_ge(y_done, e + 1)
                    if k >= 8:
                        pe.wait_ge(t_lo, NTURN * e + 4 + (1, 2, 3, 5)[k - 8])
                    for half in range(2):
                        pe.wait_ge(w_lo, 2 * CHUNKS * e + 2 * k + half + 1)
                        hi, lo = whi[(2 * k + half) % 4], wlo[(2 * k + half) % 4]
                        if k < 8:
                            bank = (gb, ub)[k % 2][k // 2 % 2]
                            for i in range(4):
                                t = 4 * half + i
                                w = slice(i * FCH, (i + 1) * FCH)
                                last = three_passes(nc, bank[0:SLOTS, :], xT[0][:, t, :], xT[1][:, t, :], hi[:, w], lo[:, w],
                                                    t == 0, t == KT - 1)
                        else:
                            for i in range(2):
                                f = 4 * (k - 8) + 2 * half + i
                                for b in range(2):
                                    w = slice(i * D + b * BANK, i * D + (b + 1) * BANK)
                                    last = three_passes(nc, yb[b][0:SLOTS, :], hT[0][:, f, :], hT[1][:, f, :], hi[:, w], lo[:, w],
                                                        f == 0, f == 4 * FT - 1)
                        last.then_inc(used, 1)
                    for n, (after, kind, c) in enumerate(TURNS):
                        if after == k:
                            pe.wait_ge(t_lo, NTURN * e + n + 3)
                            if kind == "h":
                                pe.wait_ge(hid_done, 4 * e + c + 3)
                            elif c == 0:
                                pe.wait_ge(gath, 16 * e + 32)
                            turn(kind, c, n)
            pe.wait_ge(gath, 16)
            turn("x", 0, 0)
            turn("x", 1, 1)
            with pe.Fori(0, E) as e:
                body(e)

        def slot_free(eng, e, k, half):
            eng.wait_ge(used, 2 * CHUNKS * e + 2 * k + half - 3)

        @block.scalar
        def _(act):
            def hi_of(e, k, half):
                act.wait_ge(g.ring_in[k % RING], 32 * e + 16 * (k // RING + 1))
                act.activation(whi[(2 * k + half) % 4][:, :], ring[k % RING][:, half * HC:(half + 1) * HC], ACT.Copy).then_inc(w_hi, 1)

            def turn_hi(e, n, kind, c):
                act.wait_ge(turned, NTURN * e + n + 3)
                act.activation(turn_dst(kind, c, 0), turn_bank(n), ACT.Copy).then_inc(t_hi, 1)

            def body(e, last):
                for k in range(2, CHUNKS + 2):
                    slot_free(act, e, k, 0)
                    if k < CHUNKS or not last:
                        hi_of(e, k, 0)
                    slot_free(act, e, k, 1)
                    if k % 2 and k < 10:
                        c = (k - 3) // 2
                        act.wait_ge(silu_done, 4 * e + c + 1)
                        act.activation(sig[0:SLOTS, :], gb[c % 2][0:SLOTS, :], ACT.Sigmoid).then_inc(sg_done, 1)
                    for n, (after, kind, c) in enumerate(TURNS):
                        if after == k - 2:
                            turn_hi(e, n, kind, c)
                    if k < CHUNKS or not last:
                        hi_of(e, k, 1)
            for u in range(4):
                hi_of(0, u // 2, u % 2)
            for c in range(2):
                act.wait_ge(turned, c + 1)
                act.activation(turn_dst("x", c, 0), turn_bank(c), ACT.Copy).then_inc(t_hi, 1)
            with act.Fori(0, E - 1) as e:
                body(e, False)
            body(E - 1, True)

        @block.vector
        def _(dve):
            def lo_of(e, k, half):
                u = (2 * k + half) % 4
                dve.wait_ge(w_hi, 2 * CHUNKS * e + 2 * k + half + 1)
                nc.vector.tensor_tensor(wlo[u][:, :], ring[k % RING][:, half * HC:(half + 1) * HC], whi[u][:, :].bitcast(F32),
                                        ALU.subtract).then_inc(w_lo, 1)

            def turn_lo(n, kind, c):
                nc.vector.tensor_tensor(turn_dst(kind, c, 1), turn_bank(n), turn_dst(kind, c, 0).bitcast(F32), ALU.subtract)\
                  .then_inc(t_lo, 1)

            def body(e, last):
                dve.wait_ge(gath, 16 * e + 16)
                nc.vector.tensor_copy(nxt[0:SLOTS, :], g.slot_tok[0:SLOTS, bass.ds(e + 1, 1)]).then_inc(nxt_set, 1)
                for k in range(2, CHUNKS + 2):
                    slot_free(dve, e, k, 0)
                    if k < CHUNKS or not last:
                        lo_of(e, k, 0)
                    slot_free(dve, e, k, 1)
                    if k % 2 and k < 10:
                        c = (k - 3) // 2
                        dve.wait_ge(sg_done, 4 * e + c + 1)
                        nc.vector.tensor_tensor(silu[0:SLOTS, :], gb[c % 2][0:SLOTS, :], sig[0:SLOTS, :], ALU.mult).then_inc(silu_done, 1)
                        dve.wait_ge(silu_done, 4 * e + c + 2)
                        dve.wait_ge(turned, NTURN * e + 2 + (0, 1, 2, 3)[c])
                        nc.vector.tensor_tensor(hid[0:SLOTS, :], ub[c % 2][0:SLOTS, :], silu[0:SLOTS, :], ALU.mult).then_inc(hid_done, 1)
                    for n, (after, kind, c) in enumerate(TURNS):
                        if after == k - 2:
                            dve.wait_ge(t_hi, NTURN * e + n + 3)
                            turn_lo(n, kind, c)
                    if k == CHUNKS + 1:
                        dve.wait_ge(gath, 16 * e + 32)
                        nc.vector.tensor_copy(gcur[0:SLOTS, :], g.gate_w[0:SLOTS, bass.ds(e, 1)]).then_inc(cur_set, 1)
                        nc.vector.tensor_copy(cur[0:SLOTS, :], g.slot_tok[0:SLOTS, bass.ds(e, 1)]).then_inc(cur_set, 1)
                        dve.wait_ge(cur_set, 2 * e + 1)
                        for b in range(2):
                            end = nc.vector.tensor_scalar(ye[0:SLOTS, b * BANK:(b + 1) * BANK], yb[b][0:SLOTS, :], gcur[0:SLOTS, :],
                                                          None, ALU.mult)
                        end.then_inc(y_done, 1)
                    if k < CHUNKS or not last:
                        lo_of(e, k, 1)
            nc.vector.tensor_copy(nxt[0:SLOTS, :], g.slot_tok[0:SLOTS, 0:1]).then_inc(nxt_set, 1)
            nc.vector.memset(credit[0:1, 0:1], 0.0).then_inc(hid_done, 2)
            nc.vector.memset(credit[0:1, 1:2], 0.0).then_inc(silu_done, 1)
            nc.vector.memset(credit[0:1, 2:3], 0.0).then_inc(y_done, 1)
            nc.vector.memset(credit[0:1, 3:4], 0.0).then_inc(t_lo, 2)
            for u in range(4):
                lo_of(0, u // 2, u % 2)
            for c in range(2):
                dve.wait_ge(t_hi, c + 1)
                turn_lo(c, "x", c)
            with dve.Fori(0, E - 1) as e:
                body(e, False)
            body(E - 1, True)
    sb.at = top


def stage_finish(g):
    nc, io, S = g.nc, g.io, g.sem
    sb = g.sb
    top = sb.at
    NTOK = len(TOK_TILES)
    h = [sb("h_final", [P, D]) for _ in range(NTOK)]
    o = [sb("out_rows", [P, D]) for _ in range(NTOK)]
    gain = sb("final_gain", [P, D])
    ss = sb("square_sums", [P, 2 * NTOK])
    (cin, sq, mean, root, outd, outs, own) = S("fi_cin fi_sq fi_mean fi_root fi_out fi_stored fi_own")
    hin = S(" ".join(f"fi_in{k}" for k in range(NTOK)))
    with nc.Block() as block:
        @block.sync
        def _(sp):
            for i, (t0, m) in enumerate(TOK_TILES):
                sp.dma_start(h[i][0:m, :], g.accS[t0:t0 + m, :]).then_inc(hin[i], 16)
                if i == 0:
                    sp.dma_start(gain[:, :], io["norm_final_g"].partition_broadcast(P)).then_inc(cin, 16)
            n = 0
            for i, (t0, m) in enumerate(TOK_TILES):
                sp.wait_ge(outd, i + 1)
                for s, y in enumerate(g.out):
                    lo, hi = max(t0, STARTS[s] + N_META), min(t0 + m, STARTS[s] + LENS[s])
                    if lo < hi:
                        off = STARTS[s] + N_META
                        sp.dma_start(y[0, lo - off:hi - off, :], o[i][lo - t0:hi - t0, :]).then_inc(outs, 16)
                        n += 16
            sp.wait_ge(outs, n)

        @block.scalar
        def _(act):
            for i, (t0, m) in enumerate(TOK_TILES):
                act.wait_ge(hin[i], 16)
                act.activation(o[i][0:m, :], h[i][0:m, :], ACT.Square, accum_out=ss[0:m, i:i + 1]).then_inc(sq, 1)
                act.wait_ge(mean, i + 1)
                act.activation(ss[0:m, NTOK + i:NTOK + i + 1], ss[0:m, i:i + 1], ACT.Sqrt).then_inc(root, 1)

        @block.vector
        def _(dve):
            link = linked(dve, own)
            dve.wait_ge(cin, 16)
            for i, (t0, m) in enumerate(TOK_TILES):
                dve.wait_ge(sq, i + 1)
                nc.vector.tensor_scalar(ss[0:m, i:i + 1], ss[0:m, i:i + 1], 1.0 / D, EPS, ALU.mult, ALU.add).then_inc(mean, 1)
                dve.wait_ge(root, i + 1)
                link(nc.vector.reciprocal(ss[0:m, i:i + 1], ss[0:m, NTOK + i:NTOK + i + 1]))
                nc.vector.scalar_tensor_tensor(o[i][0:m, :], h[i][0:m, :], ss[0:m, i:i + 1], gain[0:m, :], ALU.mult, ALU.mult).then_inc(outd, 1)
    sb.at = top


def encode_layer(nc, io, out, debug=None):
    with ExitStack() as ctx:
        g = Ctx()
        g.nc, g.io, g.out = nc, io, out
        g.sem = Semaphores(nc)
        sb = g.sb = Map(nc)
        g.ps = [ctx.enter_context(nc.psum_tensor(f"bank{k}", [P, BANK], F32)) for k in range(8)]

        def scratch(name, shape):
            if debug is not None and name in debug:
                return debug[name]
            return nc.dram_tensor(name, shape, F32, kind="Internal").ap()
        g.hyS = scratch("hy_conv_rows", (3 * HYW, T + 1))
        g.sigS = scratch("gate_rows", (2 * D, T))
        g.upS = scratch("mixer_rows", (D, T))
        g.accS = scratch("residual_rows", (T, D))
        g.hnS = scratch("ffn_rows", (T, D))
        g.ident = sb("ident", [P, P])
        g.taps = sb("conv_taps", [P, 4 * HY_TILES + 2 * CT])
        g.gate_w = sb("slot_gates", [P, E])
        g.slot_tok = sb("slot_tokens", [P, E + 1], U32)
        top = sb.at
        g.feat = sb("filter_features", [FILT_HIDDEN, T])
        g.qk = sb("q_k_rotated", [P, GROUP + 1, T])
        g.v = sb("values", [P, len(VB), P])
        stage_project(g)
        g.sem.end_stage()
        stage_filter_mlp(g)
        g.sem.end_stage()
        stage_attend(g)
        g.sem.end_stage()
        sb.at = top
        sb.at = top + T * 4
        g.zx = sb("z_second", [P, LENS[0]])
        stage_hyena(g)
        g.sem.end_stage()
        sb.at = top
        g.ring = [sb(f"w_ring{k}", [P, 4096]) for k in range(RING)]
        g.ring_end = sb.at
        g.ring_in = [nc.alloc_semaphore(f"ring_in{k}") for k in range(RING)]
        sb.at = top
        g.mhi = sb("merged_hi", [P, KT, T], F32R)
        g.mlo = sb("merged_lo", [P, KT, T], F32R)
        stage_merge(g)
        g.sem.end_stage()
        stage_route(g)
        g.sem.end_stage()
        sb.at = top
        stage_experts(g)
        g.sem.end_stage()
        stage_finish(g)
        g.sem.end_stage()


_INS = ["x_prompt", "x_sample", "meta_tokens", "norm_mix_g", "w_in", "attn_sink", "hy_conv_w", "hy_conv_b",
        "hy_filt_w1", "hy_filt_b1", "hy_filt_w2", "hy_filt_b2", "hy_filt_w3", "hy_filt_b3", "hy_filt_freq",
        "hy_filt_wout", "hy_skip", "w_attn_up", "w_hyena_up", "w_out", "norm_ffn_g", "w_router", "w_exp_gate",
        "w_exp_up", "w_exp_down", "norm_final_g"]
_OUTS = [(1, SEQS[0], D), (1, SEQS[1], D)]


def kernel(**inputs):
    import concourse.bacc as _bacc
    from concourse.bass_utils import run_bass_kernel_spmd as _run

    nc = _bacc.Bacc("TRN2", target_bir_lowering=False, num_devices=1)
    arrays = {f"in_{name}": np.ascontiguousarray(inputs[name]) for name in _INS}
    arrays.update({f"in_{name}": a for name, a in shape_tables().items()})
    io = {name[3:]: nc.dram_tensor(name, a.shape, mybir.dt.from_np(a.dtype), kind="ExternalInput").ap()
          for name, a in arrays.items()}
    out = [nc.dram_tensor(f"out_{i}", shape, F32, kind="ExternalOutput").ap() for i, shape in enumerate(_OUTS)]
    encode_layer(nc, io, out)
    r = _run(nc, [arrays], core_ids=[0])
    return tuple(r.results[0][f"out_{i}"] for i in range(len(_OUTS)))
```

```python
import math
from contextlib import ExitStack

import numpy as np

import concourse.bass as bass
from concourse import mybir

F32 = mybir.dt.float32
F32R = mybir.dt.float32r
U32 = mybir.dt.uint32
ALU = mybir.AluOpType
ACT = mybir.ActivationFunctionType
AX = mybir.AxisListType

P = 128
BANK = 512

D = 1024
KT = D // P
N_META = 16
SEQS = (512, 256)
LENS = tuple(s + N_META for s in SEQS)
STARTS = (0, LENS[0])
T = sum(LENS)
HALF = T // 2
TOK_TILES = [(t, min(P, T - t)) for t in range(0, T, P)]

HEAD_DIM = 64
N_HEADS = 8
N_KV = 2
GROUP = N_HEADS // N_KV
ATTN = N_HEADS * HEAD_DIM
KVW = N_KV * HEAD_DIM
WINDOW = 128
HYW = D // 2
CT = HYW // P
HY_TILES = 3 * CT
C_K, C_V = ATTN, ATTN + KVW
C_HY = ATTN + 2 * KVW
C_GATE = C_HY + 3 * HYW
WCH = 256

FILT_EMB, FILT_BANDS, FILT_HIDDEN = 33, 16, 64
E = 16
FE = 2048
CAPS = tuple(2 * n // E for n in LENS)
SLOTS = sum(CAPS)
EPS = 1e-6

BLOCKS = []
for _s, _n in zip(STARTS, LENS):
    for _q in range(0, _n, P):
        _k0, _k1 = max(0, _q - P), min(_n, _q + 2 * P)
        BLOCKS.append((_s + _q, min(P, _n - _q), _s + _k0, _k1 - _k0, _k0 - (_q - P)))
VBLOCK0 = {s + q: i for i, (s, q) in enumerate((s, q) for s, n in zip(STARTS, LENS) for q in range(0, n, P))}

GROUPS = (3, 2)
FG = (178, 138)
W = tuple(2 * g * f for g, f in zip(GROUPS, FG))
NT = tuple(-(-n // P) for n in LENS)
NK = tuple(-(-w // P) for w in W)

TWO_PI = 2.0 * math.pi
MAGIC = 1.5 * 2.0 ** 23
NEG = -1e30


def dft_tables(s):
    n, g, f = LENS[s], GROUPS[s], FG[s]
    size = 2 * n
    k = np.arange(g * f)
    live = (k <= n).astype(np.float64)
    phase = 2 * np.pi * ((np.arange(n)[:, None] * k[None]) % size) / size
    cos, sin = np.cos(phase) * live, np.sin(phase) * live
    ahead = np.stack([cos.reshape(n, g, f), sin.reshape(n, g, f)], 2).reshape(n, 2 * g * f)
    weight = np.where((k == 0) | (k == n), 1.0, 2.0) / size
    back = np.stack([(cos * weight).reshape(n, g, f), (sin * weight).reshape(n, g, f)], 2)
    return ahead.astype(np.float32), np.ascontiguousarray(back.reshape(n, 2 * g * f).T).astype(np.float32)


def halves12(x):
    def top(v):
        u = v.view(np.uint32).astype(np.uint64)
        return (((u + 0x7FF + ((u >> 12) & 1)) >> 12) << 12).astype(np.uint32).view(np.float32)
    hi = top(x)
    return np.stack([hi, top(x - hi)])


def shape_tables():
    c = {}
    pos = np.concatenate([np.arange(n, dtype=np.float32) for n in LENS])
    half = HEAD_DIM // 2
    inv = (np.float32(1.0) / (np.float32(10000.0) ** (np.arange(half, dtype=np.float32) / np.float32(half)))).astype(np.float32)
    ang = (pos[None, :] * inv[:, None]).astype(np.float32)
    cos, sin = np.cos(ang), np.sin(ang)
    c["rope_cos"] = np.tile(cos, (4, 1)).astype(np.float32)
    c["rope_sin"] = np.concatenate([-sin, sin, -sin, sin]).astype(np.float32)
    rel = np.arange(3 * P)[None, :] - P - np.arange(P)[:, None]
    c["band"] = np.where(np.abs(rel) <= WINDOW, 0.0, NEG).astype(np.float32)
    c["ident"] = np.eye(P, dtype=np.float32)
    feats = []
    for s, n in enumerate(LENS):
        k = np.arange(n, dtype=np.float32)
        t = (k / np.float32(max(n - 1, 1))).astype(np.float32)
        step = (np.arange(FILT_BANDS, dtype=np.float32) / np.float32(FILT_BANDS - 1)).astype(np.float32)
        f = (np.float32(1e-4) * (np.float32(1) - step) + np.float32(FILT_BANDS - 1) * step).astype(np.float32)
        f[-1] = FILT_BANDS - 1
        ang = ((np.float32(2.0 * math.pi / n) * k)[:, None] * f[None]).astype(np.float32)
        feats.append(np.concatenate([t[:, None], np.cos(ang), -np.sin(ang)], -1).astype(np.float32).T)
        lo, hi = math.log(1e-2) / 1.5, math.log(1e-2) / 0.3
        step = (np.arange(HYW, dtype=np.float32) / np.float32(HYW - 1)).astype(np.float32)
        dl = np.abs((np.float32(lo) * (np.float32(1) - step) + np.float32(hi) * step).astype(np.float32))
        dl[-1] = abs(np.float32(hi))
        c[f"decay{s}"] = np.exp((-t[:, None] * dl[None]).astype(np.float32)).astype(np.float32)
        ahead, back = dft_tables(s)
        c[f"ahead{s}"] = halves12(ahead)
        c[f"back{s}"] = halves12(back)
    c["filt_z"] = np.ascontiguousarray(np.concatenate(feats, 1))
    return c


class Map:

    def __init__(self, nc):
        self.nc, self.at, self.n = nc, -(-nc.sbuf_base // 64) * 64, 0

    def __call__(self, name, shape, dt=F32):
        self.n += 1
        size = 4
        for x in shape[1:]:
            size *= x
        t = self.nc.alloc_sbuf_tensor_at(f"{name}_{self.n}", list(shape), dt, offset=self.at)
        self.at += -(-size // 64) * 64
        return t


class Ctx:
    pass


class Semaphores:

    def __init__(self, nc):
        self.nc, self.held = nc, []

    def __call__(self, names):
        new = [self.nc.alloc_semaphore(n) for n in names.split()]
        self.held += new
        return new

    def end_stage(self):
        self.nc.clear_and_free_semaphores(self.held)
        self.nc.all_engine_barrier()
        self.held = []


def linked(eng, sem):
    n = [0]

    def link(ins):
        n[0] += 1
        ins.then_inc(sem, 1)
        eng.wait_ge(sem, n[0])
    return link


def three_passes(nc, out, whi, wlo, xhi, xlo, first, last):
    nc.tensor.matmul(out, whi, xhi, start=first, stop=False)
    nc.tensor.matmul(out, whi, xlo, start=False, stop=False)
    return nc.tensor.matmul(out, wlo, xhi, start=False, stop=last)


def token_pieces(t0, n, x_prompt, x_sample, meta):
    out = []
    for s, x in enumerate((x_prompt, x_sample)):
        for a, b, src, off in ((STARTS[s], STARTS[s] + N_META, meta, STARTS[s]),
                               (STARTS[s] + N_META, STARTS[s] + LENS[s], x, STARTS[s] + N_META)):
            lo, hi = max(a, t0), min(b, t0 + n)
            if lo < hi:
                out.append((lo - t0, src[lo - off:hi - off, :]))
    return out


VB = [(s + q, min(P, n - q)) for s, n in zip(STARTS, LENS) for q in range(0, n, P)]


VBI = {t0: i for i, (t0, _) in enumerate(VB)}


PROJ = [("hy", i) for i in range(6)] + [("q", 0), ("q", 1), ("kv", 0)] + [("gate", i) for i in range(8)]
PROJ_TILES = [(c, kind, i, sub) for c, (kind, i) in enumerate(PROJ) for sub in range(2)]
MLP_AFTER = {2: 0, 5: 1, 8: 2}
FIRST_GATE = PROJ_TILES.index((9, "gate", 0, 0))
HEADS = [(j, kv) for j in range(GROUP) for kv in range(N_KV)]


def key_tiles(b):
    nk = BLOCKS[b][3]
    return [(c, min(P, nk - c)) for c in range(0, nk, P)]


TURNED = [(b, kv, ci) for b in range(len(BLOCKS)) for kv in range(N_KV) for ci in range(len(key_tiles(b)))]


def stage_mix(g):
    nc, io, S = g.nc, g.io, g.sem
    top = g.sb.at
    sb = g.sb
    nhi = sb("normed_hi", [P, KT, T], F32R)
    nlo = sb("normed_lo", [P, KT, T], F32R)
    raw = [sb("w_raw", [P, KT, WCH]) for _ in range(3)]
    whi = [sb("w_hi", [P, KT, WCH], F32R) for _ in range(2)]
    wlo = [sb("w_lo", [P, KT, WCH], F32R) for _ in range(2)]
    rows = sb("conv_rows", [3 * HY_TILES + HY_TILES + 2 * CT, P])
    ss = sb("square_sums", [P, 2 * len(TOK_TILES)])
    cosT = sb("rope_cos", [P, 2, HALF])
    sinT = sb("rope_sin", [P, 2, HALF])
    sg = [sb("gate_sig", [P, 2, HALF]) for _ in range(2)]
    small = [sb("softmax_cols", [P, 6, N_HEADS]) for _ in range(2)]
    sinks = sb("sinks", [P, N_HEADS])
    H = FILT_HIDDEN
    w1, w2, w3 = sb("filt_w1", [FILT_EMB, H]), sb("filt_w2", [H, H]), sb("filt_w3", [H, H])
    col = sb("filt_cols", [H, 4])
    here = sb.at
    gain = sb("mix_gain", [P, D])
    h = [sb("tokens", [P, D]) for _ in range(2)]
    n = [sb("normed", [P, D]) for _ in range(2)]
    junk = sb("squares", [P, D])
    end = sb.at
    sb.at = here
    s = [sb("scores", [P, N_HEADS, 3 * P]) for _ in range(2)]
    here = sb.at = max(end, sb.at)
    upad = [sb("u_padded", [P, T + 3]) for _ in range(2)]
    uc = [sb("u_conv", [P, T + 1]) for _ in range(2)]
    part = sb("conv_part", [P, T + 1])
    end = sb.at
    sb.at = here
    pt = [sb("probs_turned", [P, GROUP, P]) for _ in range(3)]
    band = sb("band", [P, 3 * P])
    o = [sb("attn_out", [P, GROUP, P]) for _ in range(2)]
    here = sb.at = max(end, sb.at)
    fa, fx, fk, fy = [sb(f"filt_{x}", [H, T]) for x in ("in", "x", "k", "y")]
    end = sb.at
    sb.at = here
    qr = [sb("q_plain", [P, 2, HALF]) for _ in range(2)]
    qs = [sb("q_swapped", [P, 2, HALF]) for _ in range(2)]
    ident, qk, v, taps = g.ident, g.qk, g.v, g.taps
    tp = [g.ps[0], g.ps[1], g.ps[2], g.ps[3]]
    acc = [g.ps[4], g.ps[5]]
    sc = [g.ps[0], g.ps[1]]
    tr = [g.ps[2], g.ps[3], g.ps[6]]
    ob = g.ps[7]

    (tok_in, tok_in2, const_in, rows_in, w_in0, w_in1, w_in2, squared, meaned, rooted, normed, n_turned, hi_out, lo_out,
     w_hi, w_lo, prod, taken, conv_out, uc_store0, uc_store1, sig_store0, sig_store1, rope_own,
     rope_sin_done, roped, v_own, pads, taps_turned, taps_out, rope_tab) = S(
        "tok_in_even tok_in_odd const_in rows_in w_in0 w_in1 w_in2 squared meaned rooted normed n_turned hi_out lo_out "
        "w_hi w_lo prod taken conv_out uc_store0 uc_store1 sig_store0 sig_store1 rope_own "
        "rope_sin_done roped norm_own pads taps_turned taps_out rope_tab")
    filt_in, filt_mm, filt_own, filt_sine = S("filt_in filt_mm filt_own filt_sine")
    at_in, scored, masked, prep, exped, divided, turned, copied, pv, o_out, store0, store1, at_own = S(
        "at_in at_scored at_masked at_prep at_exped at_divided at_turned at_copied at_pv at_out at_store0 at_store1 at_own")
    w_in = [w_in0, w_in1, w_in2]
    store = [store0, store1]
    uc_store, sig_store = [uc_store0, uc_store1], [sig_store0, sig_store1]
    ntok, nb = len(TOK_TILES), len(BLOCKS)
    nchunk = len(PROJ)
    w = io["w_in"][0].rearrange("(t p) c -> p t c", p=P)
    tok_ins = [tok_in, tok_in2]
    pieces = [token_pieces(t0, m, io["x_prompt"][0], io["x_sample"][0], io["meta_tokens"]) for t0, m in TOK_TILES]
    tok_total = [[0, 0]]
    for i, ps_ in enumerate(pieces):
        now = list(tok_total[-1])
        now[i % 2] += 16 * len(ps_)
        tok_total.append(now)
    c1 = float(np.float32(6.28125))
    c2 = float(halves12(np.array([TWO_PI - c1], np.float32))[0, 0])
    c3 = float(np.float32(TWO_PI - c1 - c2))
    pi = float(np.nextafter(np.float32(math.pi), np.float32(0)))

    def turn_tile(b):
        return b[:, :].rearrange("p (a c) -> p a c", a=4)

    with nc.Block() as block:
        @block.sync
        def _(sp):
            def load_tokens(i):
                if i >= 2:
                    sp.wait_ge(normed, i - 1)
                for r0, src in pieces[i]:
                    sp.dma_start(h[i % 2][r0:r0 + src.shape[0], :], src).then_inc(tok_ins[i % 2], 16)

            def load_w(c):
                kind, i = PROJ[c]
                dst = raw[c % 3]
                if c >= 3:
                    sp.wait_ge(w_hi, c - 2)
                    sp.wait_ge(w_lo, c - 2)
                if kind == "q":
                    for j in range(2):
                        for kv in range(2):
                            c0 = (2 * i + j + kv * GROUP) * HEAD_DIM
                            at = j * P + kv * HEAD_DIM
                            sp.dma_start(dst[:, :, at:at + HEAD_DIM], w[:, :, c0:c0 + HEAD_DIM]).then_inc(w_in[c % 3], 16)
                    return
                c0 = {"hy": C_HY, "kv": C_K, "gate": C_GATE}[kind] + i * WCH
                for j in range(4):
                    sp.dma_start(dst[:, 2 * j:2 * j + 2, :], w[:, 2 * j:2 * j + 2, c0:c0 + WCH]).then_inc(w_in[c % 3], 16)

            load_tokens(0)
            sp.dma_start(gain[:, :], io["norm_mix_g"][0].partition_broadcast(P)).then_inc(const_in, 16)
            sp.dma_start(ident[:, :], io["ident"]).then_inc(const_in, 16)
            load_tokens(1)
            load_w(0)
            r = io["hy_conv_w"][0].rearrange("k (m p) -> (k m) p", p=P)
            sp.dma_start(rows[0:36, :], r).then_inc(rows_in, 16)
            sp.dma_start(rows[36:48, :], io["hy_conv_b"][0].rearrange("(m p) -> m p", p=P)).then_inc(rows_in, 16)
            sp.dma_start(rows[48:56, :], io["hy_skip"][0].rearrange("o (m p) -> (o m) p", p=P)).then_inc(rows_in, 16)
            load_w(1)
            for i in range(2, ntok):
                load_tokens(i)
            load_w(2)
            sp.dma_start(fa[0:FILT_EMB, :], io["filt_z"]).then_inc(filt_in, 16)
            for t, name in ((w1, "w1"), (w2, "w2"), (w3, "w3")):
                sp.dma_start(t[:, :], io[f"hy_filt_{name}"][0]).then_inc(filt_in, 16)
            for j, name in enumerate(("b1", "b2", "b3", "freq")):
                sp.dma_start(col[:, j:j + 1], io[f"hy_filt_{name}"][0].rearrange("(p a) -> p a", a=1)).then_inc(filt_in, 16)
            sp.dma_start(cosT[:, :, :], io["rope_cos"].rearrange("p (a c) -> p a c", a=2)).then_inc(rope_tab, 16)
            sp.dma_start(sinT[:, :, :], io["rope_sin"].rearrange("p (a c) -> p a c", a=2)).then_inc(rope_tab, 16)
            sp.dma_start(sinks[:, :], io["attn_sink"][0].partition_broadcast(P)).then_inc(at_in, 16)
            hy = gt = 0
            for a, (c, kind, i, sub) in enumerate(PROJ_TILES):
                if sub == 0 and c + 3 < nchunk:
                    load_w(c + 3)
                if kind == "hy":
                    sp.wait_ge(conv_out, 3 * (hy + 1))
                    sp.dma_start(g.hyS[hy * P:(hy + 1) * P, :], uc[hy % 2][:, :]).then_inc(uc_store[hy % 2], 16)
                    hy += 1
                    if hy == HY_TILES:
                        for k in range(2):
                            sp.wait_ge(uc_store[k], 16 * (HY_TILES // 2))
                        sp.dma_start(band[:, :], io["band"]).then_inc(at_in, 16)
                if kind == "gate":
                    sp.wait_ge(taken, 2 * a + 2)
                    sp.dma_start(g.sigS[gt * P:(gt + 1) * P, :].rearrange("p (a c) -> p a c", a=2), sg[gt % 2][:, :, :])\
                      .then_inc(sig_store[gt % 2], 16)
                    gt += 1
                    if sub == 1:
                        q0, lq = BLOCKS[i][0:2]
                        sp.wait_ge(o_out, i + 1)
                        sp.dma_start(g.upS[0:ATTN, :].rearrange("(j p) t -> p j t", p=P)[:, :, q0:q0 + lq],
                                     o[i % 2][:, :, 0:lq]).then_inc(store[i % 2], 16)
            for k in range(2):
                sp.wait_ge(sig_store[k], 16 * 8)
                sp.wait_ge(store[k], 16 * (nb // 2))

        @block.tensor
        def _(pe):
            def filter_layer(layer):
                wt = (w1, w2, w3)[layer]
                if layer:
                    pe.wait_ge(filt_sine, layer)
                else:
                    pe.wait_ge(filt_in, 128)
                for b in range(2):
                    last = nc.tensor.matmul(sc[b][0:H, 0:HALF], wt[:, :], fa[0:wt.shape[0], b * HALF:(b + 1) * HALF],
                                            start=True, stop=True)
                last.then_inc(filt_mm, 1)

            def project(a, halves=(0, 1)):
                c, kind, i, sub = PROJ_TILES[a]
                if sub == 0:
                    pe.wait_ge(w_hi, c + 1)
                    pe.wait_ge(w_lo, c + 1)
                hi, lo = whi[c % 2], wlo[c % 2]
                for k in halves:
                    if a >= 1:
                        pe.wait_ge(taken, 2 * a + k - 1)
                    if kind == "kv" and sub == 1:
                        for j in range(4 * k, 4 * k + 4):
                            t0, m = VB[j]
                            for kt in range(KT):
                                last = three_passes(nc, acc[k][0:m, (j % 4) * P:(j % 4 + 1) * P], nhi[:, kt, t0:t0 + m],
                                                    nlo[:, kt, t0:t0 + m], hi[:, kt, P:2 * P], lo[:, kt, P:2 * P],
                                                    kt == 0, kt == KT - 1)
                    else:
                        for kt in range(KT):
                            last = three_passes(nc, acc[k][:, 0:HALF], hi[:, kt, sub * P:(sub + 1) * P],
                                                lo[:, kt, sub * P:(sub + 1) * P], nhi[:, kt, k * HALF:(k + 1) * HALF],
                                                nlo[:, kt, k * HALF:(k + 1) * HALF], kt == 0, kt == KT - 1)
                    last.then_inc(prod, 1)

            def scores(b):
                q0, lq, k0, nk, m0 = BLOCKS[b]
                for i, (j, kv) in enumerate(HEADS):
                    u = b * N_HEADS + i
                    if u >= 2:
                        pe.wait_ge(masked, u - 1)
                    r = slice(kv * HEAD_DIM, (kv + 1) * HEAD_DIM)
                    nc.tensor.matmul(sc[kv][0:lq, 0:nk], qk[r, j, q0:q0 + lq], qk[r, GROUP, k0:k0 + nk],
                                     start=True, stop=True).then_inc(scored, 1)

            def turn_probs(b, kv):
                q0, lq, k0, nk, m0 = BLOCKS[b]
                for ci, (c, m) in enumerate(key_tiles(b)):
                    u = TURNED.index((b, kv, ci))
                    if u >= 3:
                        pe.wait_ge(copied, u - 2)
                    for j in range(GROUP):
                        last = nc.tensor.transpose(tr[u % 3][0:m, j * P:j * P + lq],
                                                   s[b % 2][0:lq, kv * GROUP + j, c:c + m], ident[0:lq, 0:lq])
                    last.then_inc(turned, 1)

            def weigh(b, kv):
                q0, lq, k0, nk, m0 = BLOCKS[b]
                cts = key_tiles(b)
                if kv == 0 and b >= 1:
                    pe.wait_ge(o_out, b)
                for ci, (c, m) in enumerate(cts):
                    u = TURNED.index((b, kv, ci))
                    pe.wait_ge(copied, u + 1)
                    last = nc.tensor.matmul(ob[kv * HEAD_DIM:(kv + 1) * HEAD_DIM, :]
                                            .rearrange("p (j q) -> p j q", j=GROUP)[:, :, 0:lq],
                                            v[0:m, VBI[k0 + c], kv * HEAD_DIM:(kv + 1) * HEAD_DIM],
                                            pt[u % 3][0:m, :, 0:lq], start=(ci == 0), stop=(ci == len(cts) - 1))
                last.then_inc(pv, 1)

            EARLY = len(TOK_TILES) - 3
            pe.wait_ge(const_in, 32)
            for i, (t0, m) in enumerate(TOK_TILES):
                pe.wait_ge(normed, i + 1)
                for b in range(2):
                    u = 2 * i + b
                    if u >= 4:
                        pe.wait_ge(lo_out, u - 3)
                    for k in range(4):
                        kt = 4 * b + k
                        last = nc.tensor.transpose(tp[u % 4][:, k * P:k * P + m], n[i % 2][0:m, kt * P:(kt + 1) * P],
                                                   ident[0:m, 0:m])
                    last.then_inc(n_turned, 1)
                if i == EARLY:
                    pe.wait_ge(lo_out, 2 * -(-HALF // P))
                    project(0, (0,))
            pe.wait_ge(rows_in, 48)
            pe.wait_ge(lo_out, 2 * ntok - 3)
            nc.tensor.transpose(tp[2 * ntok % 4][:, 0:rows.shape[0]], rows[:, :], ident[0:rows.shape[0], 0:rows.shape[0]])\
              .then_inc(taps_turned, 1)
            pe.wait_ge(lo_out, 2 * ntok)
            for a in range(FIRST_GATE):
                project(a, (1,) if a == 0 else (0, 1))
                if a in MLP_AFTER:
                    filter_layer(MLP_AFTER[a])
            pe.wait_ge(roped, GROUP + 1)
            pe.wait_ge(filt_own, 24)
            scores(0)
            for i in range(nb):
                project(FIRST_GATE + 2 * i)
                if i + 1 < nb:
                    scores(i + 1)
                project(FIRST_GATE + 2 * i + 1)
                pe.wait_ge(divided, i + 1)
                turn_probs(i, 0)
                weigh(i, 0)
                turn_probs(i, 1)
                weigh(i, 1)

        @block.scalar
        def _(act):
            def take_hi(c):
                act.wait_ge(w_in[c % 3], 64 * (c // 3 + 1))
                if c >= 2:
                    act.wait_ge(prod, 4 * (c - 1))
                act.activation(whi[c % 2][:, :, :], raw[c % 3][:, :, :], ACT.Copy).then_inc(w_hi, 1)

            def turn_out(i):
                t0, m = TOK_TILES[i]
                for b in range(2):
                    act.wait_ge(n_turned, 2 * i + b + 1)
                    act.activation(nhi[:, 4 * b:4 * b + 4, t0:t0 + m], turn_tile(tp[(2 * i + b) % 4])[:, :, 0:m], ACT.Copy)\
                       .then_inc(hi_out, 1)

            def sine(layer):
                act.wait_ge(filt_own, 8 * (layer + 1))
                act.activation((fa if layer < 2 else g.feat)[:, :], fx[:, :], ACT.Sin).then_inc(filt_sine, 1)

            def take(a):
                c, kind, i, sub = PROJ_TILES[a]
                if sub == 0 and 1 <= c and c + 1 < nchunk:
                    take_hi(c + 1)
                if kind == "hy" and a >= 2:
                    act.wait_ge(conv_out, 3 * (a - 1))
                gt = a - FIRST_GATE
                if kind == "gate" and gt >= 2:
                    act.wait_ge(sig_store[gt % 2], 16 * (gt // 2))
                rp = a - HY_TILES
                if (kind == "q" or (kind == "kv" and sub == 0)) and rp >= 2:
                    act.wait_ge(roped, rp - 1)
                for k in range(2):
                    act.wait_ge(prod, 2 * a + k + 1)
                    b = acc[k]
                    if kind == "hy":
                        u = upad[a % 2]
                        if k == 0:
                            last = act.activation(u[:, 1:1 + HALF], b[:, 0:HALF], ACT.Copy)
                        else:
                            act.activation(u[:, 1 + HALF:1 + LENS[0]], b[:, 0:LENS[0] - HALF], ACT.Copy)
                            last = act.activation(u[:, 2 + LENS[0]:2 + T], b[:, LENS[0] - HALF:HALF], ACT.Copy)
                    elif kind == "gate":
                        last = act.activation(sg[gt % 2][:, k, :], b[:, 0:HALF], ACT.Sigmoid)
                    elif kind == "kv" and sub == 1:
                        for j in range(4 * k, 4 * k + 4):
                            m = VB[j][1]
                            last = act.activation(v[0:m, j, :], b[0:m, (j % 4) * P:(j % 4 + 1) * P], ACT.Copy)
                    else:
                        act.activation(qr[rp % 2][:, k, :], b[:, 0:HALF], ACT.Copy)
                        for x in range(4):
                            last = act.activation(qs[rp % 2][32 * x:32 * x + 32, k, :],
                                                  b[32 * (x ^ 1):32 * (x ^ 1) + 32, 0:HALF], ACT.Copy)
                    last.then_inc(taken, 1)

            def exps(b):
                lq, nk = BLOCKS[b][1], BLOCKS[b][3]
                act.wait_ge(prep, b + 1)
                k = small[b % 2]
                for hd in range(N_HEADS):
                    act.activation(s[b % 2][0:lq, hd, 0:nk], s[b % 2][0:lq, hd, 0:nk], ACT.Exp, bias=k[0:lq, 2, hd:hd + 1],
                                   scale=HEAD_DIM ** -0.5, accum_out=k[0:lq, 4, hd:hd + 1])
                act.activation(k[0:lq, 3, :], k[0:lq, 3, :], ACT.Exp).then_inc(exped, 1)

            def copies(b):
                lq = BLOCKS[b][1]
                for kv in range(N_KV):
                    for ci, (c, m) in enumerate(key_tiles(b)):
                        u = TURNED.index((b, kv, ci))
                        act.wait_ge(turned, u + 1)
                        if u >= 3 and kv == 0:
                            act.wait_ge(pv, 2 * b)
                        if kv == 1:
                            act.wait_ge(pv, 2 * b + 1)
                        act.activation(pt[u % 3][0:m, :, 0:lq], tr[u % 3][0:m, :].rearrange("p (j q) -> p j q", j=GROUP)[:, :, 0:lq],
                                       ACT.Copy).then_inc(copied, 1)

            act.wait_ge(pads, 2)
            for i, (t0, m) in enumerate(TOK_TILES):
                act.wait_ge(tok_ins[i % 2], tok_total[i + 1][i % 2])
                act.activation(junk[0:m, :], h[i % 2][0:m, :], ACT.Square, accum_out=ss[0:m, i:i + 1]).then_inc(squared, 1)
                act.wait_ge(meaned, i + 1)
                act.activation(ss[0:m, ntok + i:ntok + i + 1], ss[0:m, i:i + 1], ACT.Sqrt).then_inc(rooted, 1)
                if i == 1:
                    take_hi(0)
                if i == 3:
                    take_hi(1)
                if i >= 1:
                    turn_out(i - 1)
            turn_out(ntok - 1)
            for a in range(FIRST_GATE):
                if a == HY_TILES:
                    act.wait_ge(filt_own, 24)
                take(a)
                if a in MLP_AFTER:
                    sine(MLP_AFTER[a])
            for i in range(nb):
                exps(i)
                take(FIRST_GATE + 2 * i)
                take(FIRST_GATE + 2 * i + 1)
                copies(i)

        @block.vector
        def _(dve):
            link = linked(dve, v_own)

            def take_lo(i):
                t0, m = TOK_TILES[i]
                for b in range(2):
                    dve.wait_ge(hi_out, 2 * i + b + 1)
                    nc.vector.tensor_tensor(nlo[:, 4 * b:4 * b + 4, t0:t0 + m], turn_tile(tp[(2 * i + b) % 4])[:, :, 0:m],
                                            nhi[:, 4 * b:4 * b + 4, t0:t0 + m].bitcast(F32), ALU.subtract).then_inc(lo_out, 1)

            def convolve(m):
                dve.wait_ge(taken, 2 * m + 2)
                u, y = upad[m % 2], uc[m % 2]
                tap = [taps[:, k * HY_TILES + m:k * HY_TILES + m + 1] for k in range(4)]
                if m >= 2:
                    dve.wait_ge(uc_store[m % 2], 16 * (m // 2))
                nc.vector.tensor_scalar(y[:, :], u[:, 0:T + 1], tap[0], tap[3], ALU.mult, ALU.add).then_inc(conv_out, 1)
                dve.wait_ge(conv_out, 3 * m + 1)
                nc.vector.scalar_tensor_tensor(part[:, :], u[:, 1:T + 2], tap[1], y[:, :], ALU.mult, ALU.add).then_inc(conv_out, 1)
                dve.wait_ge(conv_out, 3 * m + 2)
                nc.vector.scalar_tensor_tensor(y[:, :], u[:, 2:T + 3], tap[2], part[:, :], ALU.mult, ALU.add).then_inc(conv_out, 1)

            def rotate(rp):
                dve.wait_ge(taken, 2 * (HY_TILES + rp) + 2)
                nc.vector.tensor_tensor(qr[rp % 2][:, :, :], qr[rp % 2][:, :, :], cosT[:, :, :], ALU.mult).then_inc(rope_own, 1)
                dve.wait_ge(rope_own, rp + 1)
                dve.wait_ge(rope_sin_done, rp + 1)
                nc.vector.tensor_tensor(qk[:, rp, :].rearrange("p (a c) -> p a c", a=2), qr[rp % 2][:, :, :],
                                        qs[rp % 2][:, :, :], ALU.add).then_inc(roped, 1)

            flink = linked(dve, filt_own)

            def sine_argument(layer):
                dve.wait_ge(filt_mm, layer + 1)
                for b in range(2):
                    flink(nc.vector.tensor_scalar(fx[:, b * HALF:(b + 1) * HALF], sc[b][0:H, 0:HALF], col[:, layer:layer + 1],
                                                  col[:, 3:4], ALU.add, ALU.mult))
                flink(nc.vector.tensor_scalar(fk[:, :], fx[:, :], 1.0 / TWO_PI, MAGIC, ALU.mult, ALU.add))
                flink(nc.vector.tensor_scalar(fk[:, :], fk[:, :], MAGIC, None, ALU.subtract))
                flink(nc.vector.scalar_tensor_tensor(fy[:, :], fk[:, :], -c1, fx[:, :], ALU.mult, ALU.add))
                flink(nc.vector.scalar_tensor_tensor(fx[:, :], fk[:, :], -c2, fy[:, :], ALU.mult, ALU.add))
                flink(nc.vector.scalar_tensor_tensor(fy[:, :], fk[:, :], -c3, fx[:, :], ALU.mult, ALU.add))
                flink(nc.vector.tensor_scalar(fx[:, :], fy[:, :], pi, -pi, ALU.min, ALU.max))

            alink = linked(dve, at_own)

            def mask(b):
                q0, lq, k0, nk, m0 = BLOCKS[b]
                if b >= 2:
                    dve.wait_ge(pv, 2 * (b - 1))
                for i, (j, kv) in enumerate(HEADS):
                    dve.wait_ge(scored, b * N_HEADS + i + 1)
                    hd = kv * GROUP + j
                    nc.vector.tensor_tensor_reduce(s[b % 2][0:lq, hd, 0:nk], sc[kv][0:lq, 0:nk], band[0:lq, m0:m0 + nk],
                                                   1.0, NEG, ALU.add, ALU.max, small[b % 2][0:lq, 0, hd:hd + 1]).then_inc(masked, 1)
                dve.wait_ge(masked, N_HEADS * (b + 1))
                k = small[b % 2]
                alink(nc.vector.scalar_tensor_tensor(k[0:lq, 1, :], k[0:lq, 0, :], HEAD_DIM ** -0.5, sinks[0:lq, :], ALU.mult, ALU.max))
                alink(nc.vector.tensor_scalar(k[0:lq, 2, :], k[0:lq, 1, :], -1.0, None, ALU.mult))
                nc.vector.tensor_tensor(k[0:lq, 3, :], sinks[0:lq, :], k[0:lq, 1, :], ALU.subtract).then_inc(prep, 1)

            def divide(b):
                q0, lq, k0, nk, m0 = BLOCKS[b]
                k = small[b % 2]
                dve.wait_ge(exped, b + 1)
                alink(nc.vector.tensor_tensor(k[0:lq, 1, :], k[0:lq, 4, :], k[0:lq, 3, :], ALU.add))
                alink(nc.vector.reciprocal(k[0:lq, 5, :], k[0:lq, 1, :]))
                for hd in range(N_HEADS):
                    last = nc.vector.tensor_scalar(s[b % 2][0:lq, hd, 0:nk], s[b % 2][0:lq, hd, 0:nk], k[0:lq, 5, hd:hd + 1],
                                                   None, ALU.mult)
                last.then_inc(divided, 1)

            def attention_out(b):
                lq = BLOCKS[b][1]
                dve.wait_ge(pv, 2 * b + 2)
                if b >= 2:
                    dve.wait_ge(store[b % 2], 16 * (b // 2))
                nc.vector.tensor_copy(o[b % 2][:, :, 0:lq], ob[:, :].rearrange("p (j q) -> p j q", j=GROUP)[:, :, 0:lq])\
                  .then_inc(o_out, 1)

            for k in range(2):
                nc.vector.memset(upad[k][:, :], 0.0).then_inc(pads, 1)
            dve.wait_ge(const_in, 32)
            for i, (t0, m) in enumerate(TOK_TILES):
                dve.wait_ge(squared, i + 1)
                nc.vector.tensor_scalar(ss[0:m, i:i + 1], ss[0:m, i:i + 1], 1.0 / D, EPS, ALU.mult, ALU.add).then_inc(meaned, 1)
                dve.wait_ge(rooted, i + 1)
                link(nc.vector.reciprocal(ss[0:m, i:i + 1], ss[0:m, ntok + i:ntok + i + 1]))
                if i >= 2:
                    dve.wait_ge(n_turned, 2 * (i - 1))
                nc.vector.scalar_tensor_tensor(n[i % 2][0:m, :], h[i % 2][0:m, :], ss[0:m, i:i + 1], gain[0:m, :],
                                               ALU.mult, ALU.mult).then_inc(normed, 1)
                if i >= 1:
                    take_lo(i - 1)
            take_lo(ntok - 1)
            dve.wait_ge(taps_turned, 1)
            nc.vector.tensor_copy(taps[:, :], tp[2 * ntok % 4][:, 0:taps.shape[1]]).then_inc(taps_out, 1)
            dve.wait_ge(taps_out, 1)
            dve.wait_ge(filt_in, 128)
            for m in range(HY_TILES):
                convolve(m)
                if m in MLP_AFTER:
                    sine_argument(MLP_AFTER[m])
            dve.wait_ge(rope_tab, 32)
            for rp in range(GROUP + 1):
                rotate(rp)
            dve.wait_ge(at_in, 32)
            mask(0)
            for i in range(nb):
                divide(i)
                if i + 1 < nb:
                    mask(i + 1)
                attention_out(i)

        @block.gpsimd
        def _(pool):
            def take_lo(c):
                pool.wait_ge(w_hi, c + 1)
                nc.gpsimd.tensor_tensor(wlo[c % 2][:, :, :], raw[c % 3][:, :, :], whi[c % 2][:, :, :].bitcast(F32),
                                        ALU.subtract).then_inc(w_lo, 1)
            take_lo(0)
            take_lo(1)
            pool.wait_ge(rope_tab, 32)
            for a, (c, kind, i, sub) in enumerate(PROJ_TILES):
                if sub == 0 and 1 <= c and c + 1 < nchunk:
                    take_lo(c + 1)
                if kind == "q" or (kind == "kv" and sub == 0):
                    rp = a - HY_TILES
                    pool.wait_ge(taken, 2 * a + 2)
                    nc.gpsimd.tensor_tensor(qs[rp % 2][:, :, :], qs[rp % 2][:, :, :], sinT[:, :, :], ALU.mult)\
                      .then_inc(rope_sin_done, 1)
    g.sb.at = top




CUTS = (((0, 264), (264, 264)), ((0, 272),))
KF_FILLS = (((0, 0, 2), (1, 0, 2), (2, 2, 1)), ((0, 0, 2), (1, 0, 2)))


def hyena_steps():
    units = [(s, j) for s in (1, 0) for j in range(CT)]
    turns = [(a + b, o) for a in range(0, len(units), 2) for o in range(2) for b in range(2)]
    spectra = {-2: (0, 0), -1: (0, 1)}
    for i in range(len(turns)):
        spectra[i] = divmod(i + 2, 2)

    def taps_steps(u):
        parts = [(u, t, min(2, NT[units[u][0]] - t)) for t in range(0, NT[units[u][0]], 2)]
        return [[("hgen",) + parts[0]]] + [[("hsplit",) + a, ("hgen",) + b] for a, b in zip(parts, parts[1:])] + [[("hsplit",) + parts[-1]]]

    def spectrum_steps(u, o):
        return [("kf", u, o, q) for q in range(len(KF_FILLS[units[u][0]]))]
    steps = sum(taps_steps(0), []) + [("zt",) + turns[0]] + spectrum_steps(0, 0) + spectrum_steps(0, 1)
    taps = taps_steps(1)
    for i, turn in enumerate(turns):
        taps += [[]] * (4 - len(taps))
        steps += taps[0] + [("fwd",) + turn] + taps[1]
        if i:
            steps.append(("inv",) + turns[i - 1])
        steps += taps[2] + [("yt",) + turn] + taps[3]
        u, o = spectra[i]
        fills = spectrum_steps(u, o) if u < len(units) else []
        if i + 1 < len(turns):
            steps.append(("zt",) + turns[i + 1])
        steps += fills
        taps = taps_steps(u + 1) if o == 1 and u + 1 < len(units) else []
    steps.append(("inv",) + turns[-1])
    return units, steps


def stage_hyena(g):
    nc, io, S = g.nc, g.io, g.sem
    top = g.sb.at
    sb = g.sb
    ahead = [[sb(f"ahead{s}_{x}", [P, NT[s], W[s]], F32R) for x in ("hi", "lo")] for s in range(2)]
    back = [[sb(f"back{s}_{x}", [P, NK[s], LENS[s]], F32R) for x in ("hi", "lo")] for s in range(2)]
    decay = [sb("decay", [P, NT[0], P]) for _ in range(2)]
    wout = [sb("filt_wout", [FILT_HIDDEN, 4, P]) for _ in range(2)]
    taps = [sb("filter_taps", [P, 4, P]) for _ in range(2)]
    pair = [sb("taps_sum_diff", [P, 2, 2, P]) for _ in range(2)]
    hs = [sb(f"taps_{x}", [P, NT[0], 2, 2, P], F32R) for x in ("hi", "lo")]
    kf = [sb("spectrum", [P, 2, W[0]]) for _ in range(2)]
    src = [sb("v_x1_x2", [P, 3, LENS[0]]) for _ in range(3)]
    z = [sb("z", [P, LENS[0]]) for _ in range(2)]
    zt = [sb(f"z_turned_{x}", [P, NT[0], P], F32R) for x in ("hi", "lo")]
    prodA = [sb("zk_real", [P, 2, FG[0]]) for _ in range(2)]
    prodB = [sb("zk_imag", [P, 2, FG[0]]) for _ in range(2)]
    y = sb("y_spectrum", [P, W[0]])
    yt = [sb(f"y_turned_{x}", [P, NK[0], P], F32R) for x in ("hi", "lo")]
    ident = g.ident
    (ca1, hg, h_decayed, h_sum, h_hi, h_lo, kmm, k_out, v_in0, v_in1, v_in2, dec_in0, dec_in1, ztm, zt_hi, zt_lo, fmm, f_mul, y_out,
     ytm, yt_hi, yt_lo, imm_, gated, st0, st1) = S(
        "hy_ahead1 hy_taps_mm hy_decayed hy_sum_diff hy_taps_hi hy_taps_lo hy_spec_mm hy_spec_out hy_v_in0 hy_v_in1 hy_v_in2 hy_dec_in0 "
        "hy_dec_in1 hy_zt_mm hy_zt_hi hy_zt_lo hy_fwd_mm hy_fwd_mul hy_y_out hy_yt_mm hy_yt_hi hy_yt_lo hy_inv_mm hy_gated "
        "hy_store0 hy_store1")
    cb1, ca0, cb0 = S("hy_back1 hy_ahead0 hy_back0")
    ahead_in = [ca0, ca1]
    back_in = [cb0, cb1]
    v_in, dec_in, store = [v_in0, v_in1, v_in2], [dec_in0, dec_in1], [st0, st1]
    units, steps = hyena_steps()
    hz, kb, tb, ib = [g.ps[0], g.ps[1]], [g.ps[2], g.ps[3]], [g.ps[4], g.ps[5]], [g.ps[6], g.ps[7]]
    pos, nl, nh, nk, nhz, nf, nyt, nkf, nzt = {}, 0, 0, 0, 0, 0, 0, 0, 0
    for st in steps:
        s = units[st[1]][0]
        pos[st] = dict(h=nh, l=nl, k=nk, hz=nhz, f=nf, yt=nyt, kf=nkf, zt=nzt)
        if st[0] == "hgen":
            nh += st[3]
            nhz += st[3]
        elif st[0] == "hsplit":
            nl += st[3]
        elif st[0] == "kf":
            nk += 1
            nkf += 1
        elif st[0] == "fwd":
            nk += GROUPS[s]
            nf += GROUPS[s]
        elif st[0] == "zt":
            nhz += -(-NT[s] // 4)
            nzt += -(-NT[s] // 4)
        elif st[0] == "yt":
            nyt += -(-NK[s] // 4)
    kuse, hzuse = [], []
    for st in steps:
        s = units[st[1]][0]
        if st[0] in ("kf", "fwd"):
            for q in range(1 if st[0] == "kf" else GROUPS[s]):
                kuse.append((k_out, 1 + sum(1 for a, _ in kuse if a is k_out)) if st[0] == "kf"
                            else (f_mul, 1 + sum(1 for a, _ in kuse if a is f_mul)))
        if st[0] == "hgen":
            hzuse += [(h_decayed, pos[st]["h"] + q + 1) for q in range(st[3])]
        if st[0] == "zt":
            hzuse += [(zt_lo, pos[st]["zt"] + q + 1) for q in range(-(-NT[s] // 4))]

    def tsize(s, t):
        return min(P, LENS[s] - t * P)

    def ksize(s, k):
        return min(P, W[s] - k * P)

    def taps_until(u):
        return sum(NT[units[x][0]] for x in range(u + 1))

    def fills_until(u, o):
        return sum(len(KF_FILLS[units[x][0]]) * (2 if x < u else o + 1) for x in range(u + 1))

    def cuts_before(st):
        return sum(len(CUTS[units[x[1]][0]]) for x in steps[:steps.index(st)] if x[0] == "inv")

    def order(st):
        return sum(1 for x in steps[:steps.index(st)] if x[0] == st[0])

    with nc.Block() as block:
        @block.gpsimd
        def _(pool):
            def table_load(s, inverse, x):
                tab, dst, sem, rows = ((f"ahead{s}", ahead[s], ahead_in[s], LENS[s]), (f"back{s}", back[s], back_in[s], W[s]))[inverse]
                full = rows // P
                nc.gpsimd.dma_start(dst[x][:, 0:full, :], io[tab][x, 0:full * P, :].rearrange("(t p) w -> p t w", p=P)).then_inc(sem, 16)
                nc.gpsimd.dma_start(dst[x][0:rows - full * P, full, :], io[tab][x, full * P:rows, :]).then_inc(sem, 16)
            for x in range(2):
                table_load(1, 0, x)
            for st in steps:
                s, j = units[st[1]]
                if st[0] == "hgen":
                    for t in range(st[2], st[2] + st[3]):
                        u, m = pos[st]["h"] + t - st[2], tsize(s, t)
                        pool.wait_ge(h_decayed, u + 1)
                        if u >= 2:
                            pool.wait_ge(h_lo, u - 1)
                        nc.gpsimd.tensor_tensor(pair[u % 2][0:m, 0, :, :], taps[u % 2][0:m, 0:2, :], taps[u % 2][0:m, 2:4, :], ALU.add)
                        nc.gpsimd.tensor_tensor(pair[u % 2][0:m, 1, :, :], taps[u % 2][0:m, 0:2, :], taps[u % 2][0:m, 2:4, :], ALU.subtract)\
                          .then_inc(h_sum, 1)
                    if st[1] == 0 and st[2] + st[3] == NT[s]:
                        for x in range(2):
                            table_load(1, 1, x)
                elif st[0] == "fwd":
                    f = FG[s]
                    for q in range(GROUPS[s]):
                        u = pos[st]["f"] + q
                        pool.wait_ge(f_mul, u + 1)
                        if q == 0:
                            k = order(st)
                            if k:
                                pool.wait_ge(ytm, sum(-(-NK[units[x[1]][0]] // 4) for x in steps if x[0] == "yt" and order(x) < k))
                        A, B = prodA[u % 2], prodB[u % 2]
                        yy = y[:, 2 * f * q:2 * f * (q + 1)].rearrange("p (c f) -> p c f", c=2)
                        nc.gpsimd.tensor_tensor(yy[:, 0, :], A[:, 0, 0:f], B[:, 1, 0:f], ALU.subtract)
                        nc.gpsimd.tensor_tensor(yy[:, 1, :], B[:, 0, 0:f], A[:, 1, 0:f], ALU.add).then_inc(y_out, 1)
                    if order(st) < 4:
                        table_load(0, order(st) // 2, order(st) % 2)

        @block.sync
        def _(sp):
            def unit_in(u):
                s, j = units[u]
                n = LENS[s]
                full = NT[s] - 1
                if u >= 2:
                    sp.wait_ge(hg, taps_until(u - 2))
                    sp.wait_ge(h_decayed, taps_until(u - 2))
                sp.dma_start(wout[u % 2][:, :, :], io["hy_filt_wout"][0].rearrange("k (q c) -> k q c", q=4)[:, :, j * P:(j + 1) * P])\
                  .then_inc(dec_in[u % 2], 16)
                sp.dma_start(decay[u % 2][:, 0:full, :], io[f"decay{s}"][0:full * P, j * P:(j + 1) * P].rearrange("(t p) c -> p t c", p=P))\
                  .then_inc(dec_in[u % 2], 16)
                sp.dma_start(decay[u % 2][0:n - full * P, full, :], io[f"decay{s}"][full * P:n, j * P:(j + 1) * P]).then_inc(dec_in[u % 2], 16)

            def gates_in(u):
                s, j = units[u]
                n = LENS[s]
                if u >= 3:
                    sp.wait_ge(gated, cuts_before(("inv", u - 3, 1)) + len(CUTS[units[u - 3][0]]))
                at = (0, LENS[0] + 1)[s]
                sp.dma_start(src[u % 3][:, :, 0:n], g.hyS.rearrange("(q j p) t -> j p q t", q=3, p=P)[j, :, :, at:at + n]).then_inc(v_in[u % 3], 16)

            unit_in(0)
            gates_in(0)
            unit_in(1)
            gates_in(1)
            gates_in(2)
            for u in range(2, 5):
                unit_in(u)
            for u, (s, j) in enumerate(units):
                if u == len(units) - 1:
                    sp.wait_ge(kmm, nkf)
                    for i in range(3):
                        load_up_weights(sp, g, i)
                    for k in range(GROUP):
                        sp.dma_start(g.up_attn[:, k, :], g.upS[k * P:(k + 1) * P, :]).then_inc(g.up_attn_in, 16)
                sp.wait_ge(gated, cuts_before(("inv", u, 1)) + len(CUTS[s]))
                sp.dma_start(g.upS[ATTN + j * P:ATTN + (j + 1) * P, STARTS[s]:STARTS[s] + LENS[s]], z[u % 2][:, 0:LENS[s]]).then_inc(store[u % 2], 16)
                if u + 3 < len(units):
                    gates_in(u + 3)
                if u + 5 < len(units):
                    unit_in(u + 5)
            sp.wait_ge(store[0], 16 * CT)
            sp.wait_ge(store[1], 16 * CT)

        @block.tensor
        def _(pe):
            for st in steps:
                s, j = units[st[1]]
                p_ = pos[st]
                n, f = LENS[s], FG[s]
                if st[0] == "hgen":
                    pe.wait_ge(dec_in[st[1] % 2], 48 * (st[1] // 2 + 1))
                    for t in range(st[2], st[2] + st[3]):
                        at = p_["hz"] + t - st[2]
                        if at >= 2:
                            pe.wait_ge(*hzuse[at - 2])
                        t0 = STARTS[s] + t * P
                        nc.tensor.matmul(hz[at % 2][0:tsize(s, t), :], g.feat[:, t0:t0 + tsize(s, t)],
                                         wout[st[1] % 2][:, :, :].rearrange("k q c -> k (q c)"), start=True, stop=True).then_inc(hg, 1)
                elif st[0] == "kf":
                    o = st[2]
                    pe.wait_ge(h_lo, taps_until(st[1]))
                    pe.wait_ge(ahead_in[s], 64)
                    for part, g0, ng in (KF_FILLS[s][st[3]],):
                        u = p_["k"]
                        if u >= 2:
                            pe.wait_ge(*kuse[u - 2])
                        for c in ((0, 1) if part == 2 else (part,)):
                            at = c * f if part == 2 else 0
                            for t in range(NT[s]):
                                m = tsize(s, t)
                                tab = [ahead[s][x][0:m, t, :].rearrange("p (g c f) -> p g c f", c=2, f=f)[:, g0:g0 + ng, c, :] for x in range(2)]
                                last = three_passes(nc, kb[u % 2][:, at:at + ng * f], hs[0][0:m, t, c, o, :], hs[1][0:m, t, c, o, :],
                                                    tab[0], tab[1], t == 0, t == NT[s] - 1)
                        last.then_inc(kmm, 1)
                elif st[0] == "zt":
                    o = st[2]
                    if o == 0:
                        pe.wait_ge(v_in[st[1] % 3], 16 * (st[1] // 3 + 1))
                        zz = src[st[1] % 3][:, 0, :]
                    else:
                        zz = z[st[1] % 2]
                    for b in range(-(-NT[s] // 4)):
                        u = p_["hz"] + b
                        if u >= 2:
                            pe.wait_ge(*hzuse[u - 2])
                        for t in range(4 * b, min(4 * b + 4, NT[s])):
                            m = tsize(s, t)
                            if o == 1:
                                pe.wait_ge(gated, cuts_before(("inv", st[1], 0)) + sum(c0 < t * P + m for c0, cn in CUTS[s]))
                            last = nc.tensor.transpose(hz[u % 2][0:m, (t % 4) * P:(t % 4 + 1) * P], zz[:, t * P:t * P + m], ident[:, :])
                        last.then_inc(ztm, 1)
                elif st[0] == "fwd":
                    pe.wait_ge(zt_lo, pos[("zt", st[1], st[2])]["zt"] + -(-NT[s] // 4))
                    for q in range(GROUPS[s]):
                        u = p_["k"] + q
                        if u >= 2:
                            pe.wait_ge(*kuse[u - 2])
                        for t in range(NT[s]):
                            m = tsize(s, t)
                            at = 2 * q * f
                            last = three_passes(nc, kb[u % 2][:, 0:2 * f], zt[0][0:m, t, :], zt[1][0:m, t, :],
                                                ahead[s][0][0:m, t, at:at + 2 * f], ahead[s][1][0:m, t, at:at + 2 * f], t == 0, t == NT[s] - 1)
                        last.then_inc(fmm, 1)
                elif st[0] == "yt":
                    pe.wait_ge(y_out, pos[("fwd", st[1], st[2])]["f"] + GROUPS[s])
                    for b in range(-(-NK[s] // 4)):
                        u = p_["yt"] + b
                        if u >= 2:
                            pe.wait_ge(yt_lo, u - 1)
                        for k in range(4 * b, min(4 * b + 4, NK[s])):
                            m = ksize(s, k)
                            last = nc.tensor.transpose(tb[u % 2][0:m, (k % 4) * P:(k % 4 + 1) * P], y[:, k * P:k * P + m], ident[:, :])
                        last.then_inc(ytm, 1)
                elif st[0] == "inv":
                    pe.wait_ge(back_in[s], 64)
                    if order(st):
                        pe.wait_ge(gated, cuts_before(st))
                    runs = [(b, range(0, 4)) for b in range(len(CUTS[s]))] + [(b, range(4, NK[s])) for b in range(len(CUTS[s]))]
                    for b, ks in runs:
                        c0, cn = CUTS[s][b]
                        for k in ks:
                            pe.wait_ge(yt_lo, pos[("yt", st[1], st[2])]["yt"] + k // 4 + 1)
                            m = ksize(s, k)
                            last = three_passes(nc, ib[b][:, 0:cn], yt[0][0:m, k, :], yt[1][0:m, k, :],
                                                back[s][0][0:m, k, c0:c0 + cn], back[s][1][0:m, k, c0:c0 + cn], k == 0, k == NK[s] - 1)
                        if ks[0]:
                            last.then_inc(imm_, 1)

        def split_turns(eng, st, count, filled, base, dst, size):
            s = units[st[1]][0]
            for b in range(-(-count // 4)):
                bank = hz[(pos[st]["hz"] + b) % 2] if st[0] == "zt" else tb[(pos[st]["yt"] + b) % 2]
                eng.wait_ge(filled, base + b + 1)
                tiles = list(range(4 * b, min(4 * b + 4, count)))
                full = [t for t in tiles if size(s, t) == P]
                parts = ([(full[0], len(full), P)] if full else []) + [(t, 1, size(s, t)) for t in tiles if size(s, t) < P]
                for i, (t, k, m) in enumerate(parts):
                    rows = bank[0:m, :].rearrange("p (k c) -> p k c", k=4)[:, t % 4:t % 4 + k, :]
                    yield b, i == len(parts) - 1, rows, [d[0:m, t:t + k, :] for d in dst]

        @block.scalar
        def _(act):
            for st in steps:
                s, j = units[st[1]]
                f = FG[s]
                if st[0] == "hsplit":
                    for t in range(st[2], st[2] + st[3]):
                        u, m = pos[st]["l"] + t - st[2], tsize(s, t)
                        act.wait_ge(h_sum, u + 1)
                        if t == 0 and st[1]:
                            act.wait_ge(kmm, fills_until(st[1] - 1, 1))
                        act.activation(hs[0][0:m, t, :, :, :], pair[u % 2][0:m, :, :, :], ACT.Copy).then_inc(h_hi, 1)
                elif st[0] == "kf":
                    o = st[2]
                    if st[1] >= 2:
                        act.wait_ge(f_mul, pos[("fwd", st[1] - 2, o)]["f"] + GROUPS[units[st[1] - 2][0]])
                    skip = g.taps[:, 4 * HY_TILES + o * CT + j:4 * HY_TILES + o * CT + j + 1]
                    spec = kf[st[1] % 2][:, o, 0:W[s]].rearrange("p (g c f) -> p g c f", c=2, f=f)
                    for part, g0, ng in (KF_FILLS[s][st[3]],):
                        u = pos[st]["k"]
                        act.wait_ge(kmm, pos[st]["kf"] + 1)
                        for c in ((0, 1) if part == 2 else (part,)):
                            at = c * f if part == 2 else 0
                            bank = kb[u % 2][:, at:at + ng * f].rearrange("p (g f) -> p g f", f=f)
                            if c == 0:
                                ins = act.activation(spec[:, g0:g0 + ng, c, :], bank, ACT.Identity, bias=skip)
                            else:
                                ins = act.activation(spec[:, g0:g0 + ng, c, :], bank, ACT.Copy)
                        ins.then_inc(k_out, 1)
                elif st[0] == "zt":
                    k = order(st)
                    if k:
                        act.wait_ge(fmm, sum(GROUPS[units[x[1]][0]] for x in steps if x[0] == "fwd" and order(x) < k))
                    for b, last, bank, (hi, lo) in split_turns(act, st, NT[s], ztm, pos[st]["zt"], zt, tsize):
                        ins = act.activation(hi, bank, ACT.Copy)
                        if last:
                            ins.then_inc(zt_hi, 1)
                elif st[0] == "yt":
                    k = order(st)
                    if k:
                        act.wait_ge(imm_, cuts_before(("inv",) + st[1:]))
                    for b, last, bank, (hi, lo) in split_turns(act, st, NK[s], ytm, pos[st]["yt"], yt, ksize):
                        ins = act.activation(hi, bank, ACT.Copy)
                        if last:
                            ins.then_inc(yt_hi, 1)

        @block.vector
        def _(dve):
            for st in steps:
                s, j = units[st[1]]
                n, f = LENS[s], FG[s]
                if st[0] == "hgen":
                    dve.wait_ge(dec_in[st[1] % 2], 48 * (st[1] // 2 + 1))
                    for t in range(st[2], st[2] + st[3]):
                        u, m = pos[st]["h"] + t - st[2], tsize(s, t)
                        dve.wait_ge(hg, u + 1)
                        if u >= 2:
                            dve.wait_ge(h_sum, u - 1)
                        nc.vector.tensor_tensor(taps[u % 2][0:m, :, :], hz[(pos[st]["hz"] + t - st[2]) % 2][0:m, :].rearrange("p (q c) -> p q c", q=4),
                                                decay[st[1] % 2][0:m, t, :].unsqueeze(1).broadcast_to([m, 4, P]), ALU.mult).then_inc(h_decayed, 1)
                elif st[0] == "hsplit":
                    for t in range(st[2], st[2] + st[3]):
                        u, m = pos[st]["l"] + t - st[2], tsize(s, t)
                        dve.wait_ge(h_hi, u + 1)
                        nc.vector.tensor_tensor(hs[1][0:m, t, :, :, :], pair[u % 2][0:m, :, :, :], hs[0][0:m, t, :, :, :].bitcast(F32),
                                                ALU.subtract).then_inc(h_lo, 1)
                elif st[0] == "zt":
                    for b, last, bank, (hi, lo) in split_turns(dve, st, NT[s], zt_hi, pos[st]["zt"], zt, tsize):
                        ins = nc.vector.tensor_tensor(lo, bank, hi.bitcast(F32), ALU.subtract)
                        if last:
                            ins.then_inc(zt_lo, 1)
                elif st[0] == "yt":
                    for b, last, bank, (hi, lo) in split_turns(dve, st, NK[s], yt_hi, pos[st]["yt"], yt, ksize):
                        ins = nc.vector.tensor_tensor(lo, bank, hi.bitcast(F32), ALU.subtract)
                        if last:
                            ins.then_inc(yt_lo, 1)
                elif st[0] == "fwd":
                    o = st[2]
                    dve.wait_ge(k_out, fills_until(st[1], o))
                    for q in range(GROUPS[s]):
                        u, b = pos[st]["f"] + q, pos[st]["k"] + q
                        dve.wait_ge(fmm, u + 1)
                        if u >= 2:
                            dve.wait_ge(y_out, u - 1)
                        zf = kb[b % 2][:, 0:2 * f].rearrange("p (c f) -> p c f", c=2)
                        spec = kf[st[1] % 2][:, o, :]
                        for c, dst in enumerate((prodA[u % 2], prodB[u % 2])):
                            at = (2 * q + c) * f
                            last = nc.vector.tensor_tensor(dst[:, :, 0:f], zf, spec[:, at:at + f].unsqueeze(1).broadcast_to([P, 2, f]), ALU.mult)
                        last.then_inc(f_mul, 1)
                elif st[0] == "inv":
                    o, u = st[2], st[1]
                    dst = z[u % 2]
                    if o == 0:
                        if u >= 2:
                            dve.wait_ge(store[u % 2], 16 * (u // 2))
                        dve.wait_ge(v_in[u % 3], 16 * (u // 3 + 1))
                    else:
                        dve.wait_ge(ztm, pos[("zt", u, 1)]["zt"] + -(-NT[s] // 4))
                    for b, (c0, cn) in enumerate(CUTS[s]):
                        dve.wait_ge(imm_, cuts_before(st) + b + 1)
                        nc.vector.tensor_tensor(dst[:, c0:c0 + cn], ib[b][:, 0:cn], src[u % 3][:, 1 + o, c0:c0 + cn], ALU.mult)\
                          .then_inc(gated, 1)
    g.sb.at = top


NCH = D // WCH


def load_up_weights(sp, g, i):
    c0, w = i // 2 * WCH, g.up_w[i % 4]
    if i % 2 == 0:
        rows = g.io["w_attn_up"][0].rearrange("(v j d) n -> v d j n", v=N_KV, d=HEAD_DIM)
        for kv in range(N_KV):
            sp.dma_start(w[kv * HEAD_DIM:(kv + 1) * HEAD_DIM, :, :], rows[kv, :, :, c0:c0 + WCH]).then_inc(g.up_w_in[i % 4], 16)
    else:
        sp.dma_start(w[:, :, :], g.io["w_hyena_up"][0].rearrange("(j p) n -> p j n", p=P)[:, :, c0:c0 + WCH]).then_inc(g.up_w_in[i % 4], 16)


def stage_merge(g):
    nc, io, S = g.nc, g.io, g.sem
    mhi, mlo = g.mhi, g.mlo
    top = g.sb.at
    sb = g.sb
    sb.at = g.up_split_at
    uhi = sb("up_in_hi", [P, KT, T], F32R)
    ulo = sb("up_in_lo", [P, KT, T], F32R)
    sb.at = g.merge_rest_at
    whi = [sb("wu_hi", [P, GROUP, WCH], F32R) for _ in range(2)]
    wlo = [sb("wu_lo", [P, GROUP, WCH], F32R) for _ in range(2)]
    sig = [sb("sig_pair", [P, 2, T]) for _ in range(2)]
    ga = sb("gated_pair", [P, 2, HALF])
    mm_ = sb("merged", [P, HALF])
    (up_in, u_hi, u_lo, wh, wl, sg0, sg1, prod, gd, summed, m_hi, m_lo) = S(
        "mg_up_in mg_u_hi mg_u_lo mg_wh mg_wl mg_sg0 mg_sg1 mg_prod mg_gated mg_sum mg_m_hi mg_m_lo")
    sgs = [sg0, sg1]
    banks = [(g.ps[0], g.ps[1]), (g.ps[2], g.ps[3]), (g.ps[4], g.ps[5]), (g.ps[6], g.ps[7])]
    NW = 2 * NCH

    def up(k):
        return g.up_attn[:, k, :] if k < GROUP else g.up_hyena[:, k - GROUP, :]

    with nc.Block() as block:
        @block.sync
        def _(sp):
            def load_sig(m):
                if m >= 2:
                    sp.wait_ge(gd, 2 * (m - 1))
                sp.dma_start(sig[m % 2][:, :, :], g.sigS.rearrange("(q m p) t -> m p q t", q=2, p=P)[m]).then_inc(sgs[m % 2], 16)
            for k in range(GROUP, KT):
                sp.dma_start(up(k), g.upS[k * P:(k + 1) * P, :]).then_inc(up_in, 16)
            load_up_weights(sp, g, 3)
            load_sig(0)
            load_sig(1)
            for i in range(4, NW):
                sp.wait_ge(wl, i - 3)
                load_up_weights(sp, g, i)
                if i == 5:
                    sp.wait_ge(u_lo, KT)
                    for k in range(KT):
                        sp.dma_start(g.w_out[:, k, :], io["w_out"][0, k * P:(k + 1) * P, :]).then_inc(g.w_out_in[k], 16)
                if i % 2 == 1:
                    load_sig(i // 2)
            for m in range(NW // 2, KT):
                load_sig(m)

        @block.scalar
        def _(act):
            def weights(i):
                act.wait_ge(g.up_w_in[i % 4], (32 if i % 2 == 0 else 16) * (i // 4 + 1))
                if i >= 2:
                    act.wait_ge(prod, 4 * (i - 1))
                act.activation(whi[i % 2][:, :, :], g.up_w[i % 4][:, :, :], ACT.Copy).then_inc(wh, 1)

            def rows(k):
                act.activation(uhi[:, k, :], up(k), ACT.Copy).then_inc(u_hi, 1)
            act.wait_ge(g.up_attn_in, 16 * GROUP)
            rows(0)
            weights(0)
            for k in range(1, GROUP):
                rows(k)
            act.wait_ge(up_in, 16 * (KT - GROUP))
            rows(GROUP)
            weights(1)
            for k in range(GROUP + 1, KT):
                rows(k)
            for m in range(KT):
                for h in range(2):
                    act.wait_ge(summed, 2 * m + h + 1)
                    act.activation(mhi[:, m, h * HALF:(h + 1) * HALF], mm_[:, :], ACT.Copy).then_inc(m_hi, 1)
                    i = m + 2
                    if h == 0 and m % 2 == 0 and i < NW:
                        weights(i)
                    if h == 1 and m % 2 == 1 and i < NW:
                        weights(i)

        @block.vector
        def _(dve):
            for k in range(KT):
                dve.wait_ge(u_hi, k + 1)
                nc.vector.tensor_tensor(ulo[:, k, :], up(k), uhi[:, k, :].bitcast(F32), ALU.subtract).then_inc(u_lo, 1)
            for m in range(KT):
                dve.wait_ge(sgs[m % 2], 16 * (m // 2 + 1))
                for h in range(2):
                    u = 2 * m + h
                    c = m // 2
                    dve.wait_ge(prod, 8 * c + 4 + u % 4 + 1)
                    if u:
                        dve.wait_ge(summed, u)
                    for q in range(2):
                        last = nc.vector.tensor_tensor(ga[:, q, :], banks[u % 4][q][:, 0:HALF], sig[m % 2][:, q, h * HALF:(h + 1) * HALF],
                                                       ALU.mult)
                    last.then_inc(gd, 1)
                    dve.wait_ge(gd, u + 1)
                    if u:
                        dve.wait_ge(m_lo, u)
                    nc.vector.tensor_tensor(mm_[:, :], ga[:, 0, :], ga[:, 1, :], ALU.add).then_inc(summed, 1)
                    dve.wait_ge(m_hi, u + 1)
                    nc.vector.tensor_tensor(mlo[:, m, h * HALF:(h + 1) * HALF], mm_[:, :], mhi[:, m, h * HALF:(h + 1) * HALF].bitcast(F32),
                                            ALU.subtract).then_inc(m_lo, 1)

        @block.gpsimd
        def _(pool):
            for i in range(NW):
                pool.wait_ge(wh, i + 1)
                nc.gpsimd.tensor_tensor(wlo[i % 2][:, :, :], g.up_w[i % 4][:, :, :], whi[i % 2][:, :, :].bitcast(F32), ALU.subtract)\
                  .then_inc(wl, 1)

        @block.tensor
        def _(pe):
            for i in range(NW):
                c, q = divmod(i, 2)
                pe.wait_ge(wh, i + 1)
                pe.wait_ge(wl, i + 1)
                for u in range(4):
                    m, h = divmod(u, 2)
                    if c and q == 0:
                        pe.wait_ge(gd, 4 * (c - 1) + u + 1)
                    for k in range(GROUP):
                        if c == 0 and u == 0:
                            pe.wait_ge(u_lo, GROUP * q + k + 1)
                        last = three_passes(nc, banks[u][q][:, 0:HALF], whi[q][:, k, m * P:(m + 1) * P], wlo[q][:, k, m * P:(m + 1) * P],
                                            uhi[:, GROUP * q + k, h * HALF:(h + 1) * HALF], ulo[:, GROUP * q + k, h * HALF:(h + 1) * HALF],
                                            k == 0, k == GROUP - 1)
                    last.then_inc(prod, 1)
    sb.at = top


def stage_route(g):
    nc, io, S = g.nc, g.io, g.sem
    sb = g.sb
    mhi, mlo, ident = g.mhi, g.mlo, g.ident
    top = sb.at
    NTOK = len(TOK_TILES)
    raw = g.w_out
    sb.at = g.up_split_at
    whi = sb("wo_hi", [P, KT, D], F32R)
    sb.at = g.merge_rest_at - 4 * GROUP * WCH * 4
    wlo = sb("wo_lo", [P, KT, D], F32R)
    h = [sb("residual_in", [P, D]) for _ in range(2)]
    hn = [sb("ffn_normed", [P, D]) for _ in range(2)]
    gain = sb("ffn_gain", [P, D])
    hT = sb("ffn_turned", [P, KT, P])
    wr = sb("w_router", [P, KT, E])
    ss = sb("square_sums", [P, 2 * NTOK])
    lg = sb("logits", [P, NTOK, E])
    red = sb("softmax_cols", [P, 2, NTOK])
    EE = 32 + E
    ROWS = (slice(0, E), slice(32, EE))
    twice = sb("affinity_by_token", [P, NTOK, EE])
    af = [sb(f"affinity{x}", [EE, LENS[0]]) for x in range(2)]
    rounds = -(-CAPS[0] // 8)
    val = sb("top_values", [EE, 8 * rounds])
    ix = sb("top_index", [EE, 8 * rounds], U32)
    both = sb("slots_by_expert", [EE, 2, SLOTS])
    second = sb("second_group_slots", [P, 2, E])
    (w_hi, w_lo0, w_lo1, hin0, hin1, cin, prod, h2d, sq, mean, root, hnd, st0, st1, trn, t_act, t_dve, lmm, lgd, exd, afd,
     aft, own, bd, btd, hT_used, hst0, hst1) = S(
        "rt_w_hi rt_w_lo0 rt_w_lo1 rt_hin0 rt_hin1 rt_cin rt_prod rt_h2 rt_sq rt_mean rt_root rt_hn rt_st0 rt_st1 rt_trn "
        "rt_t_act rt_t_dve rt_lmm rt_lg rt_exp rt_aff rt_afft rt_own rt_both rt_both_turned rt_ht_used rt_hst0 rt_hst1")
    hin, st, hst = [hin0, hin1], [st0, st1], [hst0, hst1]
    w_lo = [w_lo0, w_lo1]
    pieces = [token_pieces(t0, m, io["x_prompt"][0], io["x_sample"][0], io["meta_tokens"]) for t0, m in TOK_TILES]
    total = [[0, 0]]
    for i, ps_ in enumerate(pieces):
        now = list(total[-1])
        now[i % 2] += 16 * len(ps_)
        total.append(now)
    acc = [(g.ps[0], g.ps[1]), (g.ps[2], g.ps[3])]

    with nc.Block() as block:
        @block.sync
        def _(sp):
            def load(i):
                if i >= 2:
                    sp.wait_ge(hnd, i - 1)
                    sp.wait_ge(hst[i % 2], 16 * (i // 2))
                for r0, src in pieces[i]:
                    sp.dma_start(h[i % 2][r0:r0 + src.shape[0], :], src).then_inc(hin[i % 2], 16)
            load(0)
            load(1)
            sp.dma_start(gain[:, :], io["norm_ffn_g"][0].partition_broadcast(P)).then_inc(cin, 16)
            sp.dma_start(wr[:, :, :], io["w_router"][0].rearrange("(t p) e -> p t e", p=P)).then_inc(cin, 16)
            load_chunk(sp, g, 0)
            for half in w_lo:
                sp.wait_ge(half, KT // 2)
            load_chunk(sp, g, 1)
            load_chunk(sp, g, 2)
            for i, (t0, m) in enumerate(TOK_TILES):
                sp.wait_ge(h2d, i + 1)
                sp.dma_start(g.accS[t0:t0 + m, :], h[i % 2][0:m, :]).then_inc(hst[i % 2], 16)
                sp.wait_ge(hnd, i + 1)
                sp.dma_start(g.hnS[t0:t0 + m, :], hn[i % 2][0:m, :]).then_inc(st[i % 2], 16)
                if i + 2 < NTOK:
                    load(i + 2)
            sp.wait_ge(prod, NTOK)
            for n in range(3, RING):
                load_chunk(sp, g, n)
            for n in range(RING, AHEAD):
                sp.wait_ge(g.ew_lo_done, 2 * (n - RING + 1))
                load_chunk(sp, g, n)
            for k in range(2):
                sp.wait_ge(st[k], 16 * ((NTOK + 1 - k) // 2))
                sp.wait_ge(hst[k], 16 * ((NTOK + 1 - k) // 2))

        @block.tensor
        def _(pe):
            def product(i, b):
                t0, m = TOK_TILES[i]
                if i >= 2 and b == 0:
                    pe.wait_ge(h2d, i - 1)
                for k in range(KT):
                    if i == 0 and b == 0:
                        pe.wait_ge(w_lo[k % 2], k // 2 + 1)
                    last = three_passes(nc, acc[i % 2][b][0:m, :], mhi[:, k, t0:t0 + m], mlo[:, k, t0:t0 + m],
                                        whi[:, k, b * BANK:(b + 1) * BANK], wlo[:, k, b * BANK:(b + 1) * BANK], k == 0, k == KT - 1)
                if b == 1:
                    last.then_inc(prod, 1)

            def turn(i):
                t0, m = TOK_TILES[i]
                pe.wait_ge(hnd, i + 1)
                if i:
                    pe.wait_ge(t_act, i)
                    pe.wait_ge(t_dve, i)
                for k in range(KT):
                    last = nc.tensor.transpose(g.ps[4 + k // 4][:, (k % 4) * P:(k % 4) * P + m], hn[i % 2][0:m, k * P:(k + 1) * P],
                                               ident[0:m, 0:m])
                last.then_inc(trn, 1)

            def logits(i):
                t0, m = TOK_TILES[i]
                pe.wait_ge(t_act, i + 1)
                pe.wait_ge(t_dve, i + 1)
                if i:
                    pe.wait_ge(lgd, i)
                for k in range(KT):
                    last = nc.tensor.matmul(g.ps[6][0:m, 0:E], hT[:, k, 0:m], wr[:, k, :], start=(k == 0), stop=(k == KT - 1))
                last.then_inc(lmm, 1)

            pe.wait_ge(cin, 32)
            product(0, 0)
            product(0, 1)
            for i in range(1, NTOK):
                product(i, 0)
                turn(i - 1)
                product(i, 1)
                logits(i - 1)
            turn(NTOK - 1)
            logits(NTOK - 1)
            pe.wait_ge(afd, 1)
            pe.wait_ge(lgd, NTOK)
            for i, (t0, m) in enumerate(TOK_TILES):
                last = nc.tensor.transpose(g.ps[7 - i // 4][0:EE, (i % 4) * P:(i % 4) * P + m], twice[0:m, i, :], ident[0:m, 0:m])
            last.then_inc(aft, 1)
            pe.wait_ge(bd, 4)
            for q in range(2):
                last = nc.tensor.transpose(g.ps[4][0:SLOTS, q * P:q * P + EE], both[:, q, :], ident[0:EE, 0:EE])
            last.then_inc(btd, 1)

        @block.gpsimd
        def _(pool):
            for k in range(0, KT, 2):
                pool.wait_ge(w_hi, k + 1)
                nc.gpsimd.tensor_tensor(wlo[:, k, :], raw[:, k, :], whi[:, k, :].bitcast(F32), ALU.subtract).then_inc(w_lo[0], 1)
            pool.wait_ge(prod, NTOK)
            for u in range(4):
                pool.wait_ge(g.ew_hi_done, u + 1)
                nc.gpsimd.tensor_tensor(g.ew_lo[u][:, :], g.ring[u // 2][:, u % 2 * HC:(u % 2 + 1) * HC], g.ew_hi[u][:, :].bitcast(F32),
                                        ALU.subtract).then_inc(g.ew_lo_done, 1)

        @block.scalar
        def _(act):
            for k in range(KT):
                act.wait_ge(g.w_out_in[k], 16)
                act.activation(whi[:, k, :], raw[:, k, :], ACT.Copy).then_inc(w_hi, 1)
            for i, (t0, m) in enumerate(TOK_TILES):
                act.wait_ge(h2d, i + 1)
                if i >= 2:
                    act.wait_ge(trn, i - 1)
                    act.wait_ge(st[i % 2], 16 * (i // 2))
                act.activation(hn[i % 2][0:m, :], h[i % 2][0:m, :], ACT.Square, accum_out=ss[0:m, i:i + 1]).then_inc(sq, 1)
                act.wait_ge(mean, i + 1)
                act.activation(ss[0:m, NTOK + i:NTOK + i + 1], ss[0:m, i:i + 1], ACT.Sqrt).then_inc(root, 1)
                act.wait_ge(trn, i + 1)
                if i:
                    act.wait_ge(lmm, i)
                act.activation(hT[:, 0:4, 0:m], g.ps[4][:, :].rearrange("p (k t) -> p k t", k=4)[:, :, 0:m], ACT.Copy).then_inc(t_act, 1)
            act.wait_ge(own, NTOK + 3)
            act.activation(lg[:, :, :], lg[:, :, :], ACT.Exp).then_inc(exd, 1)
            for u in range(4):
                act.wait_ge(g.ring_in[u // 2], 16)
                act.activation(g.ew_hi[u][:, :], g.ring[u // 2][:, u % 2 * HC:(u % 2 + 1) * HC], ACT.Copy).then_inc(g.ew_hi_done, 1)

        @block.vector
        def _(dve):
            link = linked(dve, own)
            nc.vector.memset(twice[:, :, :], 0.0)
            nc.vector.memset(af[0][:, :], -1.0)
            nc.vector.memset(both[:, :, :], 0.0)
            link(nc.vector.memset(lg[:, :, :], 0.0))
            for k in range(1, KT, 2):
                dve.wait_ge(w_hi, k + 1)
                nc.vector.tensor_tensor(wlo[:, k, :], raw[:, k, :], whi[:, k, :].bitcast(F32), ALU.subtract).then_inc(w_lo[1], 1)
            dve.wait_ge(cin, 32)
            for i, (t0, m) in enumerate(TOK_TILES):
                dve.wait_ge(hin[i % 2], total[i + 1][i % 2])
                dve.wait_ge(prod, i + 1)
                for b in range(2):
                    last = nc.vector.tensor_tensor(h[i % 2][0:m, b * BANK:(b + 1) * BANK], acc[i % 2][b][0:m, :],
                                                   h[i % 2][0:m, b * BANK:(b + 1) * BANK], ALU.add)
                last.then_inc(h2d, 1)
                dve.wait_ge(sq, i + 1)
                nc.vector.tensor_scalar(ss[0:m, i:i + 1], ss[0:m, i:i + 1], 1.0 / D, EPS, ALU.mult, ALU.add).then_inc(mean, 1)
                dve.wait_ge(root, i + 1)
                link(nc.vector.reciprocal(ss[0:m, i:i + 1], ss[0:m, NTOK + i:NTOK + i + 1]))
                nc.vector.scalar_tensor_tensor(hn[i % 2][0:m, :], h[i % 2][0:m, :], ss[0:m, i:i + 1], gain[0:m, :],
                                               ALU.mult, ALU.mult).then_inc(hnd, 1)
                dve.wait_ge(trn, i + 1)
                if i:
                    dve.wait_ge(lmm, i)
                nc.vector.tensor_copy(hT[:, 4:8, 0:m], g.ps[5][:, :].rearrange("p (k t) -> p k t", k=4)[:, :, 0:m]).then_inc(t_dve, 1)
                dve.wait_ge(lmm, i + 1)
                nc.vector.tensor_copy(lg[0:m, i, :], g.ps[6][0:m, 0:E]).then_inc(lgd, 1)
            dve.wait_ge(lgd, NTOK)
            link(nc.vector.tensor_reduce(red[:, 0, :], lg[:, :, :], AX.X, ALU.max))
            link(nc.vector.tensor_tensor(lg[:, :, :], lg[:, :, :], red[:, 0, :].unsqueeze(2).broadcast_to([P, NTOK, E]), ALU.subtract))
            dve.wait_ge(exd, 1)
            link(nc.vector.tensor_reduce(red[:, 0, :], lg[:, :, :], AX.X, ALU.add))
            link(nc.vector.reciprocal(red[:, 1, :], red[:, 0, :]))
            for rows in ROWS:
                last = nc.vector.tensor_tensor(twice[:, :, rows], lg[:, :, :], red[:, 1, :].unsqueeze(2).broadcast_to([P, NTOK, E]), ALU.mult)
            last.then_inc(afd, 1)
            dve.wait_ge(aft, 1)
            nc.vector.tensor_copy(af[0][ROWS[0], 0:BANK], g.ps[7][ROWS[0], :])
            nc.vector.tensor_copy(af[0][ROWS[0], BANK:LENS[0]], g.ps[6][ROWS[0], 0:LENS[0] - BANK])
            link(nc.vector.tensor_copy(af[0][ROWS[1], 0:LENS[1]], g.ps[6][ROWS[1], LENS[0] - BANK:T - BANK]))
            for r in range(rounds):
                a, b = af[r % 2], af[(r + 1) % 2]
                c = slice(8 * r, 8 * r + 8)
                link(nc.vector.max(val[:, c], a[:, :]))
                if r + 1 < rounds:
                    nc.vector.max_index(ix[:, c], val[:, c], a[:, :])
                    link(nc.vector.match_replace(b[:, :], val[:, c], a[:, :], -1.0))
                else:
                    link(nc.vector.max_index(ix[:, c], val[:, c], a[:, :]))
            c0 = CAPS[0]
            nc.vector.tensor_copy(both[ROWS[0], 0, 0:c0], val[ROWS[0], 0:c0]).then_inc(bd, 1)
            nc.vector.tensor_copy(both[ROWS[1], 0, c0:SLOTS], val[ROWS[1], 0:CAPS[1]]).then_inc(bd, 1)
            nc.vector.tensor_copy(both[ROWS[0], 1, 0:c0], ix[ROWS[0], 0:c0]).then_inc(bd, 1)
            nc.vector.tensor_scalar(both[ROWS[1], 1, c0:SLOTS], ix[ROWS[1], 0:CAPS[1]], float(STARTS[1]), None, ALU.add).then_inc(bd, 1)
            dve.wait_ge(btd, 1)
            turned = g.ps[4][0:SLOTS, 0:2 * P].rearrange("p (q e) -> p q e", q=2)
            link(nc.vector.tensor_copy(second[0:SLOTS, :, :], turned[:, :, ROWS[1]]))
            nc.vector.tensor_tensor(g.gate_w[0:SLOTS, :], turned[:, 0, ROWS[0]], second[0:SLOTS, 0, :], ALU.add)
            nc.vector.tensor_tensor(g.slot_tok[0:SLOTS, 0:E], turned[:, 1, ROWS[0]], second[0:SLOTS, 1, :], ALU.add)
            link(nc.vector.tensor_tensor(g.slot_tok[0:SLOTS, E:E + 1], turned[:, 1, 0:1], second[0:SLOTS, 1, 0:1], ALU.add))
    sb.at = top


CHUNKS = 12
RING = 6
AHEAD = RING + 2
FCH = FE // 4
FT = FCH // P
HC = 2048


def expert_chunk(io, e, k):
    if k < 8:
        w = io[("w_exp_gate", "w_exp_up")[k % 2]][0].rearrange("e (t p) f -> e p t f", p=P)
        return w[e, :, :, (k // 2) * FCH:(k // 2 + 1) * FCH]
    return io["w_exp_down"][0].rearrange("e (c t p) d -> e c p t d", c=4, p=P)[e, k - 8]


def load_chunk(sp, g, n):
    e, k = divmod(n, CHUNKS)
    src = expert_chunk(g.io, e, k)
    sp.dma_start(g.ring[n % RING][:, :].rearrange("p (t f) -> p t f", t=src.shape[1]), src).then_inc(g.ring_in[n % RING], 16)


def stage_experts(g):
    nc, S = g.nc, g.sem
    sb = g.sb
    ident = g.ident
    top = sb.at
    ring = g.ring
    whi, wlo, w_hi, w_lo = g.ew_hi, g.ew_lo, g.ew_hi_done, g.ew_lo_done
    sb.at = g.ew_end
    xe = sb("gathered", [P, D])
    xT = [sb(f"gathered_turned_{x}", [P, KT, SLOTS], F32R) for x in ("hi", "lo")]
    sig = sb("gate_sigmoid", [P, FCH])
    silu = sb("gate_silu", [P, FCH])
    hid = sb("hidden", [P, FCH])
    hT = [sb(f"hidden_turned_{x}", [P, 4 * FT, SLOTS], F32R) for x in ("hi", "lo")]
    ye = sb("expert_out", [P, D])
    nxt = sb("slots_next", [P, 1], U32)
    cur = sb("slots_now", [P, 1], U32)
    gcur = sb("gate_now", [P, 1])
    credit = sb("start_credits", [P, 4])
    (nxt_set, cur_set, gath, turned, t_hi, t_lo, used, sg_done, silu_done, hid_done, y_done, scat) = S(
        "ex_next ex_cur ex_gathered ex_turned ex_turned_hi ex_turned_lo ex_used ex_sig ex_silu ex_hid "
        "ex_y_done ex_scattered")
    gb, ub, tb, yb = [g.ps[0], g.ps[1]], [g.ps[2], g.ps[3]], [g.ps[4], g.ps[5]], [g.ps[6], g.ps[7]]
    TURNS = [(2, "h", 0), (4, "h", 1), (6, "h", 2), (7, "x", 0), (8, "h", 3), (9, "x", 1)]
    NTURN = len(TURNS)

    def turn_dst(kind, c, half):
        return (hT if kind == "h" else xT)[half][:, 4 * c:4 * c + 4, :]

    def turn_bank(n):
        return tb[n % 2][:, :].rearrange("p (k s) -> p k s", k=4)[:, :, 0:SLOTS]

    with nc.Block() as block:
        @block.sync
        def _(sp):
            for n in range(AHEAD, E * CHUNKS):
                sp.wait_ge(w_lo, 2 * (n - RING + 1))
                load_chunk(sp, g, n)

        @block.gpsimd
        def _(pool):
            def gather():
                pool.indirect_dma_start(xe[0:SLOTS, :], None, g.hnS[:, :], bass.IndirectOffsetOnAxis(ap=nxt[0:SLOTS, 0:1], axis=0))\
                    .then_inc(gath, 16)
            pool.wait_ge(nxt_set, 1)
            gather()
            for e in range(E):
                pool.wait_ge(nxt_set, e + 2)
                pool.wait_ge(turned, NTURN * e + 2)
                gather()
                pool.wait_ge(cur_set, 2 * e + 2)
                pool.wait_ge(y_done, e + 2)
                pool.indirect_dma_start(g.accS[:, :], bass.IndirectOffsetOnAxis(ap=cur[0:SLOTS, 0:1], axis=0), ye[0:SLOTS, :], None,
                                        compute_op=ALU.add).then_inc(scat, 16)
                pool.wait_ge(scat, 16 * e + 16)
            pool.wait_ge(gath, 16 * (E + 1))

        @block.tensor
        def _(pe):
            def turn(kind, c, n):
                for k in range(4):
                    src = hid[0:SLOTS, k * P:(k + 1) * P] if kind == "h" else xe[0:SLOTS, (4 * c + k) * P:(4 * c + k + 1) * P]
                    last = nc.tensor.transpose(tb[n % 2][:, k * P:k * P + SLOTS], src, ident[0:SLOTS, 0:SLOTS])
                last.then_inc(turned, 1)

            def body(e):
                for k in range(CHUNKS):
                    if k == 0:
                        pe.wait_ge(t_lo, NTURN * e + 4)
                    if k < 8 and k % 2 == 0:
                        pe.wait_ge(hid_done, 4 * e + k // 2 + 1)
                    if k == 8:
                        pe.wait_ge(y_done, e + 1)
                    if k >= 8:
                        pe.wait_ge(t_lo, NTURN * e + 4 + (1, 2, 3, 5)[k - 8])
                    for half in range(2):
                        pe.wait_ge(w_lo, 2 * CHUNKS * e + 2 * k + half + 1)
                        hi, lo = whi[(2 * k + half) % 4], wlo[(2 * k + half) % 4]
                        if k < 8:
                            bank = (gb, ub)[k % 2][k // 2 % 2]
                            for i in range(4):
                                t = 4 * half + i
                                w = slice(i * FCH, (i + 1) * FCH)
                                last = three_passes(nc, bank[0:SLOTS, :], xT[0][:, t, :], xT[1][:, t, :], hi[:, w], lo[:, w],
                                                    t == 0, t == KT - 1)
                        else:
                            for i in range(2):
                                f = 4 * (k - 8) + 2 * half + i
                                for b in range(2):
                                    w = slice(i * D + b * BANK, i * D + (b + 1) * BANK)
                                    last = three_passes(nc, yb[b][0:SLOTS, :], hT[0][:, f, :], hT[1][:, f, :], hi[:, w], lo[:, w],
                                                        f == 0, f == 4 * FT - 1)
                        last.then_inc(used, 1)
                    for n, (after, kind, c) in enumerate(TURNS):
                        if after == k:
                            pe.wait_ge(t_lo, NTURN * e + n + 3)
                            if kind == "h":
                                pe.wait_ge(hid_done, 4 * e + c + 3)
                            elif c == 0:
                                pe.wait_ge(gath, 16 * e + 32)
                            turn(kind, c, n)
            pe.wait_ge(gath, 16)
            turn("x", 0, 0)
            turn("x", 1, 1)
            with pe.Fori(0, E) as e:
                body(e)

        def slot_free(eng, e, k, half):
            eng.wait_ge(used, 2 * CHUNKS * e + 2 * k + half - 3)

        @block.scalar
        def _(act):
            def hi_of(e, k, half):
                act.wait_ge(g.ring_in[k % RING], 32 * e + 16 * (k // RING + 1))
                act.activation(whi[(2 * k + half) % 4][:, :], ring[k % RING][:, half * HC:(half + 1) * HC], ACT.Copy).then_inc(w_hi, 1)

            def turn_hi(e, n, kind, c):
                act.wait_ge(turned, NTURN * e + n + 3)
                act.activation(turn_dst(kind, c, 0), turn_bank(n), ACT.Copy).then_inc(t_hi, 1)

            def body(e, last):
                for k in range(2, CHUNKS + 2):
                    slot_free(act, e, k, 0)
                    if k < CHUNKS or not last:
                        hi_of(e, k, 0)
                    slot_free(act, e, k, 1)
                    if k % 2 and k < 10:
                        c = (k - 3) // 2
                        act.wait_ge(silu_done, 4 * e + c + 1)
                        act.activation(sig[0:SLOTS, :], gb[c % 2][0:SLOTS, :], ACT.Sigmoid).then_inc(sg_done, 1)
                    for n, (after, kind, c) in enumerate(TURNS):
                        if after == k - 2:
                            turn_hi(e, n, kind, c)
                    if k < CHUNKS or not last:
                        hi_of(e, k, 1)
            for c in range(2):
                act.wait_ge(turned, c + 1)
                act.activation(turn_dst("x", c, 0), turn_bank(c), ACT.Copy).then_inc(t_hi, 1)
            with act.Fori(0, E - 1) as e:
                body(e, False)
            body(E - 1, True)

        @block.vector
        def _(dve):
            def lo_of(e, k, half):
                u = (2 * k + half) % 4
                dve.wait_ge(w_hi, 2 * CHUNKS * e + 2 * k + half + 1)
                nc.vector.tensor_tensor(wlo[u][:, :], ring[k % RING][:, half * HC:(half + 1) * HC], whi[u][:, :].bitcast(F32),
                                        ALU.subtract).then_inc(w_lo, 1)

            def turn_lo(n, kind, c):
                nc.vector.tensor_tensor(turn_dst(kind, c, 1), turn_bank(n), turn_dst(kind, c, 0).bitcast(F32), ALU.subtract)\
                  .then_inc(t_lo, 1)

            def body(e, last):
                dve.wait_ge(gath, 16 * e + 16)
                nc.vector.tensor_copy(nxt[0:SLOTS, :], g.slot_tok[0:SLOTS, bass.ds(e + 1, 1)]).then_inc(nxt_set, 1)
                for k in range(2, CHUNKS + 2):
                    slot_free(dve, e, k, 0)
                    if k < CHUNKS or not last:
                        lo_of(e, k, 0)
                    slot_free(dve, e, k, 1)
                    if k % 2 and k < 10:
                        c = (k - 3) // 2
                        dve.wait_ge(sg_done, 4 * e + c + 1)
                        nc.vector.tensor_tensor(silu[0:SLOTS, :], gb[c % 2][0:SLOTS, :], sig[0:SLOTS, :], ALU.mult).then_inc(silu_done, 1)
                        dve.wait_ge(silu_done, 4 * e + c + 2)
                        dve.wait_ge(turned, NTURN * e + 2 + (0, 1, 2, 3)[c])
                        nc.vector.tensor_tensor(hid[0:SLOTS, :], ub[c % 2][0:SLOTS, :], silu[0:SLOTS, :], ALU.mult).then_inc(hid_done, 1)
                    for n, (after, kind, c) in enumerate(TURNS):
                        if after == k - 2:
                            dve.wait_ge(t_hi, NTURN * e + n + 3)
                            turn_lo(n, kind, c)
                    if k == CHUNKS + 1:
                        dve.wait_ge(gath, 16 * e + 32)
                        nc.vector.tensor_copy(gcur[0:SLOTS, :], g.gate_w[0:SLOTS, bass.ds(e, 1)]).then_inc(cur_set, 1)
                        nc.vector.tensor_copy(cur[0:SLOTS, :], g.slot_tok[0:SLOTS, bass.ds(e, 1)]).then_inc(cur_set, 1)
                        dve.wait_ge(cur_set, 2 * e + 1)
                        for b in range(2):
                            end = nc.vector.tensor_scalar(ye[0:SLOTS, b * BANK:(b + 1) * BANK], yb[b][0:SLOTS, :], gcur[0:SLOTS, :],
                                                          None, ALU.mult)
                        end.then_inc(y_done, 1)
                    if k < CHUNKS or not last:
                        lo_of(e, k, 1)
            nc.vector.tensor_copy(nxt[0:SLOTS, :], g.slot_tok[0:SLOTS, 0:1]).then_inc(nxt_set, 1)
            nc.vector.memset(credit[0:1, 0:1], 0.0).then_inc(hid_done, 2)
            nc.vector.memset(credit[0:1, 1:2], 0.0).then_inc(silu_done, 1)
            nc.vector.memset(credit[0:1, 2:3], 0.0).then_inc(y_done, 1)
            nc.vector.memset(credit[0:1, 3:4], 0.0).then_inc(t_lo, 2)
            for c in range(2):
                dve.wait_ge(t_hi, c + 1)
                turn_lo(c, "x", c)
            with dve.Fori(0, E - 1) as e:
                body(e, False)
            body(E - 1, True)
    sb.at = top


def stage_finish(g):
    nc, io, S = g.nc, g.io, g.sem
    sb = g.sb
    top = sb.at
    NTOK = len(TOK_TILES)
    h = [sb("h_final", [P, D]) for _ in range(NTOK)]
    o = [sb("out_rows", [P, D]) for _ in range(NTOK)]
    gain = sb("final_gain", [P, D])
    ss = sb("square_sums", [P, 2 * NTOK])
    (cin, sq, mean, root, outd, outs, own) = S("fi_cin fi_sq fi_mean fi_root fi_out fi_stored fi_own")
    hin = S(" ".join(f"fi_in{k}" for k in range(NTOK)))
    with nc.Block() as block:
        @block.sync
        def _(sp):
            for i, (t0, m) in enumerate(TOK_TILES):
                sp.dma_start(h[i][0:m, :], g.accS[t0:t0 + m, :]).then_inc(hin[i], 16)
                if i == 0:
                    sp.dma_start(gain[:, :], io["norm_final_g"].partition_broadcast(P)).then_inc(cin, 16)
            n = 0
            for i, (t0, m) in enumerate(TOK_TILES):
                sp.wait_ge(outd, i + 1)
                for s, y in enumerate(g.out):
                    lo, hi = max(t0, STARTS[s] + N_META), min(t0 + m, STARTS[s] + LENS[s])
                    if lo < hi:
                        off = STARTS[s] + N_META
                        sp.dma_start(y[0, lo - off:hi - off, :], o[i][lo - t0:hi - t0, :]).then_inc(outs, 16)
                        n += 16
            sp.wait_ge(outs, n)

        @block.scalar
        def _(act):
            for i, (t0, m) in enumerate(TOK_TILES):
                act.wait_ge(hin[i], 16)
                act.activation(o[i][0:m, :], h[i][0:m, :], ACT.Square, accum_out=ss[0:m, i:i + 1]).then_inc(sq, 1)
                act.wait_ge(mean, i + 1)
                act.activation(ss[0:m, NTOK + i:NTOK + i + 1], ss[0:m, i:i + 1], ACT.Sqrt).then_inc(root, 1)

        @block.vector
        def _(dve):
            link = linked(dve, own)
            dve.wait_ge(cin, 16)
            for i, (t0, m) in enumerate(TOK_TILES):
                dve.wait_ge(sq, i + 1)
                nc.vector.tensor_scalar(ss[0:m, i:i + 1], ss[0:m, i:i + 1], 1.0 / D, EPS, ALU.mult, ALU.add).then_inc(mean, 1)
                dve.wait_ge(root, i + 1)
                link(nc.vector.reciprocal(ss[0:m, i:i + 1], ss[0:m, NTOK + i:NTOK + i + 1]))
                nc.vector.scalar_tensor_tensor(o[i][0:m, :], h[i][0:m, :], ss[0:m, i:i + 1], gain[0:m, :], ALU.mult, ALU.mult).then_inc(outd, 1)
    sb.at = top


def encode_layer(nc, io, out):
    with ExitStack() as ctx:
        g = Ctx()
        g.nc, g.io, g.out = nc, io, out
        g.sem = Semaphores(nc)
        sb = g.sb = Map(nc)
        g.ps = [ctx.enter_context(nc.psum_tensor(f"bank{k}", [P, BANK], F32)) for k in range(8)]

        def scratch(name, shape):
            return nc.dram_tensor(name, shape, F32, kind="Internal").ap()
        g.hyS = scratch("hy_conv_rows", (3 * HYW, T + 1))
        g.sigS = scratch("gate_rows", (2 * D, T))
        g.upS = scratch("mixer_rows", (D, T))
        g.accS = scratch("residual_rows", (T, D))
        g.hnS = scratch("ffn_rows", (T, D))
        g.ident = sb("ident", [P, P])
        g.taps = sb("conv_taps", [P, 4 * HY_TILES + 2 * CT])
        g.gate_w = sb("slot_gates", [P, E])
        g.slot_tok = sb("slot_tokens", [P, E + 1], U32)
        top = sb.at
        g.feat = sb("filter_features", [FILT_HIDDEN, T])
        g.qk = sb("q_k_rotated", [P, GROUP + 1, T])
        g.v = sb("values", [P, len(VB), P])
        stage_mix(g)
        g.sem.end_stage()
        g.up_split_at = top + 2 * KT * T * 4
        at = g.up_split_at + 2 * KT * T * 4
        sb.at = at
        g.up_hyena = sb("hyena_rows", [P, KT - GROUP, T])
        g.up_attn = sb("attention_rows", [P, GROUP, T])
        sb.at = at
        g.w_out = sb("w_out", [P, KT, D])
        g.up_w = [sb("up_weights", [P, GROUP, WCH]) for _ in range(4)]
        g.merge_rest_at = sb.at
        g.up_w_in = [nc.alloc_semaphore(f"up_w_in{k}") for k in range(4)]
        g.w_out_in = [nc.alloc_semaphore(f"w_out_in{k}") for k in range(KT)]
        g.up_attn_in = nc.alloc_semaphore("up_attn_in")
        slot = 4 * 4096
        g.ring = []
        for k, a in enumerate((g.up_split_at + 4 * KT * D, at, at + slot, top, top + slot, top + 2 * slot)):
            sb.at = a
            g.ring.append(sb(f"w_ring{k}", [P, 4096]))
        sb.at = top + 3 * slot
        g.ew_hi = [sb("we_hi", [P, HC], F32R) for _ in range(4)]
        sb.at = at + 2 * slot
        g.ew_lo = [sb("we_lo", [P, HC], F32R) for _ in range(4)]
        g.ew_end = sb.at
        g.ew_hi_done, g.ew_lo_done = [nc.alloc_semaphore(f"expert_w_{x}") for x in ("hi", "lo")]
        g.ring_in = [nc.alloc_semaphore(f"ring_in{k}") for k in range(RING)]
        sb.at = top + T * 4
        stage_hyena(g)
        g.sem.end_stage()
        sb.at = top
        g.mhi = sb("merged_hi", [P, KT, T], F32R)
        g.mlo = sb("merged_lo", [P, KT, T], F32R)
        stage_merge(g)
        g.sem.end_stage()
        stage_route(g)
        g.sem.end_stage()
        sb.at = top
        stage_experts(g)
        g.sem.end_stage()
        stage_finish(g)
        g.sem.end_stage()


_INS = ["x_prompt", "x_sample", "meta_tokens", "norm_mix_g", "w_in", "attn_sink", "hy_conv_w", "hy_conv_b",
        "hy_filt_w1", "hy_filt_b1", "hy_filt_w2", "hy_filt_b2", "hy_filt_w3", "hy_filt_b3", "hy_filt_freq",
        "hy_filt_wout", "hy_skip", "w_attn_up", "w_hyena_up", "w_out", "norm_ffn_g", "w_router", "w_exp_gate",
        "w_exp_up", "w_exp_down", "norm_final_g"]
_OUTS = [(1, SEQS[0], D), (1, SEQS[1], D)]


def kernel(**inputs):
    import concourse.bacc as _bacc
    from concourse.bass_utils import run_bass_kernel_spmd as _run

    nc = _bacc.Bacc("TRN2", target_bir_lowering=False, num_devices=1)
    arrays = {f"in_{name}": np.ascontiguousarray(inputs[name]) for name in _INS}
    arrays.update({f"in_{name}": a for name, a in shape_tables().items()})
    io = {name[3:]: nc.dram_tensor(name, a.shape, mybir.dt.from_np(a.dtype), kind="ExternalInput").ap()
          for name, a in arrays.items()}
    out = [nc.dram_tensor(f"out_{i}", shape, F32, kind="ExternalOutput").ap() for i, shape in enumerate(_OUTS)]
    encode_layer(nc, io, out)
    r = _run(nc, [arrays], core_ids=[0])
    return tuple(r.results[0][f"out_{i}"] for i in range(len(_OUTS)))
```
